# Optimizing a Trainium2 kernel written in Bass

```python
import jax, jax.numpy as jnp
from jax import lax
import numpy as np

D_MODEL = 2048
BATCH = 1
SEQ = 256
DEPTH = 1

CHUNK = 64
MIX_WIDTH = D_MODEL
RET_HEADS = 4
RET_DIM = MIX_WIDTH // 2 // RET_HEADS
RET_WIDTH = RET_HEADS * RET_DIM
ATT_Q_HEADS = 16
ATT_KV_HEADS = 2
ATT_GROUP = ATT_Q_HEADS // ATT_KV_HEADS
ATT_DIM = (MIX_WIDTH - RET_WIDTH) // ATT_Q_HEADS
ATT_WIDTH = ATT_Q_HEADS * ATT_DIM
ATT_KV_WIDTH = ATT_KV_HEADS * ATT_DIM
WINDOW = 128
WINDOW_CHUNKS = WINDOW // CHUNK
D_FF = 5632
CONV_WIDTH = 3
RET_ROT_BASE = 10000.0
EPS = 1e-6
IN_WIDTH = 4 * RET_WIDTH + ATT_WIDTH + 2 * ATT_KV_WIDTH
N_MOD = 6

kernel_name = "hybrid_retention_swa_convglu_adaln"

def rms_norm(x, g):
    xf = x.astype(jnp.float32)
    y = xf * lax.rsqrt(jnp.mean(xf * xf, axis=-1, keepdims=True) + EPS)
    return (y * g.astype(jnp.float32)).astype(x.dtype)

def modulate(h, shift, scale):
    return h * (1.0 + scale[:, None, :]) + shift[:, None, :]

def rotate_pairs(x, cos, sin):
    x1 = x[..., 0::2]
    x2 = x[..., 1::2]
    c = cos[None, :, None, :].astype(x.dtype)
    s = sin[None, :, None, :].astype(x.dtype)
    return jnp.stack([x1 * c - x2 * s, x1 * s + x2 * c], axis=-1).reshape(x.shape)

def retention(q, k, v, g):
    B, S, _ = q.shape
    NC = S // CHUNK
    q = q.reshape(B, S, RET_HEADS, RET_DIM)
    k = k.reshape(B, S, RET_HEADS, RET_DIM)
    v = v.reshape(B, S, RET_HEADS, RET_DIM)
    pos = jnp.arange(S, dtype=jnp.float32)
    freq = RET_ROT_BASE ** (-jnp.linspace(0.0, 1.0, RET_DIM // 2, dtype=jnp.float32))
    ang = pos[:, None] * freq[None, :]
    cos, sin = jnp.cos(ang), jnp.sin(ang)
    q = rotate_pairs(q, cos, sin)
    k = rotate_pairs(k, cos, sin) * (RET_DIM ** -0.5)

    log_gamma = jnp.log(1.0 - 2.0 ** (-5.0 - jnp.arange(RET_HEADS, dtype=jnp.float32)))
    idx = jnp.arange(CHUNK, dtype=jnp.float32)
    intra_decay = jnp.exp(log_gamma[:, None, None] * jnp.abs(idx[:, None] - idx[None, :]))
    k_decay = jnp.exp(log_gamma[:, None] * (CHUNK - 1 - idx)[None, :])
    q_decay = jnp.exp(log_gamma[:, None] * (idx + 1.0)[None, :])
    chunk_decay = jnp.exp(log_gamma * CHUNK)

    qc = q.reshape(B, NC, CHUNK, RET_HEADS, RET_DIM)
    kc = k.reshape(B, NC, CHUNK, RET_HEADS, RET_DIM)
    vc = v.reshape(B, NC, CHUNK, RET_HEADS, RET_DIM)

    scores = jnp.einsum('bnchd,bnmhd->bnhcm', qc, kc) * intra_decay
    intra = jnp.einsum('bnhcm,bnmhe->bnche', scores, vc)

    def step(state, inp):
        qn, kn, vn = inp
        cross = jnp.einsum('bchd,hc,bhde->bche', qn, q_decay, state)
        kv = jnp.einsum('bchd,hc,bche->bhde', kn, k_decay, vn)
        state = state * chunk_decay[None, :, None, None] + kv
        return state, cross

    state0 = jnp.zeros((B, RET_HEADS, RET_DIM, RET_DIM), jnp.float32)
    xs = (jnp.moveaxis(qc, 1, 0), jnp.moveaxis(kc, 1, 0), jnp.moveaxis(vc, 1, 0))
    _, cross = lax.scan(step, state0, xs)
    o = intra.astype(jnp.float32) + jnp.moveaxis(cross, 0, 1)
    o = o.reshape(B, S, RET_HEADS, RET_DIM)
    o = o * lax.rsqrt(jnp.mean(o * o, axis=-1, keepdims=True) + EPS)
    o = o.reshape(B, S, RET_WIDTH).astype(g.dtype)
    return jax.nn.silu(g) * o

def shift_chunks(t, s):
    if s == 0:
        return t
    return jnp.concatenate([jnp.zeros_like(t[:, :s]), t[:, :-s]], axis=1)

def window_sink_attention(q, k, v, sinks):
    B, S, _ = q.shape
    NC = S // CHUNK
    qc = q.reshape(B, NC, CHUNK, ATT_KV_HEADS, ATT_GROUP, ATT_DIM) * (ATT_DIM ** -0.5)
    kc = k.reshape(B, NC, CHUNK, ATT_KV_HEADS, ATT_DIM)
    vc = v.reshape(B, NC, CHUNK, ATT_KV_HEADS, ATT_DIM)
    shifts = list(range(WINDOW_CHUNKS - 1, -1, -1))
    kw = jnp.concatenate([shift_chunks(kc, s) for s in shifts], axis=2)
    vw = jnp.concatenate([shift_chunks(vc, s) for s in shifts], axis=2)
    key_shift = jnp.repeat(jnp.array(shifts, jnp.int32), CHUNK)
    valid = (jnp.arange(NC, dtype=jnp.int32)[:, None] - key_shift[None, :]) >= 0

    s = jnp.einsum('bncKgd,bnmKd->bnKgcm', qc, kw).astype(jnp.float32)
    s = jnp.where(valid[None, :, None, None, None, :], s, -jnp.inf)
    sink = sinks.astype(jnp.float32).reshape(ATT_KV_HEADS, ATT_GROUP)[None, None, :, :, None, None]
    m = jnp.maximum(jnp.max(s, axis=-1, keepdims=True), sink)
    p = jnp.exp(s - m)
    denom = jnp.sum(p, axis=-1, keepdims=True) + jnp.exp(sink - m)
    p = (p / denom).astype(v.dtype)
    o = jnp.einsum('bnKgcm,bnmKd->bncKgd', p, vw)
    return o.reshape(B, S, ATT_WIDTH)

def conv_glu(h, w_up, w_conv, b_conv, w_down):
    u = h @ w_up
    a, b = jnp.split(u, 2, axis=-1)
    a = lax.conv_general_dilated(
        a, w_conv[:, None, :], window_strides=(1,), padding=[(CONV_WIDTH - 1, 0)],
        dimension_numbers=('NWC', 'WIO', 'NWC'), feature_group_count=D_FF) + b_conv
    return (jax.nn.silu(a) * b) @ w_down

def setup_inputs(seed: int = 0) -> dict:
    key = jax.random.key(seed)
    ks = jax.random.split(key, 20)
    f32 = jnp.float32
    n = lambda k, shape, s: jax.random.normal(k, shape, f32) * s
    return {
        "x": n(ks[0], (BATCH, SEQ, D_MODEL), 1.0),
        "c": n(ks[1], (BATCH, D_MODEL), 1.0),
        "w_ada": n(ks[2], (DEPTH, D_MODEL, N_MOD * D_MODEL), 0.5 * D_MODEL ** -0.5),
        "b_ada": n(ks[3], (DEPTH, N_MOD * D_MODEL), 0.02),
        "g_mix": 1.0 + n(ks[4], (DEPTH, D_MODEL), 0.05),
        "w_in": n(ks[5], (DEPTH, D_MODEL, IN_WIDTH), D_MODEL ** -0.5),
        "b_in": n(ks[6], (DEPTH, IN_WIDTH), 0.02),
        "sinks": n(ks[7], (DEPTH, ATT_Q_HEADS), 1.0),
        "w_out": n(ks[8], (DEPTH, MIX_WIDTH, D_MODEL), MIX_WIDTH ** -0.5),
        "g_ffn": 1.0 + n(ks[9], (DEPTH, D_MODEL), 0.05),
        "w_up": n(ks[10], (DEPTH, D_MODEL, 2 * D_FF), D_MODEL ** -0.5),
        "w_conv": n(ks[11], (DEPTH, CONV_WIDTH, D_FF), CONV_WIDTH ** -0.5),
        "b_conv": n(ks[12], (DEPTH, D_FF), 0.02),
        "w_down": n(ks[13], (DEPTH, D_FF, D_MODEL), D_FF ** -0.5),
        "w_final_ada": n(ks[14], (D_MODEL, 2 * D_MODEL), 0.5 * D_MODEL ** -0.5),
        "b_final_ada": n(ks[15], (2 * D_MODEL,), 0.02),
        "g_final": 1.0 + n(ks[16], (D_MODEL,), 0.05),
    }

def reference(x, c, w_ada, b_ada, g_mix, w_in, b_in, sinks, w_out, g_ffn,
              w_up, w_conv, b_conv, w_down, w_final_ada, b_final_ada, g_final):
    split_at = [RET_WIDTH, 2 * RET_WIDTH, 3 * RET_WIDTH, 4 * RET_WIDTH,
                4 * RET_WIDTH + ATT_WIDTH, 4 * RET_WIDTH + ATT_WIDTH + ATT_KV_WIDTH]
    c_act = jax.nn.silu(c)
    for l in range(DEPTH):
        mod = c_act @ w_ada[l] + b_ada[l]
        sh1, sc1, gt1, sh2, sc2, gt2 = jnp.split(mod, N_MOD, axis=-1)

        h = modulate(rms_norm(x, g_mix[l]), sh1, sc1)
        proj = h @ w_in[l] + b_in[l]
        rq, rk, rv, rg, aq, ak, av = jnp.split(proj, split_at, axis=-1)
        ret = retention(rq, rk, rv, rg).astype(x.dtype)
        att = window_sink_attention(aq, ak, av, sinks[l])
        mix = jnp.concatenate([ret, att], axis=-1) @ w_out[l]
        x = x + gt1[:, None, :] * mix

        h = modulate(rms_norm(x, g_ffn[l]), sh2, sc2)
        x = x + gt2[:, None, :] * conv_glu(h, w_up[l], w_conv[l], b_conv[l], w_down[l])

    fmod = c_act @ w_final_ada + b_final_ada
    f_shift, f_scale = jnp.split(fmod, 2, axis=-1)
    return modulate(rms_norm(x, g_final), f_shift, f_scale)


_drawn_inputs = setup_inputs


def setup_inputs(seed=0):
    import zlib

    import numpy as np

    out = dict(_drawn_inputs(seed))
    spreads = {}
    factors = {'g_mix': 4.289, 'b_in': 6.597, 'sinks': 8.0, 'g_ffn': 3.695, 'b_conv': 8.0}
    for name, (base, spread) in spreads.items():
        noise = np.random.default_rng([zlib.crc32(name.encode()), seed]).standard_normal(out[name].shape)
        drawn = base * np.exp(spread * noise) if base else spread * noise
        out[name] = __import__('jax').numpy.asarray(drawn.astype(out[name].dtype))
    for name, factor in factors.items():
        out[name] = (out[name] * factor).astype(out[name].dtype)
    return out
```

```python
from contextlib import ExitStack

import numpy as np

import concourse.bass as bass
from concourse import mybir

F32 = mybir.dt.float32
F32R = mybir.dt.float32r
ALU = mybir.AluOpType
ACT = mybir.ActivationFunctionType

P = 128
D, S, FF = 2048, 256, 5632
CHUNK = 64
KT = D // P
TT = S // P
RH, RD = 4, 256
AH, AKV, AD = 16, 2, 64
FT = FF // P
EPS = 1e-6
GW = 1024
RING = 4

COL_RQ, COL_RK, COL_RV, COL_RG, COL_AQ, COL_AK = (i * GW for i in range(6))
COL_AV = COL_AK + AKV * AD
AKV_W = 2 * AKV * AD

STEP_AQ, STEP_AK, STEP_RQ, STEP_RK, STEP_RV, STEP_RG, STEP_WO0, STEP_WO1, STEP_UP = (KT * i for i in range(9))
UG = FF // (GW // 2)
STEP_DN = STEP_UP + UG * KT
STEPS = STEP_DN + 2 * FT
LOOP = 8
ADA_PAIRS = 4

JOB_SH2, JOB_SC2, JOB_GT1, JOB_GT2, JOB_FSC, JOB_FSH = 4, 6, 8, 10, 12, 14
JOBS = 16


def build(nc, x, c, w_ada, b_ada, g_mix, w_in, b_in, sinks, w_out, g_ffn, w_up, w_conv, b_conv,
          w_down, w_final_ada, b_final_ada, g_final, rot, decay, masks, eye, out):
    ctx = ExitStack()
    with ctx:
        def sb(name, shape, dt=F32):
            return ctx.enter_context(nc.sbuf_tensor(name, shape, dt))

        def sem(name):
            return ctx.enter_context(nc.semaphore(name))

        raw = sb("raw", [P, RING, 2 * GW])
        whi = sb("whi", [P, RING, GW], F32R)
        wlo = sb("wlo", [P, RING, GW], F32R)
        hhi = sb("hhi", [P, KT, S], F32R)
        hlo = sb("hlo", [P, KT, S], F32R)
        ada_raw = sb("ada_raw", [P, RING, GW])
        acc = sb("acc", [P, 4, GW])
        xb = sb("xb", [P, TT, D])
        gate = sb("gate", [P, D])
        arena = sb("arena", [P, 12288])
        ident = sb("ident", [P, P])
        ones = sb("ones", [P, P])
        av_bias = sb("av_bias", [P, P])
        c_act = sb("c_act", [P, KT])
        g_col = sb("g_col", [P, 2, KT])
        conv_col = sb("conv_col", [P, 2 * FT])
        conv_col2 = sb("conv_col2", [P, 2 * FT + 9])
        rqk_col = sb("rqk_col", [P, 2, 8])
        mod_col = sb("mod_col", [P, 4, KT])
        sink_b = sb("sink_b", [P, AH])
        ssq = sb("ssq", [P, 16])
        rstd = sb("rstd", [P, 8])
        smx = sb("smx", [P, 6, 16])
        aqT = arena[:, 0:2048].rearrange("p (i s) -> p i s", s=S)
        k2 = arena[:, 2048:2560].rearrange("p (i s) -> p i s", s=S)
        av = arena[:, 2560:2816].rearrange("p (t d) -> p t d", d=P)
        cs = arena[:, 2816:3328].rearrange("p (i s) -> p i s", s=S)
        p0 = arena[:, 3328:4352].rearrange("p (h k) -> p h k", k=P)
        p1 = arena[:, 4352:6400].rearrange("p (h k) -> p h k", k=S)
        dec = arena[:, 3328:4864].rearrange("p (h k) -> p h k", k=384)
        sT = arena[:, 4864:6400].rearrange("p (h k) -> p h k", k=384)
        rows = arena[:, 3328:3328 + 4 * 256].rearrange("p (i n) -> p i n", n=256)
        qT = arena[:, 6400:8448].rearrange("p (h e s) -> p h e s", e=2, s=S)
        kT = arena[:, 8448:10496].rearrange("p (h e s) -> p h e s", e=2, s=S)
        xT = arena[:, 6400:10496].rearrange("p (k s) -> p k s", s=S)
        mask = arena[:, 10496:10880]
        pT = arena[:, 10880:11520].rearrange("p (i k) -> p i k", k=320)
        mod_tmp = arena[:, 11520:12032].rearrange("p (i s) -> p i s", s=S)
        rot_tmp = xb[:, 0, :].rearrange("p (i h s) -> p i h s", i=2, s=S)
        v_sb = xb[:, 0, :].rearrange("p (t e) -> p t e", t=TT)
        g_sb = xb[:, 1, :].rearrange("p (t e) -> p t e", t=TT)
        xn = arena[:, 0:4096].rearrange("p (t n) -> p t n", t=TT)
        actT = arena[:, 0:FT * S]
        glu_tmp = arena[:, FT * S:FT * S + 4 * S].rearrange("p (i s) -> p i s", s=S)
        res1_tmp, res2_tmp = (a.rearrange("p i s -> p (i s)") for a in (mod_tmp, glu_tmp[:, 0:2, :]))

        ps = ctx.enter_context(nc.psum_tensor("ps", [P, 8, 512], F32))

        x_in = sem("x_in")
        rows_in = sem("rows_in")
        const_in = sem("const_in")
        cact_in = sem("cact_in")
        x_again = sem("x_again")
        dec_in = sem("dec_in")
        gfin_in = sem("gfin_in")
        stored = sem("stored")
        raw_in = [sem(f"raw_in{i}") for i in range(RING)]
        ada_in = [sem(f"ada_in{i}") for i in range(RING)]
        bias_in = sem("bias_in")
        hi_ready = sem("hi_ready")
        lo_ready = sem("lo_ready")
        step_done = sem("step_done")
        acc_zero = sem("acc_zero")
        ada_acc = sem("ada_acc")
        ada_red = sem("ada_red")
        mod_ready = sem("mod_ready")
        cact_ready = sem("cact_ready")
        ones_ready = sem("ones_ready")
        ssq_ready = sem("ssq_ready")
        xn_ready = sem("xn_ready")
        xt_ps = sem("xt_ps")
        xt_even = sem("xt_even")
        xt_odd = sem("xt_odd")
        cols_ps = sem("cols_ps")
        cols_ready = sem("cols_ready")
        tmp_ready = sem("tmp_ready")
        hhi_ready = sem("hhi_ready")
        hlo_ready = sem("hlo_ready")
        aq_ready = sem("aq_ready")
        k2_ready = sem("k2_ready")
        av_ready = sem("av_ready")
        rq_raw = sem("rq_raw")
        rk_raw = sem("rk_raw")
        rot_done = sem("rot_done")
        sc_ps = sem("sc_ps")
        sc_done = sem("sc_done")
        nm_ready = sem("nm_ready")
        exp_done = sem("exp_done")
        esink = sem("esink")
        p_norm = sem("p_norm")
        pt_ps = sem("pt_ps")
        pt_done = sem("pt_done")
        pt_used = sem("pt_used")
        att_ready = sem("att_ready")
        v_ready = sem("v_ready")
        g_raw = sem("g_raw")
        g_ready = sem("g_ready")
        st_ps = sem("st_ps")
        st_ready = sem("st_ready")
        o_ps = sem("o_ps")
        o_ssq = sem("o_ssq")
        mix_ready = sem("mix_ready")
        mixt_ps = sem("mixt_ps")
        gt_ps = sem("gt_ps")
        gt_ready = sem("gt_ready")
        x1_part = sem("x1_part")
        x1_ssq = sem("x1_ssq")
        var_ready = sem("var_ready")
        rstd_ready = sem("rstd_ready")
        xn2_dve = sem("xn2_dve")
        xn2_act = sem("xn2_act")
        xn2_ps = sem("xn2_ps")
        glu_lin = sem("glu_lin")
        glu_conv = sem("glu_conv")
        glu_silu = sem("glu_silu")
        glu_done = sem("glu_done")
        x2_part = sem("x2_part")
        x2_ssq = sem("x2_ssq")
        fsc_ps = sem("fsc_ps")
        fsh_ps = sem("fsh_ps")
        y_ready = sem("y_ready")
        dve_link = sem("dve_link")

        block = ctx.enter_context(nc.Block())

        def chunk_of(step):
            if step < STEP_AK:
                return step // 2, step % 2
            if step < STEP_RQ:
                return 8 + (step - STEP_AK) // 4, step % 4
            return 12 + (step - STEP_RQ) // 2, step % 2

        def raw_of(step):
            chunk, part = chunk_of(step)
            width = AKV_W if STEP_AK <= step < STEP_RQ else GW
            return raw[:, chunk % RING, part * width:(part + 1) * width], width

        def raw_value(step):
            turns, up, down = (chunk_of(s)[0] // RING for s in (step, STEP_UP, STEP_DN))
            return 16 * (turns + 1 + min(max(turns + 1 - up, 0), down - up))

        def acc_of(job):
            return job % 4 if job < JOB_GT2 else (job - JOB_GT2) % 4

        def mod_parts(job):
            if job < JOB_SH2:
                return [(1, 4 * job, 4, 0), (0, 4 * job, 4, 4)]
            return [(3 if job < JOB_SC2 else 2, 8 * (job % 2), 8, 0)]

        H_ATT, H_RET, H_UP, H_ACT = KT, KT + 4, KT + 8, 2 * KT + 8

        @block.sync
        def _(sp):
            def load(chunk, reader, src, k):
                if chunk >= RING:
                    sp.wait_ge(lo_ready, reader)
                width = AKV_W if 8 <= chunk < 12 else GW
                sp.dma_start(raw[:, chunk % RING, 0:k * width].rearrange("p (k n) -> p k n", k=k), src)\
                    .then_inc(raw_in[chunk % RING], 16)

            xin = x[0].rearrange("(t p) n -> p t n", p=P)
            for t in range(TT):
                sp.dma_start(xb[:, t, :], xin[:, t, :]).then_inc(x_in, 16)
            sp.dma_start(ident[:, :], eye[:, :]).then_inc(rows_in, 16)
            sp.dma_start(rows[0:KT, 0, 0:P], g_mix[0].rearrange("(k p) -> k p", p=P)).then_inc(rows_in, 16)
            sp.dma_start(rows[KT:2 * KT, 0, 0:P], g_ffn[0].rearrange("(k p) -> k p", p=P)).then_inc(rows_in, 16)
            for j in range(2):
                sp.dma_start(rows[FT * j:FT * (j + 1), 1, 0:P],
                             w_conv[0, j].rearrange("(k p) -> k p", p=P)).then_inc(rows_in, 16)
            sp.dma_start(rows[0:FT, 2, 0:P], w_conv[0, 2].rearrange("(k p) -> k p", p=P)).then_inc(rows_in, 16)
            sp.dma_start(rows[FT:2 * FT, 2, 0:P], b_conv[0].rearrange("(k p) -> k p", p=P)).then_inc(rows_in, 16)
            sp.dma_start(rows[2 * FT:2 * FT + 9, 2, 0:P],
                         b_in[0, COL_AQ:COL_AV].rearrange("(k p) -> k p", p=P)).then_inc(rows_in, 16)
            sp.dma_start(rows[0:8, 3, :], b_in[0, 0:2 * GW].rearrange("(k p) -> k p", p=RD)).then_inc(rows_in, 16)

            w_in_k = w_in[0].rearrange("(k p) n -> p k n", p=P)
            for i in range(8):
                load(i, 2 * (i - 3), w_in_k[:, 2 * i:2 * i + 2, COL_AQ:COL_AQ + GW], 2)
            sp.dma_start(cs, rot[:, :, :]).then_inc(const_in, 16)
            sp.dma_start(mask, masks[:, :]).then_inc(const_in, 16)
            sp.dma_start(gate[:, :], b_in[0:1, COL_RV:COL_AQ].broadcast_to([P, D])).then_inc(const_in, 16)
            sp.dma_start(av_bias[:, :], b_in[0:1, COL_AV:COL_AV + P].broadcast_to([P, P])).then_inc(const_in, 16)
            sp.dma_start(sink_b[:, :], sinks[0:1, :].broadcast_to([P, AH])).then_inc(const_in, 16)
            for i in range(4):
                load(8 + i, 2 * (i + 5), w_in_k[:, 4 * i:4 * i + 4, COL_AK:COL_AK + AKV_W], 4)
            chunk = 12
            for col in (COL_RQ, COL_RK, COL_RV, COL_RG):
                for i in range(8):
                    reader = STEP_AK + 4 * (i + 1) if chunk < 16 else STEP_RQ + 2 * (chunk - 15)
                    load(chunk, reader, w_in_k[:, 2 * i:2 * i + 2, col:col + GW], 2)
                    chunk += 1
            w_out_k = w_out[0].rearrange("(k p) n -> p k n", p=P)
            for group in range(2):
                for i in range(8):
                    k = (2 * i + 8) % KT
                    load(chunk, STEP_RQ + 2 * (chunk - 15), w_out_k[:, k:k + 2, group * GW:(group + 1) * GW], 2)
                    chunk += 1
            w_up_k = w_up[0].rearrange("(k p) (b n) -> p k b n", p=P, b=2)
            with sp.Fori(0, UG) as g:
                with sp.Fori(0, 2) as half:
                    for i in range(4):
                        sp.wait_ge(lo_ready, g * KT + half * LOOP + (STEP_UP - LOOP + 2 * (i + 1)))
                        for j in range(2):
                            sp.dma_start(raw[:, i:i + 1, j * GW:(j + 1) * GW].rearrange("p a (b n) -> p a b n", b=2),
                                         w_up_k[:, bass.ds(half * LOOP + (2 * i + j), 1), :, bass.ds(g * 512, 512)])\
                                .then_inc(raw_in[i], 16)
            w_dn_k = w_down[0].rearrange("(k p) n -> p k n", p=P)

            def down_turn(turn, k0, group, slots):
                for n, i in enumerate(slots):
                    sp.wait_ge(lo_ready, turn * LOOP + (STEP_DN - LOOP + 2 * (i + 1)))
                    sp.dma_start(raw[:, i, :].rearrange("p (k n) -> p k n", k=2),
                                 w_dn_k[:, bass.ds(k0 + 2 * n, 2), group * GW:(group + 1) * GW])\
                        .then_inc(raw_in[i], 16)

            with sp.Fori(0, 5) as turn:
                down_turn(turn, turn * LOOP, 0, range(4))
            down_turn(5, 40, 0, range(2))
            down_turn(5, 0, 1, range(2, 4))
            with sp.Fori(6, 11) as turn:
                down_turn(turn, turn * LOOP - FT, 1, range(4))
            sp.wait_ge(lo_ready, STEPS - 6)
            sp.dma_start(raw[:, 0, :], g_final.rearrange("(a n) -> a n", a=1).broadcast_to([P, D])).then_inc(gfin_in, 16)
            yout = out[0].rearrange("(t p) n -> p t n", p=P)
            for t in range(TT):
                for q in range(2):
                    sp.wait_ge(y_ready, 2 * t + q + 1)
                    sp.dma_start(yout[:, t, q * GW:(q + 1) * GW], xb[:, t, q * GW:(q + 1) * GW]).then_inc(stored, 16)
            sp.wait_ge(stored, 16 * 2 * TT)

        @block.gpsimd
        def _(pool):
            ada_k = w_ada[0].rearrange("(p k) n -> p k n", k=KT)
            ada_2k = w_ada[0, :, 0:2 * D].rearrange("(p k) (s n) -> p k s n", k=KT, s=2)
            fin_k = w_final_ada.rearrange("(p k) n -> p k n", k=KT)

            def column(job):
                if job < JOB_SH2:
                    return job * 512
                part = {JOB_SH2: 3 * D, JOB_SC2: 4 * D, JOB_GT1: 2 * D, JOB_GT2: 5 * D, JOB_FSC: D, JOB_FSH: 0}
                return part[job - job % 2] + (job % 2) * GW

            def start_acc(job):
                a, col = acc[:, acc_of(job), :], column(job)
                before = [j for j in range(job) if acc_of(j) == acc_of(job)]
                if before and before[-1] < JOB_GT1:
                    pool.wait_ge(ada_red, before[-1] + 1)
                elif before:
                    pool.wait_ge(gt_ps, 2 * (before[-1] - JOB_GT1 + 1))
                nc.gpsimd.memset(a, 0.0).then_inc(acc_zero, 1)
                pool.wait_ge(acc_zero, job + 1)
                if job < JOB_SH2:
                    src = b_ada[0:1, 0:2 * D].rearrange("a (s n) -> a s n", s=2)[:, :, col:col + 512]
                    pool.dma_start(a[0:1, :].rearrange("a (s n) -> a s n", s=2), src).then_inc(bias_in, 16)
                elif job < JOB_FSC:
                    pool.dma_start(a[0:1, :], b_ada[0:1, col:col + GW]).then_inc(bias_in, 16)
                else:
                    pool.dma_start(a[0:1, :], b_final_ada[col:col + GW].rearrange("(a n) -> a n", a=1)).then_inc(bias_in, 16)

            def units(job, turn):
                col = column(job)
                for i in range(RING):
                    if job or type(turn) is not int:
                        pool.wait_ge(ada_acc, turn * RING + (KT * job - RING + i + 1))
                    if job < JOB_SH2:
                        src = ada_2k[:, bass.ds(turn * RING + i, 1), :, col:col + 512]
                        dst = ada_raw[:, i:i + 1, :].rearrange("p a (s n) -> p a s n", s=2)
                    else:
                        src = (ada_k if job < JOB_FSC else fin_k)[:, bass.ds(turn * RING + i, 1), col:col + GW]
                        dst = ada_raw[:, i:i + 1, :]
                    pool.dma_start(dst, src).then_inc(ada_in[i], 16)

            pool.dma_start(c_act[:, :], c[0].rearrange("(p k) -> p k", k=KT)).then_inc(cact_in, 16)
            nc.gpsimd.memset(ones[:, :], 1.0).then_inc(ones_ready, 1)
            start_acc(0)
            for job in range(JOBS):
                pool.wait_ge(bias_in, 16 * (job + 1))
                if job < 3:
                    start_acc(job + 1)
                if job == 0:
                    units(0, 0)
                with pool.Fori(0 if job else 1, KT // RING) as turn:
                    units(job, turn)
                if 3 <= job < JOBS - 1:
                    start_acc(job + 1)

        @block.scalar
        def _(act):
            def hi(step):
                src, width = raw_of(step)
                act.wait_ge(raw_in[chunk_of(step)[0] % RING], raw_value(step))
                if step >= RING:
                    act.wait_ge(step_done, step - RING + 1)
                nc.scalar.activation(whi[:, step % RING, 0:width], src, ACT.Copy).then_inc(hi_ready, 1)

            def hi_turn(i, step0, steps):
                if i % 2 == 0:
                    act.wait_ge(raw_in[i // 2], steps * (4 if step0 < STEP_DN else 2) + raw_value(step0))
                act.wait_ge(step_done, steps + (step0 + i - RING + 1))
                nc.scalar.activation(whi[:, i % RING, :], raw[:, i // 2, (i % 2) * GW:(i % 2 + 1) * GW],
                                     ACT.Copy).then_inc(hi_ready, 1)

            def hi_group(step0, start=0, stop=KT):
                for step in range(step0 + start, step0 + stop):
                    hi(step)

            def modulate(k, kind, src, tmp_base, h_base):
                if k >= 2:
                    act.wait_ge(hlo_ready, h_base + k - 1)
                nc.scalar.activation(mod_tmp[:, k % 2, :], src, ACT.Identity, scale=mod_col[:, kind, k:k + 1],
                                     bias=mod_col[:, kind + 1, k:k + 1]).then_inc(tmp_ready, 1)
                act.wait_ge(tmp_ready, tmp_base + k + 1)
                nc.scalar.activation(hhi[:, k, :], mod_tmp[:, k % 2, :], ACT.Copy).then_inc(hhi_ready, 1)

            def root(n, width):
                act.wait_ge(var_ready, n)
                nc.scalar.activation(rstd[:, 0:width], rstd[:, 0:width], ACT.Sqrt).then_inc(rstd_ready, 1)

            act.wait_ge(cact_in, 16)
            nc.scalar.activation(c_act[:, :], c_act[:, :], ACT.Silu).then_inc(cact_ready, 1)
            act.wait_ge(x_in, 32)
            sink = arena[:, 6400:8448]
            for t in range(TT):
                if t:
                    act.wait_ge(ssq_ready, t)
                nc.scalar.activation(sink, xb[:, t, :], ACT.Square, accum_out=ssq[:, t:t + 1]).then_inc(ssq_ready, 1)
            root(1, TT)
            for b in range(0, 8, 2):
                act.wait_ge(xt_ps, b + 1)
                nc.scalar.activation(xT[:, 2 * b:2 * b + 2, :].rearrange("p k s -> p (k s)"), ps[:, b, :],
                                     ACT.Copy).then_inc(xt_even, 1)

            act.wait_ge(xt_odd, 4)
            act.wait_ge(xt_even, 4)
            for job in range(4):
                act.wait_ge(mod_ready, job + 1)
                for k in range(4 * job, 4 * job + 4):
                    modulate(k, 0, xT[:, k, :], 0, 0)
                hi_group(STEP_AQ, 4 * job, 4 * job + 4)
            hi_group(STEP_AK, 0, 4)
            act.wait_ge(step_done, STEP_AK)
            for i in range(8):
                nc.scalar.activation(aqT[:, i, :], ps[:, i // 2, (i % 2) * S:(i % 2 + 1) * S], ACT.Identity,
                                     bias=conv_col2[:, 2 * FT + i:2 * FT + i + 1]).then_inc(aq_ready, 1)
            hi_group(STEP_AK, 4, 16)
            act.wait_ge(step_done, STEP_RQ)
            for head in range(AKV):
                src = slice(AD * head, AD * (head + 1))
                for half in range(2):
                    nc.scalar.activation(k2[AD * half:AD * (half + 1), head, :], ps[src, 4, 0:S], ACT.Identity,
                                         bias=conv_col2[src, 2 * FT + 8:2 * FT + 9]).then_inc(k2_ready, 1)

            def retention_in(step_end, dst, which, done):
                act.wait_ge(step_done, step_end)
                for h in range(RH):
                    for e in range(2):
                        nc.scalar.activation(dst[:, h, e, :], ps[:, 4 + h, e * S:(e + 1) * S], ACT.Identity,
                                             bias=rqk_col[:, e, 4 * which + h:4 * which + h + 1]).then_inc(done, 1)

            def exps(batch):
                act.wait_ge(nm_ready, 2 * batch + 2)
                for i in range(16):
                    pt = (p0, p1)[i % 2][:, i // 2, :]
                    nc.scalar.activation(pt, pt, ACT.Exp, bias=smx[:, 2, i:i + 1], scale=AD ** -0.5,
                                         accum_out=smx[:, 3, i:i + 1]).then_inc(exp_done, 1)
                nc.scalar.activation(smx[:, 4, :], smx[:, 4, :], ACT.Exp).then_inc(esink, 1)

            def att_tile(n):
                act.wait_ge(pt_used, 2 * n + 2)
                nc.scalar.activation(aqT[:, n, :], ps[:, 2 + n % 2, 0:S], ACT.Copy).then_inc(att_ready, 1)

            def attention_out(batch):
                for h in range(8):
                    n = 8 * batch + h
                    act.wait_ge(pt_ps, n + 1)
                    if n >= 2:
                        act.wait_ge(pt_used, n - 1)
                    nc.scalar.activation(pT[:, h % 2, :], ps[:, h % 2, 0:320], ACT.Copy).then_inc(pt_done, 1)
                    if h % 2 == 0 and h:
                        att_tile(4 * batch + h // 2 - 1)
                att_tile(4 * batch + 3)

            hi_group(STEP_RQ)
            retention_in(STEP_RK, qT, 0, rq_raw)
            hi_group(STEP_RK, 0, 8)
            exps(0)
            hi_group(STEP_RK, 8, 16)
            retention_in(STEP_RV, kT, 1, rk_raw)
            attention_out(0)
            hi_group(STEP_RV, 0, 8)
            exps(1)
            hi_group(STEP_RV, 8, 16)
            attention_out(1)
            act.dma_start(dec, decay[:, :, :]).then_inc(dec_in, 16)
            hi_group(STEP_RG)
            act.wait_ge(step_done, STEP_WO0)
            for i in range(4):
                nc.scalar.activation(hhi[:, 8 + 2 * i:10 + 2 * i, :], aqT[:, 2 * i:2 * i + 2, :], ACT.Copy)\
                    .then_inc(hhi_ready, 1)
            hi_group(STEP_WO0, 0, 4)
            for i in range(8):
                h, t = i // 2, i % 2
                act.wait_ge(o_ps, h + 1)
                if i >= 2:
                    act.wait_ge(o_ssq, i - 1)
                nc.scalar.activation(mod_tmp[:, i % 2, :], ps[:, 4 + h, t * RD:(t + 1) * RD], ACT.Square,
                                     accum_out=ssq[:, i:i + 1]).then_inc(o_ssq, 1)
            for t in range(TT):
                act.wait_ge(g_raw, 2 * t + 2)
                nc.scalar.activation(g_sb[:, t, :], g_sb[:, t, :], ACT.Silu).then_inc(g_ready, 1)
            root(2, 8)
            hi_group(STEP_WO0, 4, 8)
            for b in range(4):
                act.wait_ge(mixt_ps, b + 1)
                nc.scalar.activation(hhi[:, 2 * b:2 * b + 2, :].rearrange("p k s -> p (k s)"), ps[:, 4 + b, :],
                                     ACT.Copy).then_inc(hhi_ready, 1)
            act.dma_start(xb[:, :, :], x[0].rearrange("(t p) n -> p t n", p=P)).then_inc(x_again, 16)

            def gate_out(n, blocks, bank0):
                for i, b in enumerate(blocks):
                    act.wait_ge(gt_ps, n + i + 1)
                    nc.scalar.activation(gate[:, b * 512:(b + 1) * 512], ps[:, bank0 + i, :], ACT.Copy).then_inc(gt_ready, 1)

            def squares(n, part, done, sink):
                act.wait_ge(part, n + 1)
                t, b = (n % 4) // 2, 2 * (n // 4) + n % 2
                if n:
                    act.wait_ge(done, n)
                nc.scalar.activation(sink, xb[:, t, b * 512:(b + 1) * 512], ACT.Square,
                                     accum_out=ssq[:, 8 + n:9 + n]).then_inc(done, 1)

            hi_group(STEP_WO0, 8, 16)
            hi_group(STEP_WO1, 0, 4)
            gate_out(0, (0, 1), 4)
            hi_group(STEP_WO1, 4, 11)
            sink = arena[:, 4352:4864]
            for n in range(4):
                hi(STEP_WO1 + 11 + n)
                squares(n, x1_part, x1_ssq, sink)
            hi(STEP_WO1 + 15)
            gate_out(2, (2, 3), 0)
            for n in range(4, 8):
                squares(n, x1_part, x1_ssq, sink)
            root(3, TT)
            act.wait_ge(rstd_ready, 3)
            nc.scalar.activation(xn[:, 1, :], xb[:, 1, :], ACT.Copy, scale=rstd[:, 1:2]).then_inc(xn2_act, 1)
            hi_group(STEP_UP, 0, 2)
            for k in range(KT):
                act.wait_ge(xn2_ps, k - k % 2 + 2)
                modulate(k, 2, ps[:, (k // 2) % 4, (k % 2) * S:(k % 2 + 1) * S], KT, H_UP)
                if k % 2 and k >= 3:
                    hi(STEP_UP + (k + 1) // 2)
            hi(STEP_UP + 9)
            hi_group(STEP_UP, 10, 16)

            def glu_linear(slot, tile, src):
                nc.scalar.activation(slot, src, ACT.Identity, scale=conv_col2[:, bass.ds(tile, 1)],
                                     bias=conv_col2[:, bass.ds(tile + FT, 1)]).then_inc(glu_lin, 1)

            def glu_act(slot, tile):
                act.wait_ge(glu_conv, tile * 2 + 2)
                nc.scalar.activation(slot, slot, ACT.Silu).then_inc(glu_silu, 1)

            with act.Fori(0, UG // 2) as pair:
                with act.Fori(0, 2) as q:
                    for half in range(2):
                        for i in range(LOOP):
                            hi_turn(i, STEP_UP + KT + half * LOOP, pair * 2 * KT + q * KT)
                            if i in (3, 4):
                                m = i - 3
                                glu_linear(glu_tmp[:, 2 * half + m, :], pair * 8 + q * 4 + (half * 2 + m),
                                           ps[:, bass.ds(half + 4 - q * 4, 1), m * S:(m + 1) * S])
                        for m in range(2):
                            glu_act(glu_tmp[:, 2 * half + m, :], pair * 8 + q * 4 + (half * 2 + m))

            def down_turn(turn, tile0, tile_of=None):
                for i in range(LOOP):
                    hi_turn(i, STEP_DN, turn * LOOP)
                    tile = tile0 + i if tile_of is None else tile_of(i)
                    nc.scalar.activation(hhi[:, i, :], actT[:, bass.ds(tile * S, S)], ACT.Copy).then_inc(hhi_ready, 1)

            act.wait_ge(glu_done, FT - 4 + 1)
            down_turn(0, 0)
            act.wait_ge(step_done, STEP_DN)
            for m in range(4):
                glu_linear(glu_tmp[:, m, :], 4 * (UG - 1) + m, ps[:, 4 + m // 2, (m % 2) * S:(m % 2 + 1) * S])
            for m in range(4):
                glu_act(glu_tmp[:, m, :], 4 * (UG - 1) + m)
            down_turn(1, LOOP)
            down_turn(2, 2 * LOOP)
            gate_out(4, range(4), 4)
            with act.Fori(3, 5) as turn:
                down_turn(turn, turn * LOOP)
            act.wait_ge(glu_done, FT + 1)
            down_turn(5, 0, lambda i: 40 + i if i < 4 else i - 4)
            down_turn(6, 4)
            sink = glu_tmp[:, 2:4, :].rearrange("p i s -> p (i s)")
            for n in range(4):
                squares(n, x2_part, x2_ssq, sink)
            with act.Fori(7, 11) as turn:
                down_turn(turn, turn * LOOP - FT)
            for n in range(4, 8):
                squares(n, x2_part, x2_ssq, sink)
            root(4, TT)

        @block.vector
        def _(dve):
            links = [0]

            def link(ins):
                links[0] += 1
                ins.then_inc(dve_link, 1)
                dve.wait_ge(dve_link, links[0])

            def lo(step):
                src, width = raw_of(step)
                dve.wait_ge(hi_ready, step + 1)
                nc.vector.tensor_tensor(wlo[:, step % RING, 0:width], src, whi[:, step % RING, 0:width],
                                        ALU.subtract).then_inc(lo_ready, 1)

            def lo_turn(i, step0, steps):
                dve.wait_ge(hi_ready, steps + (step0 + i + 1))
                nc.vector.tensor_tensor(wlo[:, i % RING, :], raw[:, i // 2, (i % 2) * GW:(i % 2 + 1) * GW],
                                        whi[:, i % RING, :], ALU.subtract).then_inc(lo_ready, 1)

            def ada_row(a, slot, c_col):
                nc.vector.scalar_tensor_tensor(a, ada_raw[:, slot, :], c_col, a, ALU.mult, ALU.add).then_inc(ada_acc, 1)

            def ada(job, k):
                if k == 0:
                    dve.wait_ge(bias_in, 16 * (job + 1))
                dve.wait_ge(ada_in[k % RING], 16 * (4 * job + k // RING + 1))
                if job * KT + k:
                    dve.wait_ge(ada_acc, KT * job + k)
                ada_row(acc[:, acc_of(job), :], k % RING, c_act[:, k:k + 1])

            def ada_turn(job, buf, turn, i):
                if i == 0:
                    dve.wait_ge(bias_in, job * 16 + 16)
                dve.wait_ge(ada_in[i], job * 64 + turn * 16 + 16)
                dve.wait_ge(ada_acc, job * KT + turn * RING + i)
                ada_row(acc[:, bass.ds(buf, 1), :], slice(i, i + 1), c_act[:, bass.ds(turn * RING + i, 1)])

            def mod_cols(job, bank, col0):
                dve.wait_ge(ada_red, job + 1)
                parts = mod_parts(job)
                for kind, k, count, col in parts:
                    src = ps[:, bank, col0 + col:col0 + col + count]
                    dst = mod_col[:, kind, k:k + count]
                    if kind % 2:
                        ins = nc.vector.tensor_copy(dst, src)
                    else:
                        ins = nc.vector.scalar_tensor_tensor(dst, src, 1.0, g_col[:, kind // 2, k:k + count],
                                                             ALU.add, ALU.mult)
                    if kind == parts[-1][0]:
                        ins.then_inc(mod_ready, 1)
                    else:
                        link(ins)

            def h_lo(k, base):
                dve.wait_ge(hhi_ready, base + k + 1)
                return nc.vector.tensor_tensor(hlo[:, k, :], mod_tmp[:, k % 2, :], hhi[:, k, :],
                                               ALU.subtract).then_inc(hlo_ready, 1)

            def rstd_of(dst, src, n):
                link(nc.vector.tensor_scalar(dst, src, 1.0 / n, EPS, ALU.mult, ALU.add))
                nc.vector.reciprocal(dst, dst).then_inc(var_ready, 1)

            dve.wait_ge(ssq_ready, 2)
            rstd_of(rstd[:, 0:2], ssq[:, 0:2], D)
            dve.wait_ge(rstd_ready, 1)
            for t in range(TT):
                nc.vector.tensor_scalar(xb[:, t, :], xb[:, t, :], rstd[:, t:t + 1], None, ALU.mult).then_inc(xn_ready, 1)
            for b in range(1, 8, 2):
                dve.wait_ge(xt_ps, b + 1)
                nc.vector.tensor_copy(xT[:, 2 * b:2 * b + 2, :].rearrange("p k s -> p (k s)"), ps[:, b, :])\
                    .then_inc(xt_odd, 1)
            dve.wait_ge(cols_ps, 5)
            for dst, col, count in ((g_col[:, :, :].rearrange("p i k -> p (i k)"), 0, 2 * KT), (conv_col[:, :], 32, 2 * FT),
                                    (conv_col2[:, :], 128, 2 * FT + 9),
                                    (rqk_col[:, :, :].rearrange("p e h -> p (e h)"), 256, 16)):
                nc.vector.tensor_copy(dst, ps[:, 4, col:col + count]).then_inc(cols_ready, 1)
            dve.wait_ge(cols_ready, 4)
            dve.wait_ge(cact_ready, 1)
            for k in range(KT):
                ada(0, k)
            for job in range(4):
                nxt = list(range(KT)) if job < 3 else []
                for k in nxt[:4]:
                    ada(job + 1, k)
                mod_cols(job, 7, 8 * job)
                for k in range(4 * job, 4 * job + 4):
                    h_lo(k, 0)
                for i in range(4):
                    lo(STEP_AQ + 4 * job + i)
                    for k in nxt[4 + 3 * i:7 + 3 * i]:
                        ada(job + 1, k)
            for step in range(STEP_AK, STEP_RQ):
                lo(step)
            dve.wait_ge(const_in, 16 * 5)
            dve.wait_ge(k2_ready, 4)
            for t in range(TT):
                nc.vector.tensor_tensor(av[:, t, :], ps[:, 4, S + t * P:S + (t + 1) * P], av_bias[:, :],
                                        ALU.add).then_inc(av_ready, 1)

            def group(step0, job, start=0, stop=KT):
                for i in range(start, stop):
                    lo(step0 + i)
                    ada(job, i)

            def rotate(dst, raw_done, n):
                dve.wait_ge(raw_done, 2 * RH)
                ev, od = dst[:, :, 0, :], dst[:, :, 1, :]
                cos, sin = (cs[:, i:i + 1, :].broadcast_to([P, RH, S]) for i in range(2))
                nc.vector.tensor_tensor(rot_tmp[:, 0], od, sin, ALU.mult).then_inc(rot_done, 1)
                nc.vector.tensor_tensor(rot_tmp[:, 1], ev, sin, ALU.mult).then_inc(rot_done, 1)
                dve.wait_ge(rot_done, n + 2)
                nc.vector.tensor_tensor(ev, ev, cos, ALU.mult).then_inc(rot_done, 1)
                nc.vector.tensor_tensor(od, od, cos, ALU.mult).then_inc(rot_done, 1)
                dve.wait_ge(rot_done, n + 3)
                nc.vector.tensor_tensor(ev, ev, rot_tmp[:, 0], ALU.subtract).then_inc(rot_done, 1)
                dve.wait_ge(rot_done, n + 4)
                nc.vector.tensor_tensor(od, od, rot_tmp[:, 1], ALU.add).then_inc(rot_done, 1)

            def scores(batch):
                for i in range(16):
                    t, n = i % 2, 16 * batch + i
                    dve.wait_ge(sc_ps, n + 1)
                    pt, mk = ((p0, mask[:, 0:P]), (p1, mask[:, P:P + S]))[t]
                    nc.vector.tensor_tensor_reduce(pt[:, i // 2, :], ps[:, i % 4, 0:(1 + t) * P], mk, 1.0, -3e38,
                                                   ALU.add, ALU.max, smx[:, 0, i:i + 1]).then_inc(sc_done, 1)
                dve.wait_ge(sc_done, 16 * batch + 16)
                sk = sink_b[:, 8 * batch:8 * batch + 8].rearrange("p (h a) -> p h a", a=1).broadcast_to([P, 8, 2])

                def pair(r):
                    return smx[:, r, :].rearrange("p (h a) -> p h a", a=2)

                link(nc.vector.scalar_tensor_tensor(pair(1), pair(0), AD ** -0.5, sk, ALU.mult, ALU.max))
                nc.vector.tensor_scalar(smx[:, 2, :], smx[:, 1, :], -1.0, None, ALU.mult).then_inc(nm_ready, 1)
                nc.vector.tensor_tensor(pair(4), sk, pair(1), ALU.subtract).then_inc(nm_ready, 1)

            def normalise(batch):
                dve.wait_ge(exp_done, 16 * batch + 16)
                dve.wait_ge(esink, batch + 1)
                link(nc.vector.tensor_tensor(smx[:, 5, :], smx[:, 3, :], smx[:, 4, :], ALU.add))
                link(nc.vector.reciprocal(smx[:, 5, :], smx[:, 5, :]))
                for i in range(16):
                    pt = (p0, p1)[i % 2][:, i // 2, :]
                    nc.vector.tensor_scalar(pt, pt, smx[:, 5, i:i + 1], None, ALU.mult).then_inc(p_norm, 1)

            group(STEP_RQ, 4)
            rotate(qT, rq_raw, 0)
            scores(0)
            group(STEP_RK, 5, 0, 8)
            normalise(0)
            group(STEP_RK, 5, 8, 16)
            rotate(kT, rk_raw, 6)
            scores(1)
            group(STEP_RV, 6, 0, 8)
            normalise(1)
            group(STEP_RV, 6, 8, 16)
            mod_cols(4, 0, 0)
            mod_cols(5, 1, 0)
            dve.wait_ge(rot_done, 12)
            dve.wait_ge(step_done, STEP_RG)
            for i in range(4):
                t, b = i // 2, i % 2
                nc.vector.tensor_tensor(v_sb[:, t, b * 512:(b + 1) * 512], ps[:, 4 + i, :],
                                        gate[:, b * 512:(b + 1) * 512], ALU.add).then_inc(v_ready, 1)
            group(STEP_RG, 7)
            dve.wait_ge(dec_in, 16)
            for h in range(RH):
                dve.wait_ge(st_ps, h + 1)
                nc.vector.tensor_tensor(sT[:, h, :], ps[:, 4 + h, 0:384], dec[:, h, :], ALU.mult).then_inc(st_ready, 1)
            for i in range(4):
                dve.wait_ge(hhi_ready, H_ATT + i + 1)
                nc.vector.tensor_tensor(hlo[:, 8 + 2 * i:10 + 2 * i, :], aqT[:, 2 * i:2 * i + 2, :],
                                        hhi[:, 8 + 2 * i:10 + 2 * i, :], ALU.subtract).then_inc(hlo_ready, 1)
            lo(STEP_WO0)
            lo(STEP_WO0 + 1)
            for i in range(4):
                t, b = i // 2, i % 2
                nc.vector.tensor_tensor(g_sb[:, t, b * 512:(b + 1) * 512], ps[:, i, :],
                                        gate[:, GW + b * 512:GW + (b + 1) * 512], ALU.add).then_inc(g_raw, 1)
            for i in range(2, 4):
                lo(STEP_WO0 + i)
            dve.wait_ge(o_ssq, 8)
            rstd_of(rstd[:, 0:8], ssq[:, 0:8], RD)
            dve.wait_ge(rstd_ready, 2)
            for i in range(8):
                h, t = i // 2, i % 2
                if i < 2:
                    dve.wait_ge(g_ready, t + 1)
                g = g_sb[:, t, h * RD:(h + 1) * RD]
                nc.vector.scalar_tensor_tensor(g, ps[:, 4 + h, t * RD:(t + 1) * RD], rstd[:, i:i + 1], g,
                                               ALU.mult, ALU.mult).then_inc(mix_ready, 1)
            for i in range(4, 8):
                lo(STEP_WO0 + i)
            for b in range(4):
                dve.wait_ge(hhi_ready, H_RET + b + 1)
                nc.vector.tensor_tensor(hlo[:, 2 * b:2 * b + 2, :].rearrange("p k s -> p (k s)"), ps[:, 4 + b, :],
                                        hhi[:, 2 * b:2 * b + 2, :].rearrange("p k s -> p (k s)"),
                                        ALU.subtract).then_inc(hlo_ready, 1)
            for i in range(8, 16):
                lo(STEP_WO0 + i)
                ada(8, 2 * (i - 8))
                ada(8, 2 * (i - 8) + 1)

            def residual(n, bank0, part, gt_base, res_tmp):
                t, b = (n % 4) // 2, 2 * (n // 4) + n % 2
                dve.wait_ge(gt_ready, gt_base + b + 1)
                link(nc.vector.tensor_tensor(res_tmp, ps[:, bank0 + n % 4, :], gate[:, b * 512:(b + 1) * 512], ALU.mult))
                xs = xb[:, t, b * 512:(b + 1) * 512]
                nc.vector.tensor_tensor(xs, xs, res_tmp, ALU.add).then_inc(part, 1)
                dve.wait_ge(part, n + 1)

            dve.wait_ge(x_again, 16)
            for i in range(16):
                lo(STEP_WO1 + i)
                if i < 8:
                    ada(9, 2 * i)
                    ada(9, 2 * i + 1)
                if 8 <= i < 12:
                    residual(i - 8, 0, x1_part, 0, res1_tmp)
            dve.wait_ge(step_done, STEP_UP)
            for n in range(4, 8):
                residual(n, 4, x1_part, 0, res1_tmp)

            def total_rstd(done):
                dve.wait_ge(done, 8)
                s = ssq[:, 8:16].rearrange("p (g t b) -> p t g b", g=2, t=2)
                half = ssq[:, 0:4].rearrange("p (t b) -> p t b", t=2)
                link(nc.vector.tensor_tensor(half, s[:, :, 0, :], s[:, :, 1, :], ALU.add))
                link(nc.vector.tensor_tensor(rstd[:, 0:2].rearrange("p (t b) -> p t b", b=1), half[:, :, 0:1], half[:, :, 1:2],
                                             ALU.add))
                rstd_of(rstd[:, 0:2], rstd[:, 0:2], D)

            mod_cols(6, 2, 0)
            mod_cols(7, 3, 0)
            total_rstd(x1_ssq)
            dve.wait_ge(rstd_ready, 3)
            nc.vector.tensor_scalar(xn[:, 0, :], xb[:, 0, :], rstd[:, 0:1], None, ALU.mult).then_inc(xn2_dve, 1)
            lo(STEP_UP)
            lo(STEP_UP + 1)
            for k in range(KT):
                ins = h_lo(k, H_UP)
                if k % 2 and k >= 3:
                    lo(STEP_UP + (k + 1) // 2)
            dve.wait_ge(hlo_ready, H_ACT)
            lo(STEP_UP + 9)
            nc.vector.memset(ssq[:, 0:1], 0.0).then_inc(glu_done, 1)
            for i in range(10, 16):
                lo(STEP_UP + i)

            def taps(tile, bank_tiles, slot, bank):
                dve.wait_ge(glu_lin, bank_tiles)
                for d in (1, 2):
                    if d == 2:
                        dve.wait_ge(glu_conv, tile * 2 + 1)
                    nc.vector.scalar_tensor_tensor(slot(d), bank(d), conv_col[:, bass.ds(tile + (2 - d) * FT, 1)], slot(d),
                                                   ALU.mult, ALU.add).then_inc(glu_conv, 1)

            def glu_product(tile, slot, b_branch):
                dve.wait_ge(glu_silu, tile + 1)
                return nc.vector.tensor_tensor(actT[:, bass.ds(tile * S, S)], slot, b_branch, ALU.mult)

            def up_pair(pair, with_ada):
                with dve.Fori(0, 2) as q:
                    with dve.Fori(0, 2) as half:
                        for i in range(LOOP):
                            lo_turn(i, STEP_UP + KT, pair * 2 * KT + q * KT + half * LOOP)
                            if i in (5, 6):
                                m = i - 5
                                taps(pair * 8 + q * 4 + half * 2 + m, pair * 8 + q * 4 + half * 2 + 2,
                                     lambda d: glu_tmp[:, bass.ds(half * 2 + m, 1), d:S],
                                     lambda d: ps[:, bass.ds(half - q * 4 + 4, 1), m * S:(m + 1) * S - d])
                            if with_ada and i % 2:
                                ada_turn(pair + JOB_GT2, pair, q * 2 + half, i // 2)
                        for m in range(2):
                            glu_product(pair * 8 + q * 4 + half * 2 + m, glu_tmp[:, bass.ds(half * 2 + m, 1), :],
                                        ps[:, bass.ds(half - q * 4 + 6, 1), m * S:(m + 1) * S]).then_inc(glu_done, 1)

            with dve.Fori(0, ADA_PAIRS) as pair:
                up_pair(pair, True)
            with dve.Fori(ADA_PAIRS, UG // 2) as pair:
                up_pair(pair, False)

            def down_turn(turn, ada_of=None):
                for i in range(LOOP):
                    dve.wait_ge(hhi_ready, turn * LOOP + (H_ACT + i + 1))
                    tile = down_tile(turn, i)
                    nc.vector.tensor_tensor(hlo[:, i, :], actT[:, bass.ds(tile * S, S)], hhi[:, i, :],
                                            ALU.subtract).then_inc(hlo_ready, 1)
                    lo_turn(i, STEP_DN, turn * LOOP)
                    if ada_of is not None:
                        ada_of(i)

            def down_tile(turn, i):
                if type(turn) is int:
                    return (turn * LOOP + i) % FT
                return turn * LOOP + i - down_group[0] * FT

            down_group = [0]
            down_turn(0)
            for m in range(4):
                taps(4 * (UG - 1) + m, 4 * (UG - 1) + m - m % 2 + 2, lambda d: glu_tmp[:, m, d:S], lambda d: ps[:, 4 + m // 2, (m % 2) * S:(m % 2 + 1) * S - d])
            for m in range(4):
                glu_product(4 * (UG - 1) + m, glu_tmp[:, m, :], ps[:, 6 + m // 2, (m % 2) * S:(m % 2 + 1) * S])\
                    .then_inc(glu_done, 1)
            with dve.Fori(1, 5) as turn:
                down_turn(turn)
            down_turn(5)
            down_turn(6)
            dve.wait_ge(step_done, STEP_DN + FT)
            for n in range(4):
                residual(n, 0, x2_part, 4, res2_tmp)
            down_group[0] = 1
            with dve.Fori(0, 2) as job:
                with dve.Fori(0, 2) as half:
                    down_turn(job * 2 + half + 7, lambda i: ada_turn(job + JOB_FSH, job, half * 2 + i // RING, i % RING))
            dve.wait_ge(step_done, STEPS)
            for n in range(4, 8):
                residual(n, 4, x2_part, 4, res2_tmp)
            dve.wait_ge(gfin_in, 16)
            for b in range(4):
                dve.wait_ge(fsc_ps, b + 1)
                g = raw[:, 0, b * 512:(b + 1) * 512]
                link(nc.vector.scalar_tensor_tensor(g, ps[:, b, :], 1.0, g, ALU.add, ALU.mult))
            total_rstd(x2_ssq)
            dve.wait_ge(rstd_ready, 4)
            for t in range(TT):
                for q in range(2):
                    xs = xb[:, t, q * GW:(q + 1) * GW]
                    link(nc.vector.scalar_tensor_tensor(xs, xs, rstd[:, t:t + 1], raw[:, 0, q * GW:(q + 1) * GW],
                                                        ALU.mult, ALU.mult))
                    dve.wait_ge(fsh_ps, 2 * q + 2)
                    xs = xs.rearrange("p (b n) -> p b n", b=2)
                    nc.vector.tensor_tensor(xs, xs, ps[:, 4 + 2 * q:6 + 2 * q, :], ALU.add).then_inc(y_ready, 1)

        @block.tensor
        def _(pe):
            def passes(out_ap, lhs, rhs, start, skip):
                nc.tensor.matmul(out_ap, lhs[0], rhs[0], start=start, stop=False, skip_group_check=skip)
                nc.tensor.matmul(out_ap, lhs[0], rhs[1], start=False, stop=False, skip_group_check=skip)
                return nc.tensor.matmul(out_ap, lhs[1], rhs[0], start=False, stop=True, skip_group_check=skip)

            def columns(slot, k, start, bank_of, cols=None):
                for m in range(8):
                    c0 = cols(m) if cols else slice(m * P, (m + 1) * P)
                    last = passes(bank_of(m // 2)[:, (m % 2) * S:(m % 2 + 1) * S],
                                  (whi[:, slot, c0], wlo[:, slot, c0]), (hhi[:, k, :], hlo[:, k, :]),
                                  start and m % 2 == 0, True)
                last.then_inc(step_done, 1)

            def tokens(slot, k, start, bank0):
                for t in range(TT):
                    for b in range(2):
                        ts, cb = slice(t * P, (t + 1) * P), slice(b * 512, (b + 1) * 512)
                        last = passes(ps[:, bank0 + 2 * t + b, :], (hhi[:, k, ts], hlo[:, k, ts]),
                                      (whi[:, slot, cb], wlo[:, slot, cb]), start, True)
                last.then_inc(step_done, 1)

            def sum_columns(job, bank, col0):
                pe.wait_ge(ada_acc, KT * (job + 1))
                for i in range(8):
                    last = nc.tensor.matmul(ps[:, bank, col0 + i:col0 + i + 1], acc[:, acc_of(job), i * P:(i + 1) * P],
                                            ones[:, 0:1], start=True, stop=True)
                last.then_inc(ada_red, 1)

            def sum_rows(job, bank0, done, free=None):
                pe.wait_ge(ada_acc, KT * (job + 1))
                for b in range(2):
                    if free:
                        pe.wait_ge(*free[b])
                    nc.tensor.matmul(ps[:, bank0 + b, :], ones[:, :], acc[:, acc_of(job), b * 512:(b + 1) * 512],
                                     start=True, stop=True).then_inc(done, 1)

            pe.wait_ge(rows_in, 16 * 9)
            pe.wait_ge(xn_ready, TT)
            for k in range(KT):
                for t in range(TT):
                    c0 = (k % 2) * S + t * P
                    last = nc.tensor.transpose(ps[:, k // 2, c0:c0 + P], xb[:, t, k * P:(k + 1) * P], ident[:, :])
                if k % 2:
                    last.then_inc(xt_ps, 1)
            pe.wait_ge(xt_even, 4)
            pe.wait_ge(xt_odd, 4)
            for col, n, src in ((0, 2 * KT, rows[0:2 * KT, 0, 0:P]), (32, 2 * FT, rows[0:2 * FT, 1, 0:P]),
                                (128, 2 * FT + 9, rows[0:2 * FT + 9, 2, 0:P]), (256, 8, rows[0:8, 3, 0:RD:2]),
                                (264, 8, rows[0:8, 3, 1:RD:2])):
                nc.tensor.transpose(ps[:, 4, col:col + n], src, ident[0:n, 0:n]).then_inc(cols_ps, 1)
            pe.wait_ge(ones_ready, 1)
            for job in range(4):
                if job:
                    pe.wait_ge(mod_ready, job)
                sum_columns(job, 7, 8 * job)
                for k in range(4 * job, 4 * job + 4):
                    pe.wait_ge(hlo_ready, k + 1)
                    pe.wait_ge(lo_ready, STEP_AQ + k + 1)
                    columns(k % RING, k, k == 0, lambda b: ps[:, b, :])
            pe.wait_ge(cols_ready, 4)
            for k in range(KT):
                pe.wait_ge(lo_ready, STEP_AK + k + 1)
                slot = k % RING
                passes(ps[:, 4, 0:S], (whi[:, slot, 0:P], wlo[:, slot, 0:P]), (hhi[:, k, :], hlo[:, k, :]), k == 0, True)
                for t in range(TT):
                    ts = slice(t * P, (t + 1) * P)
                    last = passes(ps[:, 4, S + t * P:S + (t + 1) * P], (hhi[:, k, ts], hlo[:, k, ts]),
                                  (whi[:, slot, P:2 * P], wlo[:, slot, P:2 * P]), False, True)
                last.then_inc(step_done, 1)

            def group_columns(step0, cols=None):
                for k in range(KT):
                    pe.wait_ge(lo_ready, step0 + k + 1)
                    columns(k % RING, k, k == 0, lambda b: ps[:, 4 + b, :], cols)

            def group_tokens(step0, bank0):
                for k in range(KT):
                    pe.wait_ge(lo_ready, step0 + k + 1)
                    tokens(k % RING, k, k == 0, bank0)

            def split_dims(m):
                return slice((m // 2) * RD + m % 2, (m // 2 + 1) * RD, 2)

            def att_scores(batch):
                for i in range(16):
                    n, h, t = 16 * batch + i, i // 2, i % 2
                    if i >= 4:
                        pe.wait_ge(sc_done, n - 3)
                    half = slice(AD * (h % 2), AD * (h % 2 + 1))
                    nc.tensor.matmul(ps[:, i % 4, 0:(1 + t) * P], aqT[half, 4 * batch + h // 2, t * P:(t + 1) * P],
                                     k2[half, batch, 0:(1 + t) * P], start=True, stop=True).then_inc(sc_ps, 1)

            def att_values(batch, h):
                n = 8 * batch + h
                pe.wait_ge(pt_done, n + 1)
                if h % 2 == 0 and h >= 4:
                    pe.wait_ge(att_ready, n // 2 - 1)
                o = ps[AD * (h % 2):AD * (h % 2 + 1), 2 + (h // 2) % 2, :]
                v0, v1 = (av[:, t, AD * batch:AD * (batch + 1)] for t in range(TT))
                pr = pT[:, h % 2, :]
                nc.tensor.matmul(o[:, 0:P], v0, pr[:, 0:P], start=True, stop=True, skip_group_check=True)
                nc.tensor.matmul(o[:, P:2 * P], v1, pr[:, 192:320], start=False, stop=False, skip_group_check=True)
                last = nc.tensor.matmul(o[:, P:P + 64], v0, pr[:, P:192], start=False, stop=True, skip_group_check=True)
                last.then_inc(pt_used, 1)

            def attention(batch):
                for h in range(8):
                    n = 8 * batch + h
                    pe.wait_ge(p_norm, 16 * batch + 2 * h + 2)
                    if h >= 2:
                        pe.wait_ge(pt_done, n - 1)
                    bank = ps[:, h % 2, :]
                    nc.tensor.transpose(bank[:, 0:P], p0[:, h, :], ident[:, :])
                    nc.tensor.transpose(bank[:, P:192], p1[0:64, h, 0:P], ident[0:64, 0:64])
                    nc.tensor.transpose(bank[:, 192:320], p1[:, h, P:2 * P], ident[:, :]).then_inc(pt_ps, 1)
                    if h:
                        att_values(batch, h - 1)
                att_values(batch, 7)

            pe.wait_ge(k2_ready, 4)
            pe.wait_ge(av_ready, 2)
            pe.wait_ge(mod_ready, 4)
            group_columns(STEP_RQ, split_dims)
            pe.wait_ge(aq_ready, 8)
            att_scores(0)
            pe.wait_ge(rq_raw, 8)
            group_columns(STEP_RK, split_dims)
            attention(0)
            pe.wait_ge(att_ready, 4)
            att_scores(1)
            pe.wait_ge(rk_raw, 8)
            group_tokens(STEP_RV, 4)
            attention(1)
            pe.wait_ge(att_ready, 8)
            for job in (4, 5):
                sum_columns(job, job - 4, 0)
            pe.wait_ge(mod_ready, 6)
            group_tokens(STEP_RG, 0)
            pe.wait_ge(rot_done, 12)
            pe.wait_ge(v_ready, 4)
            for h in range(RH):
                for m, cols in ((0, slice(0, S)), (1, slice(P, S))):
                    o = ps[:, 4 + h, m * S:m * S + cols.stop - cols.start]
                    for e in range(2):
                        last = nc.tensor.matmul(o, kT[:, h, e, m * P:(m + 1) * P], qT[:, h, e, cols],
                                                start=m == 0 and e == 0, stop=e == 1, skip_group_check=True)
                last.then_inc(st_ps, 1)
            for h in range(RH):
                pe.wait_ge(st_ready, h + 1)
                v0, v1 = (v_sb[:, t, h * RD:(h + 1) * RD] for t in range(TT))
                o = ps[:, 4 + h, :]
                nc.tensor.matmul(o[:, 0:RD], sT[:, h, 0:P], v0, start=True, stop=True, skip_group_check=True)
                nc.tensor.matmul(o[:, RD:2 * RD], sT[:, h, P:2 * P], v0, start=False, stop=False, skip_group_check=True)
                nc.tensor.matmul(o[:, RD:2 * RD], sT[:, h, S:S + P], v1, start=False, stop=True, skip_group_check=True)\
                    .then_inc(o_ps, 1)
            pe.wait_ge(g_raw, 4)
            for i in range(8):
                if i % 2 == 0:
                    pe.wait_ge(hlo_ready, H_ATT + i // 2 + 1)
                pe.wait_ge(lo_ready, STEP_WO0 + i + 1)
                tokens(i % RING, 8 + i, i == 0, 0)
            for b in range(4):
                pe.wait_ge(mix_ready, 2 * b + 2)
                for j in range(4):
                    k, t = 2 * b + j // 2, j % 2
                    last = nc.tensor.transpose(ps[:, 4 + b, j * P:(j + 1) * P], g_sb[:, t, k * P:(k + 1) * P], ident[:, :])
                last.then_inc(mixt_ps, 1)
            for i in range(8, 16):
                if i % 2 == 0:
                    pe.wait_ge(hlo_ready, H_RET + (i - 8) // 2 + 1)
                pe.wait_ge(lo_ready, STEP_WO0 + i + 1)
                tokens(i % RING, i - 8, False, 0)
            sum_rows(JOB_GT1, 4, gt_ps)
            pe.wait_ge(gt_ready, 2)
            for i in range(16):
                pe.wait_ge(lo_ready, STEP_WO1 + i + 1)
                tokens(i % RING, (8 + i) % KT, i == 0, 4)
                if i == 13:
                    pe.wait_ge(x1_part, 4)
                    sum_rows(JOB_GT1 + 1, 0, gt_ps)
            for job in (6, 7):
                sum_columns(job, job - 4, 0)
            pe.wait_ge(xn2_dve, 1)
            pe.wait_ge(xn2_act, 1)
            pe.wait_ge(gt_ready, 4)
            pe.wait_ge(mod_ready, 8)
            for k in range(KT):
                if k >= 8 and k % 2 == 0:
                    pe.wait_ge(tmp_ready, KT + k - 6)
                for t in range(TT):
                    c0 = (k % 2) * S + t * P
                    last = nc.tensor.transpose(ps[:, (k // 2) % 4, c0:c0 + P], xn[:, t, k * P:(k + 1) * P], ident[:, :])
                last.then_inc(xn2_ps, 1)
            pe.wait_ge(x1_part, 8)
            for k in range(KT):
                pe.wait_ge(hlo_ready, H_UP + k + 1)
                pe.wait_ge(lo_ready, STEP_UP + k + 1)
                columns(k % RING, k, k == 0, lambda b: ps[:, 4 + b, :])
            with pe.Fori(0, UG // 2) as pair:
                with pe.Fori(0, 2) as q:
                    pe.wait_ge(glu_done, pair * 8 + q * 4 + 1)
                    for k in range(KT):
                        pe.wait_ge(lo_ready, pair * 2 * KT + q * KT + (STEP_UP + KT + k + 1))
                        columns(k % RING, k, k == 0, lambda b: ps[:, bass.ds(q * 4 + b, 1), :].rearrange("p a n -> p (a n)"))
            def down_turn(turn, start, bank_of):
                for i in range(LOOP):
                    pe.wait_ge(hlo_ready, turn * LOOP + (H_ACT + i + 1))
                    pe.wait_ge(lo_ready, turn * LOOP + (STEP_DN + i + 1))
                    tokens(i % RING, i, start == i, bank_of(i))

            pe.wait_ge(glu_done, FT - 4 + 1)
            down_turn(0, 0, lambda i: 0)
            down_turn(1, None, lambda i: 0)
            pe.wait_ge(glu_done, FT + 1)
            sum_rows(JOB_GT2, 4, gt_ps)
            sum_rows(JOB_GT2 + 1, 6, gt_ps)
            with pe.Fori(2, 5) as turn:
                down_turn(turn, None, lambda i: 0)
            pe.wait_ge(gt_ready, 8)
            down_turn(5, 4, lambda i: 0 if i < 4 else 4)
            with pe.Fori(6, 11) as turn:
                down_turn(turn, None, lambda i: 4)
            pe.wait_ge(x2_part, 4)
            for half in range(2):
                sum_rows(JOB_FSC + half, 2 * half, fsc_ps)
            for half in range(2):
                sum_rows(JOB_FSH + half, 4 + 2 * half, fsh_ps, [(x2_part, 5 + 2 * half + b) for b in range(2)])


_INS = ["x", "c", "w_ada", "b_ada", "g_mix", "w_in", "b_in", "sinks", "w_out", "g_ffn", "w_up", "w_conv", "b_conv",
        "w_down", "w_final_ada", "b_final_ada", "g_final"]


def _constants():
    f32 = np.float32
    freq = f32(10000.0) ** -np.linspace(0.0, 1.0, RD // 2, dtype=f32)
    angle = (freq[:, None] * np.arange(S, dtype=f32)[None, :]).astype(np.float64)
    rot = np.stack([np.cos(angle), np.sin(angle)], axis=1).astype(f32)
    pos = np.arange(S)
    gap = np.abs(pos[None, :] - pos[:, None])
    seen = (pos[None, :] // CHUNK) >= (pos[:, None] // CHUNK)
    decay = np.zeros((P, RH, 384))
    for h in range(RH):
        d = np.where(seen, (1.0 - 2.0 ** (-5.0 - h)) ** gap, 0.0) * RD ** -0.5
        decay[:, h, 0:S] = d[0:P]
        decay[:, h, S:] = d[P:, P:]
    behind = (pos[:, None] // CHUNK) - (pos[None, :] // CHUNK)
    hidden = np.where((behind >= 0) & (behind < 2), 0.0, -1e30)
    masks = np.concatenate([hidden[0:P, 0:P], hidden[P:, :]], axis=1)
    return {"rot": rot, "decay": decay.astype(f32), "masks": masks.astype(f32), "eye": np.eye(P, dtype=f32)}


def kernel(**inputs):
    import concourse.bacc as bacc
    from concourse.bass_utils import run_bass_kernel_spmd

    nc = bacc.Bacc("TRN2", target_bir_lowering=False, num_devices=1)
    arrays, args = {}, []
    given = {name: np.ascontiguousarray(inputs[name]) for name in _INS} | _constants()
    for name, a in given.items():
        arrays[f"in_{name}"] = a
        args.append(nc.dram_tensor(f"in_{name}", a.shape, mybir.dt.from_np(a.dtype), kind="ExternalInput").ap())
    args.append(nc.dram_tensor("out_y", (1, S, D), F32, kind="ExternalOutput").ap())
    build(nc, *args)
    r = run_bass_kernel_spmd(nc, [arrays], core_ids=[0])
    return r.results[0]["out_y"]
```

```python
from contextlib import ExitStack

import numpy as np

import concourse.bass as bass
from concourse import mybir

F32 = mybir.dt.float32
F32R = mybir.dt.float32r
ALU = mybir.AluOpType
ACT = mybir.ActivationFunctionType

P = 128
D, S, FF = 2048, 256, 5632
CHUNK = 64
KT = D // P
TT = S // P
RH, RD = 4, 256
AH, AKV, AD = 16, 2, 64
FT = FF // P
EPS = 1e-6
GW = 1024
RING = 4

COL_RQ, COL_RK, COL_RV, COL_RG, COL_AQ, COL_AK = (i * GW for i in range(6))
COL_AV = COL_AK + AKV * AD
AKV_W = 2 * AKV * AD

AK_TILES = GW // AKV_W
STEP_AQ, STEP_AK = 0, KT
STEP_RQ, STEP_RK, STEP_RV, STEP_RG, STEP_WO0, STEP_WO1, STEP_UP = (STEP_AK + KT // AK_TILES + KT * i for i in range(7))
UG = FF // (GW // 2)
STEP_DN = STEP_UP + UG * KT
STEPS = STEP_DN + 2 * FT
LOOP = 8
ADA_PAIRS = 4

JOB_SH2, JOB_SC2, JOB_GT1, JOB_GT2, JOB_FSC, JOB_FSH = 4, 6, 8, 10, 12, 14
JOBS = 16


def build(nc, x, c, w_ada, b_ada, g_mix, w_in, b_in, sinks, w_out, g_ffn, w_up, w_conv, b_conv,
          w_down, w_final_ada, b_final_ada, g_final, rot, decay, masks, eye, out):
    ctx = ExitStack()
    with ctx:
        def sb(name, shape, dt=F32):
            return ctx.enter_context(nc.sbuf_tensor(name, shape, dt))

        def sem(name):
            return ctx.enter_context(nc.semaphore(name))

        raw = sb("raw", [P, RING, 2 * GW])
        whi = sb("whi", [P, RING, GW], F32R)
        wlo = sb("wlo", [P, RING, GW], F32R)
        hhi = sb("hhi", [P, KT, S], F32R)
        hlo = sb("hlo", [P, KT, S], F32R)
        ada_raw = sb("ada_raw", [P, RING, GW])
        acc = sb("acc", [P, 4, GW])
        xb = sb("xb", [P, TT, D])
        gate = sb("gate", [P, D])
        arena = sb("arena", [P, 12288])
        ident = sb("ident", [P, P])
        ones = sb("ones", [P, P])
        av_bias = sb("av_bias", [P, P])
        c_act = sb("c_act", [P, KT])
        g_col = sb("g_col", [P, 2, KT])
        conv_col = sb("conv_col", [P, 2 * FT])
        conv_col2 = sb("conv_col2", [P, 2 * FT + 9])
        rqk_col = sb("rqk_col", [P, 2, 8])
        mod_col = sb("mod_col", [P, 4, KT])
        sink_b = sb("sink_b", [P, AH])
        ssq = sb("ssq", [P, 16])
        rstd = sb("rstd", [P, 8])
        smx = sb("smx", [P, 6, 16])
        aqT = arena[:, 0:2048].rearrange("p (i s) -> p i s", s=S)
        k2 = arena[:, 2048:2560].rearrange("p (i s) -> p i s", s=S)
        av = arena[:, 2560:2816].rearrange("p (t d) -> p t d", d=P)
        cs = arena[:, 2816:3328].rearrange("p (i s) -> p i s", s=S)
        p0 = arena[:, 3328:4352].rearrange("p (h k) -> p h k", k=P)
        p1 = arena[:, 4352:6400].rearrange("p (h k) -> p h k", k=S)
        dec = arena[:, 3328:4864].rearrange("p (h k) -> p h k", k=384)
        sT = arena[:, 4864:6400].rearrange("p (h k) -> p h k", k=384)
        rows = arena[:, 3328:3328 + 4 * 256].rearrange("p (i n) -> p i n", n=256)
        qT = arena[:, 6400:8448].rearrange("p (h e s) -> p h e s", e=2, s=S)
        kT = arena[:, 8448:10496].rearrange("p (h e s) -> p h e s", e=2, s=S)
        ada_more = [arena[:, c:c + GW] for c in (0, GW, 4352, 4352 + GW)]
        xT = arena[:, 6400:10496].rearrange("p (k s) -> p k s", s=S)
        mask = arena[:, 10496:10880]
        pT = arena[:, 10880:11520].rearrange("p (i k) -> p i k", k=320)
        mod_tmp = arena[:, 11520:12032].rearrange("p (i s) -> p i s", s=S)
        rot_tmp = xb[:, 0, :].rearrange("p (i h s) -> p i h s", i=2, s=S)
        v_sb = xb[:, 0, :].rearrange("p (t e) -> p t e", t=TT)
        g_sb = xb[:, 1, :].rearrange("p (t e) -> p t e", t=TT)
        xn = arena[:, 0:4096].rearrange("p (t n) -> p t n", t=TT)
        actT = arena[:, 0:FT * S]
        glu_tmp = arena[:, FT * S:FT * S + 4 * S].rearrange("p (i s) -> p i s", s=S)
        g_fin = acc[:, 2:4, :].rearrange("p a n -> p (a n)")
        res1_tmp, res2_tmp = (a.rearrange("p i s -> p (i s)") for a in (mod_tmp, glu_tmp[:, 0:2, :]))

        ps = ctx.enter_context(nc.psum_tensor("ps", [P, 8, 512], F32))

        x_in = sem("x_in")
        rows_in = sem("rows_in")
        const_in = sem("const_in")
        cact_in = sem("cact_in")
        x_again = sem("x_again")
        dec_in = sem("dec_in")
        gfin_in = sem("gfin_in")
        stored = sem("stored")
        raw_in = [sem(f"raw_in{i}") for i in range(RING)]
        ada_in = [sem(f"ada_in{i}") for i in range(2 * RING)]
        bias_in = sem("bias_in")
        hi_ready = sem("hi_ready")
        lo_ready = sem("lo_ready")
        step_done = sem("step_done")
        acc_zero = sem("acc_zero")
        ada_acc = sem("ada_acc")
        ada_pe = sem("ada_pe")
        ada_red = sem("ada_red")
        mod_ready = sem("mod_ready")
        cact_ready = sem("cact_ready")
        ones_ready = sem("ones_ready")
        ssq_ready = sem("ssq_ready")
        xn_ready = sem("xn_ready")
        xt_ps = sem("xt_ps")
        xt_even = sem("xt_even")
        xt_odd = sem("xt_odd")
        cols_ps = sem("cols_ps")
        cols_ready = sem("cols_ready")
        tmp_ready = sem("tmp_ready")
        hhi_ready = sem("hhi_ready")
        hlo_ready = sem("hlo_ready")
        aq_ready = sem("aq_ready")
        k2_ready = sem("k2_ready")
        av_ready = sem("av_ready")
        rq_raw = sem("rq_raw")
        rk_raw = sem("rk_raw")
        rot_done = sem("rot_done")
        sc_ps = sem("sc_ps")
        sc_done = sem("sc_done")
        nm_ready = sem("nm_ready")
        exp_done = sem("exp_done")
        esink = sem("esink")
        p_norm = sem("p_norm")
        pt_ps = sem("pt_ps")
        pt_done = sem("pt_done")
        pt_used = sem("pt_used")
        att_ready = sem("att_ready")
        v_ready = sem("v_ready")
        g_raw = sem("g_raw")
        g_ready = sem("g_ready")
        st_ps = sem("st_ps")
        st_ready = sem("st_ready")
        o_ps = sem("o_ps")
        o_ssq = sem("o_ssq")
        mix_ready = sem("mix_ready")
        mixt_ps = sem("mixt_ps")
        gt_ps = sem("gt_ps")
        gt_ready = sem("gt_ready")
        x1_part = sem("x1_part")
        x1_ssq = sem("x1_ssq")
        var_ready = sem("var_ready")
        rstd_ready = sem("rstd_ready")
        xn2_dve = sem("xn2_dve")
        xn2_act = sem("xn2_act")
        xn2_ps = sem("xn2_ps")
        glu_lin = sem("glu_lin")
        glu_conv = sem("glu_conv")
        glu_silu = sem("glu_silu")
        glu_done = sem("glu_done")
        x2_part = sem("x2_part")
        x2_ssq = sem("x2_ssq")
        fsc_ps = sem("fsc_ps")
        fin_scale = sem("fin_scale")
        x_scaled = sem("x_scaled")
        fsh_ps = sem("fsh_ps")
        y_ready = sem("y_ready")
        dve_link = sem("dve_link")

        block = ctx.enter_context(nc.Block())

        def raw_slot(step):
            return step // 2 % RING

        def raw_of(step):
            return raw[:, raw_slot(step), step % 2 * GW:(step % 2 + 1) * GW]

        def raw_value(step):
            chunks = range(raw_slot(step), step // 2 + 1, RING)
            return sum(32 if STEP_UP <= 2 * chunk < STEP_DN else 16 for chunk in chunks)

        def rows_before(job):
            return 13 * job if type(job) is int and job < JOB_SH2 else KT * job - 3 * JOB_SH2

        def ada_slot(job, k):
            return k % (2 * RING) if job < JOB_SH2 else k % RING

        def ada_of_slot(slot):
            return ada_raw[:, slot, :] if slot < RING else ada_more[slot - RING]

        def ada_value(job, k):
            return 16 * (2 * job + k // 8 + 1) if job < JOB_SH2 else 16 * (4 * job - 8 + k // RING + 1)

        def x_bank(b):
            return (0, 1, 2, 3, 4, 7, 0, 1)[b]

        def acc_of(job):
            return job % 4 if job < JOB_GT2 else (job - JOB_GT2) % 4

        def mod_parts(job):
            if job < JOB_SH2:
                return [(1, 4 * job, 4, 0), (0, 4 * job, 4, 4)]
            return [(3 if job < JOB_SC2 else 2, 8 * (job % 2), 8, 0)]

        H_ATT, H_RET, H_UP, H_ACT = KT, KT + 4, KT + 8, 2 * KT + 8

        @block.sync
        def _(sp):
            def load(chunk, src, k=2):
                if chunk >= RING:
                    sp.wait_ge(lo_ready, 2 * (chunk - RING + 1))
                sp.dma_start(raw[:, chunk % RING, :].rearrange("p (k n) -> p k n", k=k), src)\
                    .then_inc(raw_in[chunk % RING], 16)

            xin = x[0].rearrange("(t p) n -> p t n", p=P)
            for t in range(TT):
                sp.dma_start(xb[:, t, :], xin[:, t, :]).then_inc(x_in, 16)
            sp.dma_start(ident[:, :], eye[:, :]).then_inc(rows_in, 16)
            sp.dma_start(rows[0:KT, 0, 0:P], g_mix[0].rearrange("(k p) -> k p", p=P)).then_inc(rows_in, 16)
            sp.dma_start(rows[KT:2 * KT, 0, 0:P], g_ffn[0].rearrange("(k p) -> k p", p=P)).then_inc(rows_in, 16)
            for j in range(2):
                sp.dma_start(rows[FT * j:FT * (j + 1), 1, 0:P],
                             w_conv[0, j].rearrange("(k p) -> k p", p=P)).then_inc(rows_in, 16)
            sp.dma_start(rows[0:FT, 2, 0:P], w_conv[0, 2].rearrange("(k p) -> k p", p=P)).then_inc(rows_in, 16)
            sp.dma_start(rows[FT:2 * FT, 2, 0:P], b_conv[0].rearrange("(k p) -> k p", p=P)).then_inc(rows_in, 16)
            sp.dma_start(rows[2 * FT:2 * FT + 9, 2, 0:P],
                         b_in[0, COL_AQ:COL_AV].rearrange("(k p) -> k p", p=P)).then_inc(rows_in, 16)
            sp.dma_start(rows[0:8, 3, :], b_in[0, 0:2 * GW].rearrange("(k p) -> k p", p=RD)).then_inc(rows_in, 16)

            w_in_k = w_in[0].rearrange("(k p) n -> p k n", p=P)
            for i in range(8):
                sp.wait_ge(ada_in[3], 16 * (i + 1))
                load(i, w_in_k[:, 2 * i:2 * i + 2, COL_AQ:COL_AQ + GW])
            sp.wait_ge(ada_in[7], 16 * 2 * JOB_SH2)
            for i in range(2):
                load(8 + i, w_in_k[:, 8 * i:8 * i + 8, COL_AK:COL_AK + AKV_W], 8)
            sp.dma_start(cs, rot[:, :, :]).then_inc(const_in, 16)
            sp.dma_start(mask, masks[:, :]).then_inc(const_in, 16)
            sp.dma_start(gate[:, :], b_in[0:1, COL_RV:COL_AQ].broadcast_to([P, D])).then_inc(const_in, 16)
            sp.dma_start(av_bias[:, :], b_in[0:1, COL_AV:COL_AV + P].broadcast_to([P, P])).then_inc(const_in, 16)
            sp.dma_start(sink_b[:, :], sinks[0:1, :].broadcast_to([P, AH])).then_inc(const_in, 16)
            chunk = STEP_RQ // 2
            for col in (COL_RQ, COL_RK, COL_RV, COL_RG):
                for i in range(8):
                    k = (2 * i + 8) % KT if col == COL_RG else 2 * i
                    load(chunk, w_in_k[:, k:k + 2, col:col + GW])
                    chunk += 1
            w_out_k = w_out[0].rearrange("(k p) n -> p k n", p=P)
            for group in range(2):
                for i in range(8):
                    k = (2 * i + 8) % KT
                    load(chunk, w_out_k[:, k:k + 2, group * GW:(group + 1) * GW])
                    chunk += 1
            w_up_k = w_up[0].rearrange("(k p) (b n) -> p k b n", p=P, b=2)
            with sp.Fori(0, UG) as g:
                with sp.Fori(0, 2) as half:
                    for i in range(4):
                        sp.wait_ge(lo_ready, g * KT + half * LOOP + (STEP_UP - LOOP + 2 * (i + 1)))
                        slot = raw_slot(STEP_UP + 2 * i)
                        for j in range(2):
                            sp.dma_start(raw[:, slot:slot + 1, j * GW:(j + 1) * GW].rearrange("p a (b n) -> p a b n", b=2),
                                         w_up_k[:, bass.ds(half * LOOP + (2 * i + j), 1), :, bass.ds(g * 512, 512)])\
                                .then_inc(raw_in[slot], 16)
            w_dn_k = w_down[0].rearrange("(k p) n -> p k n", p=P)

            def down_turn(turn, k0, group, slots):
                for n, i in enumerate(slots):
                    sp.wait_ge(lo_ready, turn * LOOP + (STEP_DN - LOOP + 2 * (i + 1)))
                    slot = raw_slot(STEP_DN + 2 * i)
                    sp.dma_start(raw[:, slot, :].rearrange("p (k n) -> p k n", k=2),
                                 w_dn_k[:, bass.ds(k0 + 2 * n, 2), group * GW:(group + 1) * GW])\
                        .then_inc(raw_in[slot], 16)

            with sp.Fori(0, 5) as turn:
                down_turn(turn, turn * LOOP, 0, range(4))
            down_turn(5, 40, 0, range(2))
            down_turn(5, 0, 1, range(2, 4))
            with sp.Fori(6, 8) as turn:
                down_turn(turn, turn * LOOP - FT, 1, range(4))
            sp.wait_ge(fsc_ps, 4)
            sp.dma_start(g_fin, g_final.rearrange("(a n) -> a n", a=1).broadcast_to([P, D])).then_inc(gfin_in, 16)
            with sp.Fori(8, 11) as turn:
                down_turn(turn, turn * LOOP - FT, 1, range(4))
            yout = out[0].rearrange("(t p) n -> p t n", p=P)
            for t in range(TT):
                for q in range(2):
                    sp.wait_ge(y_ready, 2 * t + q + 1)
                    sp.dma_start(yout[:, t, q * GW:(q + 1) * GW], xb[:, t, q * GW:(q + 1) * GW]).then_inc(stored, 16)
            sp.wait_ge(stored, 16 * 2 * TT)

        @block.gpsimd
        def _(pool):
            ada_k = w_ada[0].rearrange("(p k) n -> p k n", k=KT)
            ada_2k = w_ada[0, :, 0:2 * D].rearrange("(p k) (s n) -> p k s n", k=KT, s=2)
            fin_k = w_final_ada.rearrange("(p k) n -> p k n", k=KT)

            def column(job):
                if job < JOB_SH2:
                    return job * 512
                part = {JOB_SH2: 3 * D, JOB_SC2: 4 * D, JOB_GT1: 2 * D, JOB_GT2: 5 * D, JOB_FSC: D, JOB_FSH: 0}
                return part[job - job % 2] + (job % 2) * GW

            def start_acc(job):
                a, col = acc[:, acc_of(job), :], column(job)
                before = [j for j in range(job) if acc_of(j) == acc_of(job)]
                if before and before[-1] < JOB_GT1:
                    pool.wait_ge(ada_red, before[-1] + 1)
                elif before:
                    pool.wait_ge(gt_ps, 2 * (before[-1] - JOB_GT1 + 1))
                nc.gpsimd.memset(a, 0.0).then_inc(acc_zero, 1)
                pool.wait_ge(acc_zero, job + 1)
                if job < JOB_SH2:
                    src = b_ada[0:1, 0:2 * D].rearrange("a (s n) -> a s n", s=2)[:, :, col:col + 512]
                    pool.dma_start(a[0:1, :].rearrange("a (s n) -> a s n", s=2), src).then_inc(bias_in, 16)
                elif job < JOB_FSC:
                    pool.dma_start(a[0:1, :], b_ada[0:1, col:col + GW]).then_inc(bias_in, 16)
                else:
                    pool.dma_start(a[0:1, :], b_final_ada[col:col + GW].rearrange("(a n) -> a n", a=1)).then_inc(bias_in, 16)

            def load_unit(job, k, slot):
                col, dst = column(job), ada_of_slot(slot).rearrange("p (a n) -> p a n", a=1)
                if job < JOB_SH2:
                    src = ada_2k[:, bass.ds(k, 1), :, col:col + 512]
                    dst = dst.rearrange("p a (s n) -> p a s n", s=2)
                else:
                    src = (ada_k if job < JOB_FSC else fin_k)[:, bass.ds(k, 1), col:col + GW]
                pool.dma_start(dst, src).then_inc(ada_in[slot], 16)

            def eight_units(job, turn):
                for i in range(2 * RING):
                    if i % RING == 0 and (job or turn):
                        pool.wait_ge(ada_pe, turn * 2 + (RING * job + i // RING - 1))
                    elif job or turn:
                        pool.wait_ge(ada_acc, turn * 7 + (rows_before(job) - 6 + i - 1 - i // RING))
                    load_unit(job, turn * 8 + i, i)

            def four_units(job, turn):
                for i in range(RING):
                    if job == JOB_SH2 and type(turn) is int:
                        pool.wait_ge(*((ada_acc, rows_before(3) + 6 + i) if i else (ada_pe, 4 * RING - 1)))
                    else:
                        pool.wait_ge(ada_acc, turn * RING + (rows_before(job) - RING + i + 1))
                    load_unit(job, turn * RING + i, i)

            start_acc(0)
            nc.gpsimd.memset(ones[:, :], 1.0).then_inc(ones_ready, 1)
            for job in range(JOBS):
                if job in (0, JOB_SH2):
                    (four_units if job else eight_units)(job, 0)
                pool.wait_ge(bias_in, 16 * (job + 1))
                if job < 3:
                    start_acc(job + 1)
                if job == 0:
                    eight_units(0, 1)
                elif job < JOB_SH2:
                    with pool.Fori(0, 2) as turn:
                        eight_units(job, turn)
                else:
                    with pool.Fori(1 if job == JOB_SH2 else 0, KT // RING) as turn:
                        four_units(job, turn)
                if 3 <= job < JOBS - 1:
                    start_acc(job + 1)

        @block.scalar
        def _(act):
            def hi(step):
                act.wait_ge(raw_in[raw_slot(step)], raw_value(step))
                if step >= RING:
                    act.wait_ge(step_done, step - RING + 1)
                nc.scalar.activation(whi[:, step % RING, :], raw_of(step), ACT.Copy).then_inc(hi_ready, 1)

            def hi_turn(i, step0, steps):
                if i % 2 == 0:
                    act.wait_ge(raw_in[raw_slot(step0 + i)], steps * (4 if step0 < STEP_DN else 2) + raw_value(step0 + i))
                act.wait_ge(step_done, steps + (step0 + i - RING + 1))
                nc.scalar.activation(whi[:, i % RING, :], raw_of(step0 + i),
                                     ACT.Copy).then_inc(hi_ready, 1)

            def hi_group(step0, start=0, stop=KT):
                for step in range(step0 + start, step0 + stop):
                    hi(step)

            def modulate(k, kind, src, tmp_base, h_base):
                if k >= 2:
                    act.wait_ge(hlo_ready, h_base + k - 1)
                nc.scalar.activation(mod_tmp[:, k % 2, :], src, ACT.Identity, scale=mod_col[:, kind, k:k + 1],
                                     bias=mod_col[:, kind + 1, k:k + 1]).then_inc(tmp_ready, 1)
                act.wait_ge(tmp_ready, tmp_base + k + 1)
                nc.scalar.activation(hhi[:, k, :], mod_tmp[:, k % 2, :], ACT.Copy).then_inc(hhi_ready, 1)

            def root(n, width):
                act.wait_ge(var_ready, n)
                nc.scalar.activation(rstd[:, 0:width], rstd[:, 0:width], ACT.Sqrt).then_inc(rstd_ready, 1)

            act.dma_start(c_act[:, :], c[0].rearrange("(p k) -> p k", k=KT)).then_inc(cact_in, 16)
            act.wait_ge(cact_in, 16)
            nc.scalar.activation(c_act[:, :], c_act[:, :], ACT.Silu).then_inc(cact_ready, 1)
            act.wait_ge(x_in, 32)
            sink = arena[:, 6400:8448]
            for t in range(TT):
                if t:
                    act.wait_ge(ssq_ready, t)
                nc.scalar.activation(sink, xb[:, t, :], ACT.Square, accum_out=ssq[:, t:t + 1]).then_inc(ssq_ready, 1)
            root(1, TT)
            for b in range(0, 8, 2):
                act.wait_ge(xt_ps, b + 1)
                nc.scalar.activation(xT[:, 2 * b:2 * b + 2, :].rearrange("p k s -> p (k s)"), ps[:, x_bank(b), :],
                                     ACT.Copy).then_inc(xt_even, 1)

            act.wait_ge(xt_odd, 4)
            act.wait_ge(xt_even, 4)
            for job in range(4):
                hi_group(STEP_AQ, 4 * job, 4 * job + 4)
                act.wait_ge(mod_ready, job + 1)
                for k in range(4 * job, 4 * job + 4):
                    modulate(k, 0, xT[:, k, :], 0, 0)
            hi_group(STEP_AK, 0, 3)
            act.wait_ge(step_done, STEP_AK)
            for i in range(8):
                nc.scalar.activation(aqT[:, i, :], ps[:, i // 2, (i % 2) * S:(i % 2 + 1) * S], ACT.Identity,
                                     bias=conv_col2[:, 2 * FT + i:2 * FT + i + 1]).then_inc(aq_ready, 1)
            hi(STEP_AK + 3)
            def retention_in(step_end, dst, which, done):
                act.wait_ge(step_done, step_end)
                for h in range(RH):
                    for e in range(2):
                        nc.scalar.activation(dst[:, h, e, :], ps[:, 4 + h, e * S:(e + 1) * S], ACT.Identity,
                                             bias=rqk_col[:, e, 4 * which + h:4 * which + h + 1]).then_inc(done, 1)

            def key_heads():
                act.wait_ge(step_done, STEP_RQ)
                for head in range(AKV):
                    src = slice(AD * head, AD * (head + 1))
                    for half in range(2):
                        nc.scalar.activation(k2[AD * half:AD * (half + 1), head, :], ps[src, 4, 0:S], ACT.Identity,
                                             bias=conv_col2[src, 2 * FT + 8:2 * FT + 9]).then_inc(k2_ready, 1)

            def exps(batch, part):
                act.wait_ge(nm_ready, 2 * batch + 2)
                for i in range(8 * part, 8 * part + 8):
                    pt = (p0, p1)[i % 2][:, i // 2, :]
                    nc.scalar.activation(pt, pt, ACT.Exp, bias=smx[:, 2, i:i + 1], scale=AD ** -0.5,
                                         accum_out=smx[:, 3, i:i + 1]).then_inc(exp_done, 1)
                if part:
                    nc.scalar.activation(smx[:, 4, :], smx[:, 4, :], ACT.Exp).then_inc(esink, 1)

            def att_tile(n):
                act.wait_ge(pt_used, 2 * n + 2)
                nc.scalar.activation(aqT[:, n, :], ps[:, 2 + n % 2, 0:S], ACT.Copy).then_inc(att_ready, 1)

            def probs_out(batch, h):
                n = 8 * batch + h
                act.wait_ge(pt_ps, n + 1)
                if n >= 2:
                    act.wait_ge(pt_used, n - 1)
                nc.scalar.activation(pT[:, h % 2, :], ps[:, h % 2, 0:320], ACT.Copy).then_inc(pt_done, 1)

            def head_squares(h):
                act.wait_ge(o_ps, h + 1)
                for t in range(TT):
                    i = 2 * h + t
                    if i >= 2:
                        act.wait_ge(o_ssq, i - 1)
                    nc.scalar.activation(mod_tmp[:, t, :], ps[:, 4 + h, t * RD:(t + 1) * RD], ACT.Square,
                                         accum_out=ssq[:, i:i + 1]).then_inc(o_ssq, 1)

            def mix_hi(b):
                act.wait_ge(mixt_ps, b + 1)
                nc.scalar.activation(hhi[:, 2 * b:2 * b + 2, :].rearrange("p k s -> p (k s)"), ps[:, 4 + b, :],
                                     ACT.Copy).then_inc(hhi_ready, 1)

            for p in range(STEP_WO0 - STEP_RQ):
                hi(STEP_RQ + p)
                if p == 2:
                    key_heads()
                elif p in (12, 13):
                    exps(0, p - 12)
                elif p == 18:
                    retention_in(STEP_RK, qT, 0, rq_raw)
                elif p == 34:
                    retention_in(STEP_RV, kT, 1, rk_raw)
                for batch, first in ((0, 17), (1, 39)):
                    if first <= p < first + 8:
                        probs_out(batch, p - first)
                    if first + 2 <= p < first + 10 and (p - first) % 2 == 0:
                        att_tile(4 * batch + (p - first) // 2 - 1)
                if p in (34, 35):
                    exps(1, p - 34)
                if p == 47:
                    act.dma_start(dec, decay[:, :, :]).then_inc(dec_in, 16)
                if p in (60, 62):
                    head_squares((p - 60) // 2)
                if p >= 60:
                    i = p - 60
                    act.wait_ge(att_ready, 2 * i + 2)
                    nc.scalar.activation(hhi[:, 8 + 2 * i:10 + 2 * i, :], aqT[:, 2 * i:2 * i + 2, :], ACT.Copy)\
                        .then_inc(hhi_ready, 1)
            for i in range(KT):
                hi(STEP_WO0 + i)
                if i in (0, 2):
                    head_squares(2 + i // 2)
                elif i == 4:
                    for t in range(TT):
                        act.wait_ge(g_raw, 2 * t + 2)
                        nc.scalar.activation(g_sb[:, t, :], g_sb[:, t, :], ACT.Silu).then_inc(g_ready, 1)
                    root(2, 8)
                elif i in (8, 9):
                    mix_hi(2 * (i - 8))
                    mix_hi(2 * (i - 8) + 1)
                elif i == 10:
                    act.dma_start(xb[:, :, :], x[0].rearrange("(t p) n -> p t n", p=P)).then_inc(x_again, 16)

            def gate_out(n, blocks, bank0):
                for i, b in enumerate(blocks):
                    act.wait_ge(gt_ps, n + i + 1)
                    nc.scalar.activation(gate[:, b * 512:(b + 1) * 512], ps[:, bank0 + i, :], ACT.Copy).then_inc(gt_ready, 1)

            def squares(n, part, done, sink):
                act.wait_ge(part, n + 1)
                t, b = (n % 4) // 2, 2 * (n // 4) + n % 2
                if n:
                    act.wait_ge(done, n)
                nc.scalar.activation(sink, xb[:, t, b * 512:(b + 1) * 512], ACT.Square,
                                     accum_out=ssq[:, 8 + n:9 + n]).then_inc(done, 1)

            sink = arena[:, 4352:4864]
            for i in range(KT):
                hi(STEP_WO1 + i)
                if i == 2:
                    gate_out(0, (0, 1), 6)
                elif i in (6, 8, 10, 12):
                    squares((i - 6) // 2, x1_part, x1_ssq, sink)
                elif i == 15:
                    gate_out(2, (2, 3), 0)
            hi_group(STEP_UP, 0, 3)
            for n in range(4, 8):
                squares(n, x1_part, x1_ssq, sink)
            root(3, TT)
            act.wait_ge(rstd_ready, 3)
            nc.scalar.activation(xn[:, 1, :], xb[:, 1, :], ACT.Copy, scale=rstd[:, 1:2]).then_inc(xn2_act, 1)
            for k in range(KT):
                act.wait_ge(xn2_ps, k - k % 2 + 2)
                modulate(k, 2, ps[:, (k // 2) % 4, (k % 2) * S:(k % 2 + 1) * S], KT, H_UP)
                if k >= 3:
                    hi(STEP_UP + k)

            def glu_linear(slot, tile, src):
                nc.scalar.activation(slot, src, ACT.Identity, scale=conv_col2[:, bass.ds(tile, 1)],
                                     bias=conv_col2[:, bass.ds(tile + FT, 1)]).then_inc(glu_lin, 1)

            def glu_act(slot, tile):
                act.wait_ge(glu_conv, tile * 2 + 2)
                nc.scalar.activation(slot, slot, ACT.Silu).then_inc(glu_silu, 1)

            with act.Fori(0, UG // 2) as pair:
                with act.Fori(0, 2) as q:
                    for half in range(2):
                        for i in range(LOOP):
                            hi_turn(i, STEP_UP + KT + half * LOOP, pair * 2 * KT + q * KT)
                            if i in (3, 4):
                                m = i - 3
                                glu_linear(glu_tmp[:, 2 * half + m, :], pair * 8 + q * 4 + (half * 2 + m),
                                           ps[:, bass.ds(half + 4 - q * 4, 1), m * S:(m + 1) * S])
                        for m in range(2):
                            glu_act(glu_tmp[:, 2 * half + m, :], pair * 8 + q * 4 + (half * 2 + m))

            def down_turn(turn, tile0, tile_of=None):
                for i in range(LOOP):
                    hi_turn(i, STEP_DN, turn * LOOP)
                    tile = tile0 + i if tile_of is None else tile_of(i)
                    nc.scalar.activation(hhi[:, i, :], actT[:, bass.ds(tile * S, S)], ACT.Copy).then_inc(hhi_ready, 1)

            act.wait_ge(glu_done, FT - 4 + 1)
            down_turn(0, 0)
            act.wait_ge(step_done, STEP_DN)
            for m in range(4):
                glu_linear(glu_tmp[:, m, :], 4 * (UG - 1) + m, ps[:, 4 + m // 2, (m % 2) * S:(m % 2 + 1) * S])
            for m in range(4):
                glu_act(glu_tmp[:, m, :], 4 * (UG - 1) + m)
            down_turn(1, LOOP)
            down_turn(2, 2 * LOOP)
            gate_out(4, range(4), 4)
            with act.Fori(3, 5) as turn:
                down_turn(turn, turn * LOOP)
            act.wait_ge(glu_done, FT + 1)
            down_turn(5, 0, lambda i: 40 + i if i < 4 else i - 4)
            down_turn(6, 4)
            sink = glu_tmp[:, 2:4, :].rearrange("p i s -> p (i s)")
            for n in range(4):
                squares(n, x2_part, x2_ssq, sink)
            with act.Fori(7, 11) as turn:
                down_turn(turn, turn * LOOP - FT)
            for n in range(4, 8):
                squares(n, x2_part, x2_ssq, sink)
            root(4, TT)

        @block.vector
        def _(dve):
            links = [0]

            def link(ins):
                links[0] += 1
                ins.then_inc(dve_link, 1)
                dve.wait_ge(dve_link, links[0])

            def lo(step):
                dve.wait_ge(hi_ready, step + 1)
                nc.vector.tensor_tensor(wlo[:, step % RING, :], raw_of(step), whi[:, step % RING, :],
                                        ALU.subtract).then_inc(lo_ready, 1)

            def lo_turn(i, step0, steps):
                dve.wait_ge(hi_ready, steps + (step0 + i + 1))
                nc.vector.tensor_tensor(wlo[:, i % RING, :], raw_of(step0 + i),
                                        whi[:, i % RING, :], ALU.subtract).then_inc(lo_ready, 1)

            def ada_row(a, w, c_col):
                nc.vector.scalar_tensor_tensor(a, w, c_col, a, ALU.mult, ALU.add).then_inc(ada_acc, 1)

            def ada(job, k):
                if k == 0:
                    dve.wait_ge(bias_in, 16 * (job + 1))
                dve.wait_ge(ada_in[ada_slot(job, k)], ada_value(job, k))
                before = rows_before(job) + (k - 1 - k // RING if job < JOB_SH2 else k)
                if before:
                    dve.wait_ge(ada_acc, before)
                ada_row(acc[:, acc_of(job), :], ada_of_slot(ada_slot(job, k)), c_act[:, k:k + 1])

            def pe_row(job):
                dve.wait_ge(ada_pe, RING * (job + 1))
                dve.wait_ge(ada_acc, rows_before(job) + 12)
                a = acc[0:1, acc_of(job), :].rearrange("p (b n) -> p b n", b=2)
                nc.vector.tensor_tensor(a, a, ps[0:1, 5:7, :], ALU.add).then_inc(ada_acc, 1)

            def ada_turn(job, buf, turn, i):
                if i == 0:
                    dve.wait_ge(bias_in, job * 16 + 16)
                dve.wait_ge(ada_in[i], job * 64 + turn * 16 + ada_value(JOB_SH2, 0) - 64 * JOB_SH2)
                dve.wait_ge(ada_acc, rows_before(job) + turn * RING + i)
                ada_row(acc[:, bass.ds(buf, 1), :], ada_raw[:, i:i + 1, :], c_act[:, bass.ds(turn * RING + i, 1)])

            def mod_cols(job, bank, col0):
                dve.wait_ge(ada_red, job + 1)
                parts = mod_parts(job)
                for kind, k, count, col in parts:
                    src = ps[:, bank, col0 + col:col0 + col + count]
                    dst = mod_col[:, kind, k:k + count]
                    if kind % 2:
                        ins = nc.vector.tensor_copy(dst, src)
                    else:
                        ins = nc.vector.scalar_tensor_tensor(dst, src, 1.0, g_col[:, kind // 2, k:k + count],
                                                             ALU.add, ALU.mult)
                    if kind == parts[-1][0]:
                        ins.then_inc(mod_ready, 1)
                    else:
                        link(ins)

            def h_lo(k, base):
                dve.wait_ge(hhi_ready, base + k + 1)
                return nc.vector.tensor_tensor(hlo[:, k, :], mod_tmp[:, k % 2, :], hhi[:, k, :],
                                               ALU.subtract).then_inc(hlo_ready, 1)

            def rstd_of(dst, src, n):
                link(nc.vector.tensor_scalar(dst, src, 1.0 / n, EPS, ALU.mult, ALU.add))
                nc.vector.reciprocal(dst, dst).then_inc(var_ready, 1)

            dve.wait_ge(cact_ready, 1)
            for k in (1, 2, 3):
                ada(0, k)
            dve.wait_ge(ssq_ready, 2)
            rstd_of(rstd[:, 0:2], ssq[:, 0:2], D)
            ada(0, 5)
            dve.wait_ge(rstd_ready, 1)
            for t in range(TT):
                nc.vector.tensor_scalar(xb[:, t, :], xb[:, t, :], rstd[:, t:t + 1], None, ALU.mult).then_inc(xn_ready, 1)
            for b, k in ((1, 6), (3, 7), (5, 9), (7, 10)):
                ada(0, k)
                dve.wait_ge(xt_ps, b + 1)
                nc.vector.tensor_copy(xT[:, 2 * b:2 * b + 2, :].rearrange("p k s -> p (k s)"), ps[:, x_bank(b), :])\
                    .then_inc(xt_odd, 1)
            ada(0, 11)
            ada(0, 13)
            dve.wait_ge(cols_ps, 5)
            for dst, col, count in ((g_col[:, :, :].rearrange("p i k -> p (i k)"), 0, 2 * KT), (conv_col[:, :], 32, 2 * FT),
                                    (conv_col2[:, :], 128, 2 * FT + 9),
                                    (rqk_col[:, :, :].rearrange("p e h -> p (e h)"), 256, 16)):
                nc.vector.tensor_copy(dst, ps[:, 4, col:col + count]).then_inc(cols_ready, 1)
            ada(0, 14)
            ada(0, 15)
            pe_row(0)
            dve.wait_ge(cols_ready, 4)
            for job in range(4):
                nxt = [k for k in range(KT) if k % RING] if job < 3 else []
                for k in nxt[:1]:
                    ada(job + 1, k)
                mod_cols(job, 7, 8 * job)
                h_lo(4 * job, 0)
                for i in range(4):
                    if i < 3:
                        h_lo(4 * job + i + 1, 0)
                    lo(STEP_AQ + 4 * job + i)
                    for k in nxt[1 + 2 * i:3 + 2 * i]:
                        ada(job + 1, k)
                for k in nxt[9:]:
                    ada(job + 1, k)
                if job < 3:
                    pe_row(job + 1)
            for step in range(STEP_AK, STEP_RQ):
                lo(step)
            def values_out():
                dve.wait_ge(const_in, 16 * 5)
                dve.wait_ge(k2_ready, 4)
                for t in range(TT):
                    nc.vector.tensor_tensor(av[:, t, :], ps[:, 4, S + t * P:S + (t + 1) * P], av_bias[:, :],
                                            ALU.add).then_inc(av_ready, 1)

            def rotate(dst, raw_done, n, i):
                ev, od = dst[:, :, 0, :], dst[:, :, 1, :]
                cos, sin = (cs[:, j:j + 1, :].broadcast_to([P, RH, S]) for j in range(2))
                if i == 0:
                    dve.wait_ge(raw_done, 2 * RH)
                    if n:
                        dve.wait_ge(rot_done, n)
                    ins = nc.vector.tensor_tensor(rot_tmp[:, 0], od, sin, ALU.mult)
                elif i == 1:
                    ins = nc.vector.tensor_tensor(rot_tmp[:, 1], ev, sin, ALU.mult)
                elif i == 2:
                    dve.wait_ge(rot_done, n + 2)
                    ins = nc.vector.tensor_tensor(ev, ev, cos, ALU.mult)
                elif i == 3:
                    ins = nc.vector.tensor_tensor(od, od, cos, ALU.mult)
                elif i == 4:
                    dve.wait_ge(rot_done, n + 3)
                    ins = nc.vector.tensor_tensor(ev, ev, rot_tmp[:, 0], ALU.subtract)
                else:
                    dve.wait_ge(rot_done, n + 4)
                    ins = nc.vector.tensor_tensor(od, od, rot_tmp[:, 1], ALU.add)
                ins.then_inc(rot_done, 1)

            def scores_out(batch, i):
                t, n = i % 2, 16 * batch + i
                dve.wait_ge(sc_ps, n + 1)
                pt, mk = ((p0, mask[:, 0:P]), (p1, mask[:, P:P + S]))[t]
                nc.vector.tensor_tensor_reduce(pt[:, i // 2, :], ps[:, i % 4, 0:(1 + t) * P], mk, 1.0, -3e38,
                                               ALU.add, ALU.max, smx[:, 0, i:i + 1]).then_inc(sc_done, 1)

            def maxima(batch):
                dve.wait_ge(sc_done, 16 * batch + 16)
                sk = sink_b[:, 8 * batch:8 * batch + 8].rearrange("p (h a) -> p h a", a=1).broadcast_to([P, 8, 2])

                def pair(r):
                    return smx[:, r, :].rearrange("p (h a) -> p h a", a=2)

                link(nc.vector.scalar_tensor_tensor(pair(1), pair(0), AD ** -0.5, sk, ALU.mult, ALU.max))
                nc.vector.tensor_scalar(smx[:, 2, :], smx[:, 1, :], -1.0, None, ALU.mult).then_inc(nm_ready, 1)
                nc.vector.tensor_tensor(pair(4), sk, pair(1), ALU.subtract).then_inc(nm_ready, 1)

            def normalise(batch, part):
                if part == 0:
                    dve.wait_ge(exp_done, 16 * batch + 16)
                    dve.wait_ge(esink, batch + 1)
                    link(nc.vector.tensor_tensor(smx[:, 5, :], smx[:, 3, :], smx[:, 4, :], ALU.add))
                    link(nc.vector.reciprocal(smx[:, 5, :], smx[:, 5, :]))
                for i in range(8 * part, 8 * part + 8):
                    pt = (p0, p1)[i % 2][:, i // 2, :]
                    nc.vector.tensor_scalar(pt, pt, smx[:, 5, i:i + 1], None, ALU.mult).then_inc(p_norm, 1)

            def att_lo(i):
                dve.wait_ge(hhi_ready, H_ATT + i + 1)
                nc.vector.tensor_tensor(hlo[:, 8 + 2 * i:10 + 2 * i, :], aqT[:, 2 * i:2 * i + 2, :],
                                        hhi[:, 8 + 2 * i:10 + 2 * i, :], ALU.subtract).then_inc(hlo_ready, 1)

            for p in range(STEP_WO0 - STEP_RQ):
                lo(STEP_RQ + p)
                if p == 2:
                    values_out()
                elif 3 <= p < 11:
                    scores_out(0, 2 * (p - 3))
                    scores_out(0, 2 * (p - 3) + 1)
                    if p == 10:
                        maxima(0)
                elif p in (14, 15):
                    normalise(0, p - 14)
                elif 20 <= p < 26:
                    rotate(qT, rq_raw, 0, p - 20)
                elif 27 <= p < 33:
                    for i in range(3 * (p - 27), min(3 * (p - 26), 16)):
                        scores_out(1, i)
                    if p == 32:
                        maxima(1)
                elif p in (36, 37):
                    normalise(1, p - 36)
                elif 40 <= p < 46:
                    rotate(kT, rk_raw, 6, p - 40)
                elif p == 48:
                    dve.wait_ge(ada_red, 6)
                    mod_cols(4, 0, 0)
                    mod_cols(5, 0, 8)
                elif p in (50, 51):
                    dve.wait_ge(rot_done, 12)
                    dve.wait_ge(step_done, STEP_RG)
                    t = p - 50
                    for b in range(2):
                        nc.vector.tensor_tensor(v_sb[:, t, b * 512:(b + 1) * 512], ps[:, 4 + 2 * t + b, :],
                                                gate[:, b * 512:(b + 1) * 512], ALU.add).then_inc(v_ready, 1)
                elif p in (55, 57, 59, 61):
                    h = (p - 55) // 2
                    dve.wait_ge(dec_in, 16)
                    dve.wait_ge(st_ps, h + 1)
                    nc.vector.tensor_tensor(sT[:, h, :], ps[:, 4 + h, 0:384], dec[:, h, :], ALU.mult).then_inc(st_ready, 1)
                if p >= 61:
                    att_lo(p - 61)
                ada(4 + p // KT, p % KT)
            for i in range(KT):
                lo(STEP_WO0 + i)
                if i == 0:
                    att_lo(3)
                elif i == 2:
                    dve.wait_ge(step_done, STEP_WO0)
                    for n in range(4):
                        t, b = n // 2, n % 2
                        nc.vector.tensor_tensor(g_sb[:, t, b * 512:(b + 1) * 512], ps[:, n, :],
                                                gate[:, GW + b * 512:GW + (b + 1) * 512], ALU.add).then_inc(g_raw, 1)
                elif i == 3:
                    dve.wait_ge(o_ssq, 8)
                    rstd_of(rstd[:, 0:8], ssq[:, 0:8], RD)
                elif i in (5, 6):
                    dve.wait_ge(rstd_ready, 2)
                    dve.wait_ge(g_ready, 2)
                    for n in range(4 * (i - 5), 4 * (i - 5) + 4):
                        h, t = n // 2, n % 2
                        g = g_sb[:, t, h * RD:(h + 1) * RD]
                        nc.vector.scalar_tensor_tensor(g, ps[:, 4 + h, t * RD:(t + 1) * RD], rstd[:, n:n + 1], g,
                                                       ALU.mult, ALU.mult).then_inc(mix_ready, 1)
                elif i in (9, 10):
                    for b in (2 * (i - 9), 2 * (i - 9) + 1):
                        dve.wait_ge(hhi_ready, H_RET + b + 1)
                        nc.vector.tensor_tensor(hlo[:, 2 * b:2 * b + 2, :].rearrange("p k s -> p (k s)"), ps[:, 4 + b, :],
                                                hhi[:, 2 * b:2 * b + 2, :].rearrange("p k s -> p (k s)"),
                                                ALU.subtract).then_inc(hlo_ready, 1)
                ada(8, i)

            def residual(n, bank0, part, gt_base, res_tmp):
                t, b = (n % 4) // 2, 2 * (n // 4) + n % 2
                dve.wait_ge(gt_ready, gt_base + b + 1)
                link(nc.vector.tensor_tensor(res_tmp, ps[:, bank0 + n % 4, :], gate[:, b * 512:(b + 1) * 512], ALU.mult))
                xs = xb[:, t, b * 512:(b + 1) * 512]
                nc.vector.tensor_tensor(xs, xs, res_tmp, ALU.add).then_inc(part, 1)
                dve.wait_ge(part, n + 1)

            dve.wait_ge(x_again, 16)
            for i in range(KT):
                lo(STEP_WO1 + i)
                if i in (4, 6, 8, 10):
                    residual((i - 4) // 2, 0, x1_part, 0, res1_tmp)
                for k in (i,) if i < 10 else (2 * i - 10, 2 * i - 9) if i < 13 else ():
                    ada(9, k)
            for step in range(STEP_UP, STEP_UP + 3):
                lo(step)
            dve.wait_ge(step_done, STEP_UP)
            for n in range(4, 8):
                residual(n, 4, x1_part, 0, res1_tmp)

            def total_rstd(done):
                dve.wait_ge(done, 8)
                s = ssq[:, 8:16].rearrange("p (g t b) -> p t g b", g=2, t=2)
                half = ssq[:, 0:4].rearrange("p (t b) -> p t b", t=2)
                link(nc.vector.tensor_tensor(half, s[:, :, 0, :], s[:, :, 1, :], ALU.add))
                link(nc.vector.tensor_tensor(rstd[:, 0:2].rearrange("p (t b) -> p t b", b=1), half[:, :, 0:1], half[:, :, 1:2],
                                             ALU.add))
                rstd_of(rstd[:, 0:2], rstd[:, 0:2], D)

            total_rstd(x1_ssq)
            mod_cols(6, 2, 0)
            mod_cols(7, 3, 0)
            dve.wait_ge(rstd_ready, 3)
            nc.vector.tensor_scalar(xn[:, 0, :], xb[:, 0, :], rstd[:, 0:1], None, ALU.mult).then_inc(xn2_dve, 1)
            for k in range(KT):
                h_lo(k, H_UP)
                if k >= 3:
                    lo(STEP_UP + k)
            dve.wait_ge(hlo_ready, H_ACT)
            nc.vector.memset(ssq[:, 0:1], 0.0).then_inc(glu_done, 1)

            def taps(tile, bank_tiles, slot, bank):
                dve.wait_ge(glu_lin, bank_tiles)
                for d in (1, 2):
                    if d == 2:
                        dve.wait_ge(glu_conv, tile * 2 + 1)
                    nc.vector.scalar_tensor_tensor(slot(d), bank(d), conv_col[:, bass.ds(tile + (2 - d) * FT, 1)], slot(d),
                                                   ALU.mult, ALU.add).then_inc(glu_conv, 1)

            def glu_product(tile, slot, b_branch):
                dve.wait_ge(glu_silu, tile + 1)
                return nc.vector.tensor_tensor(actT[:, bass.ds(tile * S, S)], slot, b_branch, ALU.mult)

            def up_pair(pair, with_ada):
                with dve.Fori(0, 2) as q:
                    with dve.Fori(0, 2) as half:
                        for i in range(LOOP):
                            lo_turn(i, STEP_UP + KT, pair * 2 * KT + q * KT + half * LOOP)
                            if i in (5, 6):
                                m = i - 5
                                taps(pair * 8 + q * 4 + half * 2 + m, pair * 8 + q * 4 + half * 2 + 2,
                                     lambda d: glu_tmp[:, bass.ds(half * 2 + m, 1), d:S],
                                     lambda d: ps[:, bass.ds(half - q * 4 + 4, 1), m * S:(m + 1) * S - d])
                            if with_ada and i % 2:
                                ada_turn(pair + JOB_GT2, pair, q * 2 + half, i // 2)
                        for m in range(2):
                            glu_product(pair * 8 + q * 4 + half * 2 + m, glu_tmp[:, bass.ds(half * 2 + m, 1), :],
                                        ps[:, bass.ds(half - q * 4 + 6, 1), m * S:(m + 1) * S]).then_inc(glu_done, 1)

            with dve.Fori(0, ADA_PAIRS) as pair:
                up_pair(pair, True)
            with dve.Fori(ADA_PAIRS, UG // 2) as pair:
                up_pair(pair, False)

            def down_turn(turn, ada_of=None):
                for i in range(LOOP):
                    dve.wait_ge(hhi_ready, turn * LOOP + (H_ACT + i + 1))
                    tile = down_tile(turn, i)
                    nc.vector.tensor_tensor(hlo[:, i, :], actT[:, bass.ds(tile * S, S)], hhi[:, i, :],
                                            ALU.subtract).then_inc(hlo_ready, 1)
                    lo_turn(i, STEP_DN, turn * LOOP)
                    if ada_of is not None and i % 2:
                        ada_of(i // 2)

            def down_tile(turn, i):
                if type(turn) is int:
                    return (turn * LOOP + i) % FT
                return turn * LOOP + i - down_group[0] * FT

            down_group = [0]
            down_turn(0)
            for m in range(4):
                taps(4 * (UG - 1) + m, 4 * (UG - 1) + m - m % 2 + 2, lambda d: glu_tmp[:, m, d:S], lambda d: ps[:, 4 + m // 2, (m % 2) * S:(m % 2 + 1) * S - d])
            for m in range(4):
                glu_product(4 * (UG - 1) + m, glu_tmp[:, m, :], ps[:, 6 + m // 2, (m % 2) * S:(m % 2 + 1) * S])\
                    .then_inc(glu_done, 1)
            with dve.Fori(1, 3) as turn:
                down_turn(turn)
            with dve.Fori(0, 2) as n:
                down_turn(n + 3, lambda i: ada_turn(JOB_FSH, 0, n, i))
            down_turn(5, lambda i: ada_turn(JOB_FSH, 0, 2, i))
            down_turn(6, lambda i: ada_turn(JOB_FSH, 0, 3, i))
            dve.wait_ge(step_done, STEP_DN + FT)
            for n in range(4):
                residual(n, 0, x2_part, 4, res2_tmp)
            down_group[0] = 1
            with dve.Fori(0, 2) as n:
                down_turn(n + 7, lambda i: ada_turn(JOB_FSH + 1, 1, n, i))
            dve.wait_ge(gfin_in, 16)
            for b in range(4):
                dve.wait_ge(fsc_ps, b + 1)
                g = g_fin[:, b * 512:(b + 1) * 512]
                nc.vector.scalar_tensor_tensor(g, ps[:, b, :], 1.0, g, ALU.add, ALU.mult).then_inc(fin_scale, 1)
            dve.wait_ge(x2_ssq, 4)
            dve.wait_ge(fin_scale, 2)
            for t in range(TT):
                nc.vector.tensor_tensor(xb[:, t, 0:GW], xb[:, t, 0:GW], g_fin[:, 0:GW], ALU.mult).then_inc(x_scaled, 1)
            with dve.Fori(2, 4) as n:
                down_turn(n + 7, lambda i: ada_turn(JOB_FSH + 1, 1, n, i))
            dve.wait_ge(step_done, STEPS)
            for n in range(4, 8):
                residual(n, 4, x2_part, 4, res2_tmp)
            total_rstd(x2_ssq)
            dve.wait_ge(rstd_ready, 4)
            dve.wait_ge(x_scaled, 2)
            dve.wait_ge(fin_scale, 4)
            for t in range(TT):
                for q in range(2):
                    xs = xb[:, t, q * GW:(q + 1) * GW]
                    blocks = xs.rearrange("p (b n) -> p b n", b=2)
                    dve.wait_ge(fsh_ps, 2 * q + 2)
                    if q == 0:
                        nc.vector.scalar_tensor_tensor(blocks, blocks, rstd[:, t:t + 1], ps[:, 0:2, :],
                                                       ALU.mult, ALU.add).then_inc(y_ready, 1)
                    else:
                        link(nc.vector.scalar_tensor_tensor(xs, xs, rstd[:, t:t + 1], g_fin[:, GW:D], ALU.mult, ALU.mult))
                        nc.vector.tensor_tensor(blocks, blocks, ps[:, 2:4, :], ALU.add).then_inc(y_ready, 1)

        @block.tensor
        def _(pe):
            def passes(out_ap, lhs, rhs, start, skip):
                nc.tensor.matmul(out_ap, lhs[0], rhs[0], start=start, stop=False, skip_group_check=skip)
                nc.tensor.matmul(out_ap, lhs[0], rhs[1], start=False, stop=False, skip_group_check=skip)
                return nc.tensor.matmul(out_ap, lhs[1], rhs[0], start=False, stop=True, skip_group_check=skip)

            def columns(slot, k, start, bank_of, cols=None, order=range(4), free=None):
                for b in order:
                    if free and free[b]:
                        pe.wait_ge(*free[b])
                    for m in (2 * b, 2 * b + 1):
                        c0 = cols(m) if cols else slice(m * P, (m + 1) * P)
                        last = passes(bank_of(b)[:, (m % 2) * S:(m % 2 + 1) * S],
                                      (whi[:, slot, c0], wlo[:, slot, c0]), (hhi[:, k, :], hlo[:, k, :]),
                                      start and m % 2 == 0, True)
                last.then_inc(step_done, 1)

            def tokens(slot, k, start, bank0, order=range(4), free=None):
                for n in order:
                    if free and free[n]:
                        pe.wait_ge(*free[n])
                    t, b = n // 2, n % 2
                    ts, cb = slice(t * P, (t + 1) * P), slice(b * 512, (b + 1) * 512)
                    last = passes(ps[:, bank0 + n, :], (hhi[:, k, ts], hlo[:, k, ts]),
                                  (whi[:, slot, cb], wlo[:, slot, cb]), start, True)
                last.then_inc(step_done, 1)

            def sum_columns(job, bank, col0):
                pe.wait_ge(ada_acc, rows_before(job + 1))
                for i in range(8):
                    last = nc.tensor.matmul(ps[:, bank, col0 + i:col0 + i + 1], acc[:, acc_of(job), i * P:(i + 1) * P],
                                            ones[:, 0:1], start=True, stop=True)
                last.then_inc(ada_red, 1)

            def sum_rows(job, bank0, done):
                pe.wait_ge(ada_acc, rows_before(job + 1))
                for b in range(2):
                    nc.tensor.matmul(ps[:, bank0 + b, :], ones[:, :], acc[:, acc_of(job), b * 512:(b + 1) * 512],
                                     start=True, stop=True).then_inc(done, 1)

            def ada_unit(job, turn):
                k = turn * RING
                slot = ada_slot(job, k)
                pe.wait_ge(ada_in[slot], ada_value(job, k))
                for b in range(2):
                    last = nc.tensor.matmul(ps[0:1, 5 + b, :], c_act[:, k:k + 1], ada_of_slot(slot)[:, b * 512:(b + 1) * 512],
                                            start=turn == 0, stop=True, skip_group_check=True)
                last.then_inc(ada_pe, 1)

            pe.wait_ge(cact_ready, 1)
            ada_unit(0, 0)
            ada_unit(0, 1)
            pe.wait_ge(rows_in, 16 * 9)
            pe.wait_ge(xn_ready, TT)
            for k in range(KT):
                if k == 12:
                    pe.wait_ge(xt_even, 1)
                if k == 14:
                    pe.wait_ge(xt_odd, 1)
                for t in range(TT):
                    c0 = (k % 2) * S + t * P
                    last = nc.tensor.transpose(ps[:, x_bank(k // 2), c0:c0 + P], xb[:, t, k * P:(k + 1) * P], ident[:, :])
                if k % 2:
                    last.then_inc(xt_ps, 1)
            pe.wait_ge(xt_even, 4)
            pe.wait_ge(xt_odd, 4)
            for col, n, src in ((0, 2 * KT, rows[0:2 * KT, 0, 0:P]), (32, 2 * FT, rows[0:2 * FT, 1, 0:P]),
                                (128, 2 * FT + 9, rows[0:2 * FT + 9, 2, 0:P]), (256, 8, rows[0:8, 3, 0:RD:2]),
                                (264, 8, rows[0:8, 3, 1:RD:2])):
                nc.tensor.transpose(ps[:, 4, col:col + n], src, ident[0:n, 0:n]).then_inc(cols_ps, 1)
            ada_unit(0, 2)
            ada_unit(0, 3)
            pe.wait_ge(ones_ready, 1)
            for job in range(4):
                if job:
                    pe.wait_ge(mod_ready, job)
                sum_columns(job, 7, 8 * job)
                if job < 3:
                    ada_unit(job + 1, 0)
                for i in range(4):
                    k = 4 * job + i
                    pe.wait_ge(hlo_ready, k + 1)
                    pe.wait_ge(lo_ready, STEP_AQ + k + 1)
                    columns(k % RING, k, k == 0, lambda b: ps[:, b, :])
                    if job < 3 and i < 3:
                        ada_unit(job + 1, i + 1)
            pe.wait_ge(cols_ready, 4)
            for step in range(STEP_AK, STEP_RQ):
                pe.wait_ge(lo_ready, step + 1)
                slot = step % RING
                for i in range(AK_TILES):
                    k, c0 = AK_TILES * (step - STEP_AK) + i, i * AKV_W
                    ak, av_cols = slice(c0, c0 + P), slice(c0 + P, c0 + 2 * P)
                    passes(ps[:, 4, 0:S], (whi[:, slot, ak], wlo[:, slot, ak]), (hhi[:, k, :], hlo[:, k, :]), k == 0, True)
                    for t in range(TT):
                        ts = slice(t * P, (t + 1) * P)
                        last = passes(ps[:, 4, S + t * P:S + (t + 1) * P], (hhi[:, k, ts], hlo[:, k, ts]),
                                      (whi[:, slot, av_cols], wlo[:, slot, av_cols]), False, True)
                last.then_inc(step_done, 1)

            def split_dims(m):
                return slice((m // 2) * RD + m % 2, (m // 2 + 1) * RD, 2)

            def att_scores(batch, i):
                n, h, t = 16 * batch + i, i // 2, i % 2
                if i >= 4:
                    pe.wait_ge(sc_done, n - 3)
                half = slice(AD * (h % 2), AD * (h % 2 + 1))
                nc.tensor.matmul(ps[:, i % 4, 0:(1 + t) * P], aqT[half, 4 * batch + h // 2, t * P:(t + 1) * P],
                                 k2[half, batch, 0:(1 + t) * P], start=True, stop=True).then_inc(sc_ps, 1)

            def att_values(batch, h):
                n = 8 * batch + h
                pe.wait_ge(pt_done, n + 1)
                if h % 2 == 0 and h >= 4:
                    pe.wait_ge(att_ready, n // 2 - 1)
                o = ps[AD * (h % 2):AD * (h % 2 + 1), 2 + (h // 2) % 2, :]
                v0, v1 = (av[:, t, AD * batch:AD * (batch + 1)] for t in range(TT))
                pr = pT[:, h % 2, :]
                nc.tensor.matmul(o[:, 0:P], v0, pr[:, 0:P], start=True, stop=True, skip_group_check=True)
                nc.tensor.matmul(o[:, P:2 * P], v1, pr[:, 192:320], start=False, stop=False, skip_group_check=True)
                last = nc.tensor.matmul(o[:, P:P + 64], v0, pr[:, P:192], start=False, stop=True, skip_group_check=True)
                last.then_inc(pt_used, 1)

            def att_head(batch, h):
                n = 8 * batch + h
                if h < 8:
                    pe.wait_ge(p_norm, 16 * batch + 2 * h + 2)
                    if h >= 2:
                        pe.wait_ge(pt_done, n - 1)
                    bank = ps[:, h % 2, :]
                    nc.tensor.transpose(bank[:, 0:P], p0[:, h, :], ident[:, :])
                    nc.tensor.transpose(bank[:, P:192], p1[0:64, h, 0:P], ident[0:64, 0:64])
                    nc.tensor.transpose(bank[:, 192:320], p1[:, h, P:2 * P], ident[:, :]).then_inc(pt_ps, 1)
                if h:
                    att_values(batch, h - 1)

            def ret_scores(h):
                for m, cols in ((0, slice(0, S)), (1, slice(P, S))):
                    o = ps[:, 4 + h, m * S:m * S + cols.stop - cols.start]
                    for e in range(2):
                        last = nc.tensor.matmul(o, kT[:, h, e, m * P:(m + 1) * P], qT[:, h, e, cols],
                                                start=m == 0 and e == 0, stop=e == 1, skip_group_check=True)
                last.then_inc(st_ps, 1)

            def ret_values(h):
                pe.wait_ge(st_ready, h + 1)
                v0, v1 = (v_sb[:, t, h * RD:(h + 1) * RD] for t in range(TT))
                o = ps[:, 4 + h, :]
                nc.tensor.matmul(o[:, 0:RD], sT[:, h, 0:P], v0, start=True, stop=True, skip_group_check=True)
                nc.tensor.matmul(o[:, RD:2 * RD], sT[:, h, P:2 * P], v0, start=False, stop=False, skip_group_check=True)
                nc.tensor.matmul(o[:, RD:2 * RD], sT[:, h, S:S + P], v1, start=False, stop=True, skip_group_check=True)\
                    .then_inc(o_ps, 1)

            freed = {STEP_RQ: [(av_ready, 2), None, None, None],
                     STEP_RK: [(rq_raw, 2 * b + 2) for b in range(4)],
                     STEP_RV: [(rk_raw, 2 * b + 2) for b in range(4)],
                     STEP_RG: [(mod_ready, 6), (pt_done, 16), (att_ready, 7), (att_ready, 8)]}
            pe.wait_ge(mod_ready, 4)
            for p in range(STEP_WO0 - STEP_RQ):
                step, k = STEP_RQ + p, p % KT
                order = (1, 2, 3, 0) if step in (STEP_RQ, STEP_RG) else range(4)
                pe.wait_ge(lo_ready, step + 1)
                if step < STEP_RV:
                    columns(k % RING, k, k == 0, lambda b: ps[:, 4 + b, :], split_dims, order, freed.get(step))
                elif step < STEP_RG:
                    tokens(k % RING, k, k == 0, 4, order, freed.get(step))
                else:
                    tokens(k % RING, (8 + k) % KT, k == 0, 0, order, freed.get(step))
                if p < 8:
                    if p == 0:
                        pe.wait_ge(aq_ready, 8)
                        pe.wait_ge(k2_ready, 4)
                    att_scores(0, 2 * p)
                    att_scores(0, 2 * p + 1)
                elif 14 <= p < 23:
                    att_head(0, p - 14)
                elif 24 <= p < 30:
                    if p == 24:
                        pe.wait_ge(att_ready, 4)
                    for i in range(3 * (p - 24), min(3 * (p - 23), 16)):
                        att_scores(1, i)
                elif 36 <= p < 45:
                    att_head(1, p - 36)
                elif p == 46:
                    pe.wait_ge(pt_done, 15)
                    sum_columns(4, 0, 0)
                    sum_columns(5, 0, 8)
                elif p in (52, 54, 56, 58):
                    if p == 52:
                        pe.wait_ge(rot_done, 12)
                        pe.wait_ge(v_ready, 4)
                    ret_scores((p - 52) // 2)
                elif p in (57, 59, 61, 63):
                    ret_values((p - 57) // 2)
            for i in range(KT):
                if i % 2 == 0:
                    pe.wait_ge(hlo_ready, H_ATT + i // 2 + 1)
                pe.wait_ge(lo_ready, STEP_WO0 + i + 1)
                tokens(i % RING, (8 + i) % KT, i == 0, 0, free=None if i else [(g_raw, b + 1) for b in range(4)])
                if i in (5, 6):
                    for b in (2 * (i - 5), 2 * (i - 5) + 1):
                        pe.wait_ge(mix_ready, 2 * b + 2)
                        for j in range(4):
                            k, t = 2 * b + j // 2, j % 2
                            last = nc.tensor.transpose(ps[:, 4 + b, j * P:(j + 1) * P], g_sb[:, t, k * P:(k + 1) * P],
                                                       ident[:, :])
                        last.then_inc(mixt_ps, 1)
            sum_rows(JOB_GT1, 6, gt_ps)
            for i in range(KT):
                pe.wait_ge(lo_ready, STEP_WO1 + i + 1)
                tokens(i % RING, (8 + i) % KT, i == 0, 4, free=None if i else [None, None, (gt_ready, 1), (gt_ready, 2)])
                if i == 13:
                    pe.wait_ge(x1_part, 4)
                    sum_rows(JOB_GT1 + 1, 0, gt_ps)
            for job in (6, 7):
                sum_columns(job, job - 4, 0)
            def x_tiles(k0):
                if k0 >= 8:
                    pe.wait_ge(tmp_ready, KT + k0 - 6)
                for k in (k0, k0 + 1):
                    for t in range(TT):
                        c0 = (k % 2) * S + t * P
                        last = nc.tensor.transpose(ps[:, (k // 2) % 4, c0:c0 + P], xn[:, t, k * P:(k + 1) * P], ident[:, :])
                    last.then_inc(xn2_ps, 1)

            pe.wait_ge(gt_ready, 4)
            pe.wait_ge(mod_ready, 8)
            pe.wait_ge(xn2_dve, 1)
            pe.wait_ge(xn2_act, 1)
            x_tiles(0)
            x_tiles(2)
            for k in range(KT):
                pe.wait_ge(hlo_ready, H_UP + k + 1)
                pe.wait_ge(lo_ready, STEP_UP + k + 1)
                columns(k % RING, k, k == 0, lambda b: ps[:, 4 + b, :], free=None if k else [(x1_part, 5 + b) for b in range(4)])
                if k < 6:
                    x_tiles(2 * k + 4)
            with pe.Fori(0, UG // 2) as pair:
                with pe.Fori(0, 2) as q:
                    pe.wait_ge(glu_done, pair * 8 + q * 4 + 1)
                    for k in range(KT):
                        pe.wait_ge(lo_ready, pair * 2 * KT + q * KT + (STEP_UP + KT + k + 1))
                        columns(k % RING, k, k == 0, lambda b: ps[:, bass.ds(q * 4 + b, 1), :].rearrange("p a n -> p (a n)"))
            def down_turn(turn, start, bank_of):
                for i in range(LOOP):
                    pe.wait_ge(hlo_ready, turn * LOOP + (H_ACT + i + 1))
                    pe.wait_ge(lo_ready, turn * LOOP + (STEP_DN + i + 1))
                    tokens(i % RING, i, start == i, bank_of(i))

            pe.wait_ge(glu_done, FT - 4 + 1)
            down_turn(0, 0, lambda i: 0)
            down_turn(1, None, lambda i: 0)
            pe.wait_ge(glu_done, FT + 1)
            sum_rows(JOB_GT2, 4, gt_ps)
            sum_rows(JOB_GT2 + 1, 6, gt_ps)
            with pe.Fori(2, 5) as turn:
                down_turn(turn, None, lambda i: 0)
            pe.wait_ge(gt_ready, 8)
            down_turn(5, 4, lambda i: 0 if i < 4 else 4)
            down_turn(6, None, lambda i: 4)
            pe.wait_ge(x2_part, 4)
            for half in range(2):
                sum_rows(JOB_FSC + half, 2 * half, fsc_ps)
            with pe.Fori(7, 10) as turn:
                down_turn(turn, None, lambda i: 4)
            pe.wait_ge(fin_scale, 4)
            sum_rows(JOB_FSH, 0, fsh_ps)
            down_turn(10, None, lambda i: 4)
            sum_rows(JOB_FSH + 1, 2, fsh_ps)


_INS = ["x", "c", "w_ada", "b_ada", "g_mix", "w_in", "b_in", "sinks", "w_out", "g_ffn", "w_up", "w_conv", "b_conv",
        "w_down", "w_final_ada", "b_final_ada", "g_final"]


def _constants():
    f32 = np.float32
    freq = f32(10000.0) ** -np.linspace(0.0, 1.0, RD // 2, dtype=f32)
    angle = (freq[:, None] * np.arange(S, dtype=f32)[None, :]).astype(np.float64)
    rot = np.stack([np.cos(angle), np.sin(angle)], axis=1).astype(f32)
    pos = np.arange(S)
    gap = np.abs(pos[None, :] - pos[:, None])
    seen = (pos[None, :] // CHUNK) >= (pos[:, None] // CHUNK)
    decay = np.zeros((P, RH, 384))
    for h in range(RH):
        d = np.where(seen, (1.0 - 2.0 ** (-5.0 - h)) ** gap, 0.0) * RD ** -0.5
        decay[:, h, 0:S] = d[0:P]
        decay[:, h, S:] = d[P:, P:]
    behind = (pos[:, None] // CHUNK) - (pos[None, :] // CHUNK)
    hidden = np.where((behind >= 0) & (behind < 2), 0.0, -1e30)
    masks = np.concatenate([hidden[0:P, 0:P], hidden[P:, :]], axis=1)
    return {"rot": rot, "decay": decay.astype(f32), "masks": masks.astype(f32), "eye": np.eye(P, dtype=f32)}


def kernel(**inputs):
    import concourse.bacc as bacc
    from concourse.bass_utils import run_bass_kernel_spmd

    nc = bacc.Bacc("TRN2", target_bir_lowering=False, num_devices=1)
    arrays, args = {}, []
    given = {name: np.ascontiguousarray(inputs[name]) for name in _INS} | _constants()
    for name, a in given.items():
        arrays[f"in_{name}"] = a
        args.append(nc.dram_tensor(f"in_{name}", a.shape, mybir.dt.from_np(a.dtype), kind="ExternalInput").ap())
    args.append(nc.dram_tensor("out_y", (1, S, D), F32, kind="ExternalOutput").ap())
    build(nc, *args)
    r = run_bass_kernel_spmd(nc, [arrays], core_ids=[0])
    return r.results[0]["out_y"]
```

```python
from contextlib import ExitStack

import numpy as np

import concourse.bass as bass
from concourse import mybir

F32 = mybir.dt.float32
F32R = mybir.dt.float32r
ALU = mybir.AluOpType
ACT = mybir.ActivationFunctionType

P = 128
D, S, FF = 2048, 256, 5632
CHUNK = 64
KT = D // P
TT = S // P
RH, RD = 4, 256
AH, AKV, AD = 16, 2, 64
FT = FF // P
EPS = 1e-6
GW = 1024
RING = 4

COL_RQ, COL_RK, COL_RV, COL_RG, COL_AQ, COL_AK = (i * GW for i in range(6))
AKV_W = 2 * AKV * AD
AK_TILES = GW // AKV_W

AQ_STEPS = [k if k < 12 else k + 3 for k in range(KT)]
AK_STEPS = [12, 13, 14, 19]
MIXED_CHUNKS = (7, 9)
STEP_RQ, STEP_RK, STEP_RV, STEP_RG, STEP_WO0, STEP_WO1, STEP_UP = (len(AQ_STEPS + AK_STEPS) + KT * i for i in range(7))
UG = FF // (GW // 2)
STEP_DN = STEP_UP + UG * KT
STEPS = STEP_DN + 2 * FT
LOOP = 8
ADA_PAIRS = 4

JOB_SH2, JOB_SC2, JOB_GT1, JOB_GT2, JOB_FSC, JOB_FSH = 4, 6, 8, 10, 12, 14
JOBS = 16


def build(nc, x, c, w_ada, b_ada, g_mix, w_in, b_in, sinks, w_out, g_ffn, w_up, w_conv, b_conv,
          w_down, w_final_ada, b_final_ada, g_final, rot, decay, masks, eye, out):
    ctx = ExitStack()
    with ctx:
        def sb(name, shape, dt=F32):
            return ctx.enter_context(nc.sbuf_tensor(name, shape, dt))

        def sem(name):
            return ctx.enter_context(nc.semaphore(name))

        raw = sb("raw", [P, RING, 2 * GW])
        whi = sb("whi", [P, RING, GW], F32R)
        wlo = sb("wlo", [P, RING, GW], F32R)
        hhi = sb("hhi", [P, KT, S], F32R)
        hlo = sb("hlo", [P, KT, S], F32R)
        ada_raw = sb("ada_raw", [P, RING, GW])
        acc = sb("acc", [P, 4, GW])
        xb = sb("xb", [P, TT, D])
        gate = sb("gate", [P, D])
        arena = sb("arena", [P, 12288])
        ident = sb("ident", [P, P])
        ones = sb("ones", [P, P])
        c_act = sb("c_act", [P, KT])
        g_col = sb("g_col", [P, 2, KT])
        conv_col = sb("conv_col", [P, 2 * FT])
        conv_col2 = sb("conv_col2", [P, 2 * FT + 10])
        rqk_col = sb("rqk_col", [P, 2, 8])
        mod_col = sb("mod_col", [P, 4, KT])
        sink_b = sb("sink_b", [P, AH])
        ssq = sb("ssq", [P, 16])
        rstd = sb("rstd", [P, 8])
        smx = sb("smx", [P, 6, 16])
        aqT = arena[:, 0:2048].rearrange("p (i s) -> p i s", s=S)
        k2 = arena[:, 2048:2560].rearrange("p (i s) -> p i s", s=S)
        av = arena[:, 2560:2816].rearrange("p (t d) -> p t d", d=P)
        cs = arena[:, 2816:3328].rearrange("p (i s) -> p i s", s=S)
        p0 = arena[:, 3328:4352].rearrange("p (h k) -> p h k", k=P)
        p1 = arena[:, 4352:6400].rearrange("p (h k) -> p h k", k=S)
        dec = arena[:, 3328:4864].rearrange("p (h k) -> p h k", k=384)
        sT = arena[:, 4864:6400].rearrange("p (h k) -> p h k", k=384)
        rows = arena[:, 3328:3328 + 4 * 256].rearrange("p (i n) -> p i n", n=256)
        qT = arena[:, 6400:8448].rearrange("p (h e s) -> p h e s", e=2, s=S)
        kT = arena[:, 8448:10496].rearrange("p (h e s) -> p h e s", e=2, s=S)
        ada_more = [arena[:, c:c + GW] for c in (0, GW, 4352, 4352 + GW)]
        xT = arena[:, 6400:10496].rearrange("p (k s) -> p k s", s=S)
        mask = arena[:, 10496:10880]
        pT = arena[:, 10880:11520].rearrange("p (i k) -> p i k", k=320)
        avT = arena[:, 11520:11520 + S]
        mod_tmp = arena[:, 11520:12032].rearrange("p (i s) -> p i s", s=S)
        rot_tmp = xb[:, 0, :].rearrange("p (i h s) -> p i h s", i=2, s=S)
        v_sb = xb[:, 0, :].rearrange("p (t e) -> p t e", t=TT)
        g_sb = gate[:, :].rearrange("p (t e) -> p t e", t=TT)
        xn1 = raw[:, 2:4, :]
        xn = arena[:, 0:4096].rearrange("p (t n) -> p t n", t=TT)
        actT = arena[:, 0:FT * S]
        glu_tmp = arena[:, FT * S:FT * S + 4 * S].rearrange("p (i s) -> p i s", s=S)
        g_fin = acc[:, 2:4, :].rearrange("p a n -> p (a n)")
        res1_tmp, res2_tmp = (a.rearrange("p i s -> p (i s)") for a in (mod_tmp, glu_tmp[:, 0:2, :]))

        ps = ctx.enter_context(nc.psum_tensor("ps", [P, 8, 512], F32))

        x_in = sem("x_in")
        rows_in = sem("rows_in")
        const_in = sem("const_in")
        late_in = sem("late_in")
        cact_in = sem("cact_in")
        x_again = sem("x_again")
        dec_in = sem("dec_in")
        gfin_in = sem("gfin_in")
        stored = sem("stored")
        raw_in = [sem(f"raw_in{i}") for i in range(RING)]
        ada_in = [sem(f"ada_in{i}") for i in range(2 * RING)]
        bias_in = sem("bias_in")
        hi_ready = sem("hi_ready")
        lo_ready = sem("lo_ready")
        step_done = sem("step_done")
        acc_zero = sem("acc_zero")
        ada_acc = sem("ada_acc")
        ada_pe = sem("ada_pe")
        ada_red = sem("ada_red")
        mod_ready = sem("mod_ready")
        cact_ready = sem("cact_ready")
        ones_ready = sem("ones_ready")
        ssq_ready = sem("ssq_ready")
        xn_ready = sem("xn_ready")
        xt_ps = sem("xt_ps")
        xt_even = sem("xt_even")
        xt_odd = sem("xt_odd")
        cols_ps = sem("cols_ps")
        cols_ready = sem("cols_ready")
        tmp_ready = sem("tmp_ready")
        hhi_ready = sem("hhi_ready")
        hlo_ready = sem("hlo_ready")
        aq_ready = sem("aq_ready")
        k2_ready = sem("k2_ready")
        vt_ps = sem("vt_ps")
        av_ready = sem("av_ready")
        rq_raw = sem("rq_raw")
        rk_raw = sem("rk_raw")
        rot_done = sem("rot_done")
        sc_ps = sem("sc_ps")
        sc_done = sem("sc_done")
        nm_ready = sem("nm_ready")
        exp_done = sem("exp_done")
        esink = sem("esink")
        p_norm = sem("p_norm")
        pt_ps = sem("pt_ps")
        pt_done = sem("pt_done")
        pt_used = sem("pt_used")
        att_ready = sem("att_ready")
        v_ready = sem("v_ready")
        g_raw = sem("g_raw")
        g_ready = sem("g_ready")
        st_ps = sem("st_ps")
        st_ready = sem("st_ready")
        o_ps = sem("o_ps")
        o_ssq = sem("o_ssq")
        mix_ready = sem("mix_ready")
        mixt_ps = sem("mixt_ps")
        out_ps = sem("out_ps")
        gt_ps = sem("gt_ps")
        gt_ready = sem("gt_ready")
        x1_part = sem("x1_part")
        x1_ssq = sem("x1_ssq")
        var_ready = sem("var_ready")
        rstd_ready = sem("rstd_ready")
        xn2_dve = sem("xn2_dve")
        xn2_act = sem("xn2_act")
        xn2_ps = sem("xn2_ps")
        glu_lin = sem("glu_lin")
        glu_conv = sem("glu_conv")
        glu_silu = sem("glu_silu")
        glu_done = sem("glu_done")
        x2_part = sem("x2_part")
        x2_ssq = sem("x2_ssq")
        fsc_ps = sem("fsc_ps")
        fin_scale = sem("fin_scale")
        x_scaled = sem("x_scaled")
        fsh_ps = sem("fsh_ps")
        y_ready = sem("y_ready")
        dve_link = sem("dve_link")

        block = ctx.enter_context(nc.Block())

        def raw_slot(step):
            return step // 2 % RING

        def raw_of(step):
            return raw[:, raw_slot(step), step % 2 * GW:(step % 2 + 1) * GW]

        def raw_value(step):
            chunks = range(raw_slot(step), step // 2 + 1, RING)
            return sum(32 if STEP_UP <= 2 * chunk < STEP_DN or chunk in MIXED_CHUNKS else 16 for chunk in chunks)

        def rows_before(job):
            return 13 * job if type(job) is int and job < JOB_SH2 else KT * job - 3 * JOB_SH2

        def ada_slot(job, k):
            return k % (2 * RING) if job < JOB_SH2 else k % RING

        def ada_of_slot(slot):
            return ada_raw[:, slot, :] if slot < RING else ada_more[slot - RING]

        def ada_value(job, k):
            return 16 * (2 * job + k // 8 + 1) if job < JOB_SH2 else 16 * (4 * job - 8 + k // RING + 1)

        def x_bank(b):
            return (0, 1, 2, 3, 4, 7, 0, 1)[b]

        def acc_of(job):
            return job % 4 if job < JOB_GT2 else (job - JOB_GT2) % 4

        def mod_parts(job):
            if job < JOB_SH2:
                return [(1, 4 * job, 4, 0), (0, 4 * job, 4, 4)]
            return [(3 if job < JOB_SC2 else 2, 8 * (job % 2), 8, 0)]

        H_ATT, H_RET, H_UP, H_ACT = KT, KT + 4, KT + 8, 2 * KT + 8

        @block.sync
        def _(sp):
            def load(chunk, src, k=2):
                if chunk >= RING:
                    sp.wait_ge(lo_ready, 2 * (chunk - RING + 1))
                sp.dma_start(raw[:, chunk % RING, :].rearrange("p (k n) -> p k n", k=k), src)\
                    .then_inc(raw_in[chunk % RING], 16)

            xin = x[0].rearrange("(t p) n -> p t n", p=P)
            for t in range(TT):
                sp.dma_start(xb[:, t, :], xin[:, t, :]).then_inc(x_in, 16)
            sp.dma_start(ident[:, :], eye[:, :]).then_inc(rows_in, 16)
            sp.dma_start(rows[0:KT, 0, 0:P], g_mix[0].rearrange("(k p) -> k p", p=P)).then_inc(rows_in, 16)
            sp.dma_start(rows[KT:2 * KT, 0, 0:P], g_ffn[0].rearrange("(k p) -> k p", p=P)).then_inc(rows_in, 16)
            for j in range(2):
                sp.dma_start(rows[FT * j:FT * (j + 1), 1, 0:P],
                             w_conv[0, j].rearrange("(k p) -> k p", p=P)).then_inc(rows_in, 16)
            sp.dma_start(rows[0:FT, 2, 0:P], w_conv[0, 2].rearrange("(k p) -> k p", p=P)).then_inc(rows_in, 16)
            sp.dma_start(rows[FT:2 * FT, 2, 0:P], b_conv[0].rearrange("(k p) -> k p", p=P)).then_inc(rows_in, 16)
            sp.dma_start(rows[2 * FT:2 * FT + 10, 2, 0:P],
                         b_in[0, COL_AQ:COL_AK + AKV_W].rearrange("(k p) -> k p", p=P)).then_inc(rows_in, 16)
            sp.dma_start(rows[0:8, 3, :], b_in[0, 0:2 * GW].rearrange("(k p) -> k p", p=RD)).then_inc(rows_in, 16)

            w_in_k = w_in[0].rearrange("(k p) n -> p k n", p=P)
            def load_step(step, src, k):
                if step % 2 == 0:
                    sp.wait_ge(lo_ready, step - 2 * RING + 2)
                sp.dma_start(raw_of(step).rearrange("p (k n) -> p k n", k=k), src).then_inc(raw_in[raw_slot(step)], 16)

            for i in range(6):
                sp.wait_ge(ada_in[3], 16 * (i + 1))
                if i == 2:
                    sp.wait_ge(xt_ps, 8)
                load(i, w_in_k[:, 2 * i:2 * i + 2, COL_AQ:COL_AQ + GW])
            sp.wait_ge(ada_in[7], 16 * 2 * JOB_SH2)
            w_ak, w_aq = w_in_k[:, :, COL_AK:COL_AK + AKV_W], w_in_k[:, :, COL_AQ:COL_AQ + GW]
            load(6, w_ak[:, 0:8, :], 8)
            load_step(14, w_ak[:, 8:12, :], AK_TILES)
            load_step(15, w_aq[:, 12:13, :], 1)
            load(8, w_aq[:, 13:15, :])
            load_step(18, w_aq[:, 15:16, :], 1)
            load_step(19, w_ak[:, 12:16, :], AK_TILES)
            sp.dma_start(mask, masks[:, :]).then_inc(const_in, 16)
            sp.dma_start(sink_b[:, :], sinks[0:1, :].broadcast_to([P, AH])).then_inc(const_in, 16)
            chunk = STEP_RQ // 2
            for col in (COL_RQ, COL_RK, COL_RV, COL_RG):
                if col == COL_RK:
                    sp.dma_start(cs, rot[:, :, :]).then_inc(late_in, 16)
                    sp.dma_start(gate[:, :], b_in[0:1, COL_RV:COL_AQ].broadcast_to([P, D])).then_inc(late_in, 16)
                for i in range(8):
                    k = (2 * i + 8) % KT if col == COL_RG else 2 * i
                    load(chunk, w_in_k[:, k:k + 2, col:col + GW])
                    chunk += 1
            w_out_k = w_out[0].rearrange("(k p) n -> p k n", p=P)
            for group in range(2):
                for i in range(8):
                    k = (2 * i + 8) % KT
                    load(chunk, w_out_k[:, k:k + 2, group * GW:(group + 1) * GW])
                    chunk += 1
            w_up_k = w_up[0].rearrange("(k p) (b n) -> p k b n", p=P, b=2)
            with sp.Fori(0, UG) as g:
                with sp.Fori(0, 2) as half:
                    for i in range(4):
                        sp.wait_ge(lo_ready, g * KT + half * LOOP + (STEP_UP - LOOP + 2 * (i + 1)))
                        slot = raw_slot(STEP_UP + 2 * i)
                        for j in range(2):
                            sp.dma_start(raw[:, slot:slot + 1, j * GW:(j + 1) * GW].rearrange("p a (b n) -> p a b n", b=2),
                                         w_up_k[:, bass.ds(half * LOOP + (2 * i + j), 1), :, bass.ds(g * 512, 512)])\
                                .then_inc(raw_in[slot], 16)
            w_dn_k = w_down[0].rearrange("(k p) n -> p k n", p=P)

            def down_turn(turn, k0, group, slots):
                for n, i in enumerate(slots):
                    sp.wait_ge(lo_ready, turn * LOOP + (STEP_DN - LOOP + 2 * (i + 1)))
                    slot = raw_slot(STEP_DN + 2 * i)
                    sp.dma_start(raw[:, slot, :].rearrange("p (k n) -> p k n", k=2),
                                 w_dn_k[:, bass.ds(k0 + 2 * n, 2), group * GW:(group + 1) * GW])\
                        .then_inc(raw_in[slot], 16)

            with sp.Fori(0, 5) as turn:
                down_turn(turn, turn * LOOP, 0, range(4))
            down_turn(5, 40, 0, range(2))
            down_turn(5, 0, 1, range(2, 4))
            with sp.Fori(6, 8) as turn:
                down_turn(turn, turn * LOOP - FT, 1, range(4))
            sp.wait_ge(fsc_ps, 4)
            sp.dma_start(g_fin, g_final.rearrange("(a n) -> a n", a=1).broadcast_to([P, D])).then_inc(gfin_in, 16)
            with sp.Fori(8, 11) as turn:
                down_turn(turn, turn * LOOP - FT, 1, range(4))
            yout = out[0].rearrange("(t p) n -> p t n", p=P)
            for t in range(TT):
                for q in range(2):
                    sp.wait_ge(y_ready, 2 * t + q + 1)
                    sp.dma_start(yout[:, t, q * GW:(q + 1) * GW], xb[:, t, q * GW:(q + 1) * GW]).then_inc(stored, 16)
            sp.wait_ge(stored, 16 * 2 * TT)

        @block.gpsimd
        def _(pool):
            ada_k = w_ada[0].rearrange("(p k) n -> p k n", k=KT)
            ada_2k = w_ada[0, :, 0:2 * D].rearrange("(p k) (s n) -> p k s n", k=KT, s=2)
            fin_k = w_final_ada.rearrange("(p k) n -> p k n", k=KT)

            def column(job):
                if job < JOB_SH2:
                    return job * 512
                part = {JOB_SH2: 3 * D, JOB_SC2: 4 * D, JOB_GT1: 2 * D, JOB_GT2: 5 * D, JOB_FSC: D, JOB_FSH: 0}
                return part[job - job % 2] + (job % 2) * GW

            def start_acc(job):
                a, col = acc[:, acc_of(job), :], column(job)
                before = [j for j in range(job) if acc_of(j) == acc_of(job)]
                if before and before[-1] < JOB_GT1:
                    pool.wait_ge(ada_red, before[-1] + 1)
                elif before:
                    pool.wait_ge(gt_ps, 2 * (before[-1] - JOB_GT1 + 1))
                nc.gpsimd.memset(a, 0.0).then_inc(acc_zero, 1)
                pool.wait_ge(acc_zero, job + 1)
                if job < JOB_SH2:
                    src = b_ada[0:1, 0:2 * D].rearrange("a (s n) -> a s n", s=2)[:, :, col:col + 512]
                    pool.dma_start(a[0:1, :].rearrange("a (s n) -> a s n", s=2), src).then_inc(bias_in, 16)
                elif job < JOB_FSC:
                    pool.dma_start(a[0:1, :], b_ada[0:1, col:col + GW]).then_inc(bias_in, 16)
                else:
                    pool.dma_start(a[0:1, :], b_final_ada[col:col + GW].rearrange("(a n) -> a n", a=1)).then_inc(bias_in, 16)

            def load_unit(job, k, slot):
                col, dst = column(job), ada_of_slot(slot).rearrange("p (a n) -> p a n", a=1)
                if job < JOB_SH2:
                    src = ada_2k[:, bass.ds(k, 1), :, col:col + 512]
                    dst = dst.rearrange("p a (s n) -> p a s n", s=2)
                else:
                    src = (ada_k if job < JOB_FSC else fin_k)[:, bass.ds(k, 1), col:col + GW]
                pool.dma_start(dst, src).then_inc(ada_in[slot], 16)

            def eight_units(job, turn):
                for i in range(2 * RING):
                    if i % RING == 0 and (job or turn):
                        pool.wait_ge(ada_pe, turn * 2 + (RING * job + i // RING - 1))
                    elif job or turn:
                        pool.wait_ge(ada_acc, turn * 7 + (rows_before(job) - 6 + i - 1 - i // RING))
                    load_unit(job, turn * 8 + i, i)

            def four_units(job, turn):
                for i in range(RING):
                    if job == JOB_SH2 and type(turn) is int:
                        pool.wait_ge(*((ada_acc, rows_before(3) + 6 + i) if i else (ada_pe, 4 * RING - 1)))
                    else:
                        pool.wait_ge(ada_acc, turn * RING + (rows_before(job) - RING + i + 1))
                    load_unit(job, turn * RING + i, i)

            start_acc(0)
            nc.gpsimd.memset(ones[:, :], 1.0).then_inc(ones_ready, 1)

            def next_acc(job):
                pool.wait_ge(bias_in, 16 * (job + 1))
                start_acc(job + 1)

            early = (0, 1, 2, 4, 5, 6, 8)
            for job in range(JOBS):
                if job in (0, JOB_SH2):
                    (four_units if job else eight_units)(job, 0)
                if job in early:
                    next_acc(job)
                if job == 0:
                    eight_units(0, 1)
                elif job < JOB_SH2:
                    with pool.Fori(0, 2) as turn:
                        eight_units(job, turn)
                else:
                    with pool.Fori(1 if job == JOB_SH2 else 0, KT // RING) as turn:
                        four_units(job, turn)
                if job not in early and job < JOBS - 1:
                    next_acc(job)

        @block.scalar
        def _(act):
            def hi(step):
                act.wait_ge(raw_in[raw_slot(step)], raw_value(step))
                if step >= RING:
                    act.wait_ge(step_done, step - RING + 1)
                nc.scalar.activation(whi[:, step % RING, :], raw_of(step), ACT.Copy).then_inc(hi_ready, 1)

            def hi_turn(i, step0, steps):
                if i % 2 == 0:
                    act.wait_ge(raw_in[raw_slot(step0 + i)], steps * (4 if step0 < STEP_DN else 2) + raw_value(step0 + i))
                act.wait_ge(step_done, steps + (step0 + i - RING + 1))
                nc.scalar.activation(whi[:, i % RING, :], raw_of(step0 + i),
                                     ACT.Copy).then_inc(hi_ready, 1)

            def hi_group(step0, start=0, stop=KT):
                for step in range(step0 + start, step0 + stop):
                    hi(step)

            def modulate(k, kind, src, tmp_base, h_base):
                if k >= 2:
                    act.wait_ge(hlo_ready, h_base + k - 1)
                nc.scalar.activation(mod_tmp[:, k % 2, :], src, ACT.Identity, scale=mod_col[:, kind, k:k + 1],
                                     bias=mod_col[:, kind + 1, k:k + 1]).then_inc(tmp_ready, 1)
                act.wait_ge(tmp_ready, tmp_base + k + 1)
                nc.scalar.activation(hhi[:, k, :], mod_tmp[:, k % 2, :], ACT.Copy).then_inc(hhi_ready, 1)

            def root(n, width):
                act.wait_ge(var_ready, n)
                nc.scalar.activation(rstd[:, 0:width], rstd[:, 0:width], ACT.Sqrt).then_inc(rstd_ready, 1)

            act.dma_start(c_act[:, :], c[0].rearrange("(p k) -> p k", k=KT)).then_inc(cact_in, 16)
            act.wait_ge(cact_in, 16)
            nc.scalar.activation(c_act[:, :], c_act[:, :], ACT.Silu).then_inc(cact_ready, 1)
            act.wait_ge(x_in, 32)
            sink = arena[:, 6400:8448]
            for t in range(TT):
                if t:
                    act.wait_ge(ssq_ready, t)
                nc.scalar.activation(sink, xb[:, t, :], ACT.Square, accum_out=ssq[:, t:t + 1]).then_inc(ssq_ready, 1)
            root(1, TT)
            for b in range(0, 8, 2):
                act.wait_ge(xt_ps, b + 1)
                nc.scalar.activation(xT[:, 2 * b:2 * b + 2, :].rearrange("p k s -> p (k s)"), ps[:, x_bank(b), :],
                                     ACT.Copy).then_inc(xt_even, 1)

            act.wait_ge(xt_odd, 4)
            act.wait_ge(xt_even, 4)
            for job in range(4):
                hi_group(4 * job, 0, 4 if job < 3 else 1)
                act.wait_ge(mod_ready, job + 1)
                for k in range(4 * job, 4 * job + 4):
                    modulate(k, 0, xT[:, k, :], 0, 0)
                    if k in (13, 15):
                        hi(AK_STEPS[(k - 11) // 2])
            hi_group(15, 0, 5)

            def queries():
                act.wait_ge(step_done, AQ_STEPS[-1] + 1)
                for i in range(8):
                    nc.scalar.activation(aqT[:, i, :], ps[:, i // 2, (i % 2) * S:(i % 2 + 1) * S], ACT.Identity,
                                         bias=conv_col2[:, 2 * FT + i:2 * FT + i + 1]).then_inc(aq_ready, 1)

            def retention_in(step_end, dst, which, done):
                act.wait_ge(step_done, step_end)
                for h in range(RH):
                    for e in range(2):
                        nc.scalar.activation(dst[:, h, e, :], ps[:, 4 + h, e * S:(e + 1) * S], ACT.Identity,
                                             bias=rqk_col[:, e, 4 * which + h:4 * which + h + 1]).then_inc(done, 1)

            def key_heads():
                act.wait_ge(step_done, STEP_RQ)
                for head in range(AKV):
                    src = slice(AD * head, AD * (head + 1))
                    for half in range(2):
                        nc.scalar.activation(k2[AD * half:AD * (half + 1), head, :], ps[src, 4, 0:S], ACT.Identity,
                                             bias=conv_col2[src, 2 * FT + 8:2 * FT + 9]).then_inc(k2_ready, 1)
                nc.scalar.activation(avT, ps[:, 4, S:2 * S], ACT.Identity,
                                     bias=conv_col2[:, 2 * FT + 9:2 * FT + 10]).then_inc(k2_ready, 1)

            def exps(batch, part):
                act.wait_ge(nm_ready, 2 * batch + 2)
                for i in range(8 * part, 8 * part + 8):
                    pt = (p0, p1)[i % 2][:, i // 2, :]
                    nc.scalar.activation(pt, pt, ACT.Exp, bias=smx[:, 2, i:i + 1], scale=AD ** -0.5,
                                         accum_out=smx[:, 3, i:i + 1]).then_inc(exp_done, 1)
                if part:
                    nc.scalar.activation(smx[:, 4, :], smx[:, 4, :], ACT.Exp).then_inc(esink, 1)

            def att_tile(n):
                act.wait_ge(pt_used, 2 * n + 2)
                nc.scalar.activation(aqT[:, n, :], ps[:, 2 + n % 2, 0:S], ACT.Copy).then_inc(att_ready, 1)

            def probs_out(batch, h):
                n = 8 * batch + h
                act.wait_ge(pt_ps, n + 1)
                if n >= 2:
                    act.wait_ge(pt_used, n - 1)
                nc.scalar.activation(pT[:, h % 2, :], ps[:, h % 2, 0:320], ACT.Copy).then_inc(pt_done, 1)

            def head_squares(h):
                act.wait_ge(o_ps, h + 1)
                for t in range(TT):
                    i = 2 * h + t
                    if i >= 2:
                        act.wait_ge(o_ssq, i - 1)
                    nc.scalar.activation(mod_tmp[:, t, :], ps[:, 4 + h, t * RD:(t + 1) * RD], ACT.Square,
                                         accum_out=ssq[:, i:i + 1]).then_inc(o_ssq, 1)

            def mix_hi(b):
                act.wait_ge(mixt_ps, b + 1)
                nc.scalar.activation(hhi[:, 2 * b:2 * b + 2, :].rearrange("p k s -> p (k s)"), ps[:, 4 + b, :],
                                     ACT.Copy).then_inc(hhi_ready, 1)

            for p in range(STEP_WO0 - STEP_RQ):
                hi(STEP_RQ + p)
                if p == 1:
                    queries()
                elif p == 2:
                    key_heads()
                elif p in (12, 13):
                    exps(0, p - 12)
                elif p == 18:
                    retention_in(STEP_RK, qT, 0, rq_raw)
                elif p == 34:
                    retention_in(STEP_RV, kT, 1, rk_raw)
                for batch, first in ((0, 18), (1, 40)):
                    if first <= p < first + 8:
                        probs_out(batch, p - first)
                    if first + 2 <= p < first + 10 and (p - first) % 2 == 0:
                        att_tile(4 * batch + (p - first) // 2 - 1)
                if p in (35, 36):
                    exps(1, p - 35)
                if p == 48:
                    act.dma_start(dec, decay[:, :, :]).then_inc(dec_in, 16)
                if p in (60, 62):
                    head_squares((p - 60) // 2)
                if 59 <= p < 63:
                    i = p - 59
                    act.wait_ge(att_ready, 2 * i + 2)
                    nc.scalar.activation(hhi[:, 8 + 2 * i:10 + 2 * i, :], aqT[:, 2 * i:2 * i + 2, :], ACT.Copy)\
                        .then_inc(hhi_ready, 1)
            for i in range(KT):
                hi(STEP_WO0 + i)
                if i in (0, 2):
                    head_squares(2 + i // 2)
                elif i == 4:
                    for t in range(TT):
                        act.wait_ge(g_raw, 2 * t + 2)
                        nc.scalar.activation(g_sb[:, t, :], g_sb[:, t, :], ACT.Silu).then_inc(g_ready, 1)
                    root(2, 8)
                elif i in (8, 9):
                    mix_hi(2 * (i - 8))
                    mix_hi(2 * (i - 8) + 1)
                if i == 2:
                    act.dma_start(xb[:, 0, :], x[0, 0:P, :]).then_inc(x_again, 16)

            def gate_out(n, blocks, bank0):
                for i, b in enumerate(blocks):
                    act.wait_ge(gt_ps, n + i + 1)
                    nc.scalar.activation(gate[:, b * 512:(b + 1) * 512], ps[:, bank0 + i, :], ACT.Copy).then_inc(gt_ready, 1)

            def squares(n, part, done, sink):
                act.wait_ge(part, n + 1)
                t, b = (n % 4) // 2, 2 * (n // 4) + n % 2
                if n:
                    act.wait_ge(done, n)
                nc.scalar.activation(sink, xb[:, t, b * 512:(b + 1) * 512], ACT.Square,
                                     accum_out=ssq[:, 8 + n:9 + n]).then_inc(done, 1)

            sink = arena[:, 4352:4864]
            for i in range(KT):
                hi(STEP_WO1 + i)
                if i == 2:
                    gate_out(0, (0, 1), 6)
                elif i in (6, 8, 10, 12):
                    squares((i - 6) // 2, x1_part, x1_ssq, sink)
                elif i == 15:
                    gate_out(2, (2, 3), 0)
            hi_group(STEP_UP, 0, 3)
            for n in range(4, 8):
                squares(n, x1_part, x1_ssq, sink)
            root(3, TT)
            act.wait_ge(rstd_ready, 3)
            for b in range(4):
                cb = slice(b * 512, (b + 1) * 512)
                nc.scalar.activation(xn[:, 1, cb], xb[:, 1, cb], ACT.Copy, scale=rstd[:, 1:2]).then_inc(xn2_act, 1)
            for k in range(KT):
                act.wait_ge(xn2_ps, k - k % 2 + 2)
                modulate(k, 2, ps[:, (k // 2) % 4, (k % 2) * S:(k % 2 + 1) * S], KT, H_UP)
                if k >= 3:
                    hi(STEP_UP + k)

            def glu_linear(slot, tile, src):
                nc.scalar.activation(slot, src, ACT.Identity, scale=conv_col2[:, bass.ds(tile, 1)],
                                     bias=conv_col2[:, bass.ds(tile + FT, 1)]).then_inc(glu_lin, 1)

            def glu_act(slot, tile):
                act.wait_ge(glu_conv, tile * 2 + 2)
                nc.scalar.activation(slot, slot, ACT.Silu).then_inc(glu_silu, 1)

            with act.Fori(0, UG // 2) as pair:
                with act.Fori(0, 2) as q:
                    for half in range(2):
                        for i in range(LOOP):
                            hi_turn(i, STEP_UP + KT + half * LOOP, pair * 2 * KT + q * KT)
                            if i in (3, 4):
                                m = i - 3
                                glu_linear(glu_tmp[:, 2 * half + m, :], pair * 8 + q * 4 + (half * 2 + m),
                                           ps[:, bass.ds(half + 4 - q * 4, 1), m * S:(m + 1) * S])
                        for m in range(2):
                            glu_act(glu_tmp[:, 2 * half + m, :], pair * 8 + q * 4 + (half * 2 + m))

            def down_turn(turn, tile0, tile_of=None):
                for i in range(LOOP):
                    hi_turn(i, STEP_DN, turn * LOOP)
                    tile = tile0 + i if tile_of is None else tile_of(i)
                    nc.scalar.activation(hhi[:, i, :], actT[:, bass.ds(tile * S, S)], ACT.Copy).then_inc(hhi_ready, 1)

            act.wait_ge(glu_done, FT - 4 + 1)
            down_turn(0, 0)
            act.wait_ge(step_done, STEP_DN)
            for m in range(4):
                glu_linear(glu_tmp[:, m, :], 4 * (UG - 1) + m, ps[:, 4 + m // 2, (m % 2) * S:(m % 2 + 1) * S])
            for m in range(4):
                glu_act(glu_tmp[:, m, :], 4 * (UG - 1) + m)
            down_turn(1, LOOP)
            down_turn(2, 2 * LOOP)
            gate_out(4, range(4), 4)
            with act.Fori(3, 5) as turn:
                down_turn(turn, turn * LOOP)
            act.wait_ge(glu_done, FT + 1)
            down_turn(5, 0, lambda i: 40 + i if i < 4 else i - 4)
            down_turn(6, 4)
            sink = glu_tmp[:, 2:4, :].rearrange("p i s -> p (i s)")
            for n in range(4):
                squares(n, x2_part, x2_ssq, sink)
            with act.Fori(7, 11) as turn:
                down_turn(turn, turn * LOOP - FT)
            for n in range(4, 8):
                squares(n, x2_part, x2_ssq, sink)
            root(4, TT)

        @block.vector
        def _(dve):
            links = [0]

            def link(ins):
                links[0] += 1
                ins.then_inc(dve_link, 1)
                dve.wait_ge(dve_link, links[0])

            def lo(step):
                dve.wait_ge(hi_ready, step + 1)
                nc.vector.tensor_tensor(wlo[:, step % RING, :], raw_of(step), whi[:, step % RING, :],
                                        ALU.subtract).then_inc(lo_ready, 1)

            def lo_turn(i, step0, steps):
                dve.wait_ge(hi_ready, steps + (step0 + i + 1))
                nc.vector.tensor_tensor(wlo[:, i % RING, :], raw_of(step0 + i),
                                        whi[:, i % RING, :], ALU.subtract).then_inc(lo_ready, 1)

            def ada_row(a, w, c_col):
                nc.vector.scalar_tensor_tensor(a, w, c_col, a, ALU.mult, ALU.add).then_inc(ada_acc, 1)

            def ada(job, k):
                if k == 0:
                    dve.wait_ge(bias_in, 16 * (job + 1))
                dve.wait_ge(ada_in[ada_slot(job, k)], ada_value(job, k))
                before = rows_before(job) + (k - 1 - k // RING if job < JOB_SH2 else k)
                if before:
                    dve.wait_ge(ada_acc, before)
                ada_row(acc[:, acc_of(job), :], ada_of_slot(ada_slot(job, k)), c_act[:, k:k + 1])

            def pe_row(job):
                dve.wait_ge(ada_pe, RING * (job + 1))
                dve.wait_ge(ada_acc, rows_before(job) + 12)
                a = acc[0:1, acc_of(job), :].rearrange("p (b n) -> p b n", b=2)
                nc.vector.tensor_tensor(a, a, ps[0:1, 5:7, :], ALU.add).then_inc(ada_acc, 1)

            def ada_turn(job, buf, turn, i):
                if i == 0:
                    dve.wait_ge(bias_in, job * 16 + 16)
                dve.wait_ge(ada_in[i], job * 64 + turn * 16 + ada_value(JOB_SH2, 0) - 64 * JOB_SH2)
                dve.wait_ge(ada_acc, rows_before(job) + turn * RING + i)
                ada_row(acc[:, bass.ds(buf, 1), :], ada_raw[:, i:i + 1, :], c_act[:, bass.ds(turn * RING + i, 1)])

            def mod_cols(job, bank, col0):
                dve.wait_ge(ada_red, job + 1)
                parts = mod_parts(job)
                for kind, k, count, col in parts:
                    src = ps[:, bank, col0 + col:col0 + col + count]
                    dst = mod_col[:, kind, k:k + count]
                    if kind % 2:
                        ins = nc.vector.tensor_copy(dst, src)
                    else:
                        ins = nc.vector.scalar_tensor_tensor(dst, src, 1.0, g_col[:, kind // 2, k:k + count],
                                                             ALU.add, ALU.mult)
                    if kind == parts[-1][0]:
                        ins.then_inc(mod_ready, 1)
                    else:
                        link(ins)

            def h_lo(k, base):
                dve.wait_ge(hhi_ready, base + k + 1)
                return nc.vector.tensor_tensor(hlo[:, k, :], mod_tmp[:, k % 2, :], hhi[:, k, :],
                                               ALU.subtract).then_inc(hlo_ready, 1)

            def rstd_of(dst, src, n):
                link(nc.vector.tensor_scalar(dst, src, 1.0 / n, EPS, ALU.mult, ALU.add))
                nc.vector.reciprocal(dst, dst).then_inc(var_ready, 1)

            dve.wait_ge(cact_ready, 1)
            for k in (1, 2, 3):
                ada(0, k)
            dve.wait_ge(ssq_ready, 2)
            rstd_of(rstd[:, 0:2], ssq[:, 0:2], D)
            ada(0, 5)
            dve.wait_ge(rstd_ready, 1)
            for t in range(TT):
                nc.vector.tensor_scalar(xn1[:, t, :], xb[:, t, :], rstd[:, t:t + 1], None, ALU.mult).then_inc(xn_ready, 1)
            for b, k in ((1, 6), (3, 7), (5, 9), (7, 10)):
                ada(0, k)
                dve.wait_ge(xt_ps, b + 1)
                nc.vector.tensor_copy(xT[:, 2 * b:2 * b + 2, :].rearrange("p k s -> p (k s)"), ps[:, x_bank(b), :])\
                    .then_inc(xt_odd, 1)
            ada(0, 11)
            ada(0, 13)
            dve.wait_ge(cols_ps, 5)
            for dst, col, count in ((g_col[:, :, :].rearrange("p i k -> p (i k)"), 0, 2 * KT), (conv_col[:, :], 32, 2 * FT),
                                    (conv_col2[:, :], 128, 2 * FT + 10),
                                    (rqk_col[:, :, :].rearrange("p e h -> p (e h)"), 256, 16)):
                nc.vector.tensor_copy(dst, ps[:, 4, col:col + count]).then_inc(cols_ready, 1)
            ada(0, 14)
            ada(0, 15)
            pe_row(0)
            dve.wait_ge(cols_ready, 4)
            for job in range(4):
                nxt = [k for k in range(KT) if k % RING] if job < 3 else []
                for k in nxt[:1]:
                    ada(job + 1, k)
                if job == 3:
                    lo(AK_STEPS[0])
                mod_cols(job, 7, 8 * job)
                h_lo(4 * job, 0)
                for i in range(4):
                    if i < 3:
                        h_lo(4 * job + i + 1, 0)
                    if job < 3:
                        lo(AQ_STEPS[4 * job + i])
                    elif i in (0, 2):
                        lo(AK_STEPS[1 + i // 2])
                    for k in nxt[1 + 2 * i:3 + 2 * i]:
                        ada(job + 1, k)
                for k in nxt[9:]:
                    ada(job + 1, k)
                if job < 3:
                    pe_row(job + 1)
            def unit(n):
                ada(4 + n // KT, n % KT)

            for i in range(5):
                lo(AQ_STEPS[12] + i)
                if i:
                    unit(i - 1)
            def values_out():
                dve.wait_ge(const_in, 16 * 2)
                dve.wait_ge(vt_ps, 1)
                nc.vector.tensor_copy(av.rearrange("p t d -> p (t d)"), ps[:, 3, 0:2 * P]).then_inc(av_ready, 1)

            def rotate(dst, raw_done, n, i):
                ev, od = dst[:, :, 0, :], dst[:, :, 1, :]
                cos, sin = (cs[:, j:j + 1, :].broadcast_to([P, RH, S]) for j in range(2))
                if i == 0:
                    dve.wait_ge(raw_done, 2 * RH)
                    dve.wait_ge(late_in, 16 * 2)
                    if n:
                        dve.wait_ge(rot_done, n)
                    ins = nc.vector.tensor_tensor(rot_tmp[:, 0], od, sin, ALU.mult)
                elif i == 1:
                    ins = nc.vector.tensor_tensor(rot_tmp[:, 1], ev, sin, ALU.mult)
                elif i == 2:
                    dve.wait_ge(rot_done, n + 2)
                    ins = nc.vector.tensor_tensor(ev, ev, cos, ALU.mult)
                elif i == 3:
                    ins = nc.vector.tensor_tensor(od, od, cos, ALU.mult)
                elif i == 4:
                    dve.wait_ge(rot_done, n + 3)
                    ins = nc.vector.tensor_tensor(ev, ev, rot_tmp[:, 0], ALU.subtract)
                else:
                    dve.wait_ge(rot_done, n + 4)
                    ins = nc.vector.tensor_tensor(od, od, rot_tmp[:, 1], ALU.add)
                ins.then_inc(rot_done, 1)

            def scores_out(batch, i):
                t, n = i % 2, 16 * batch + i
                dve.wait_ge(sc_ps, n + 1)
                pt, mk = ((p0, mask[:, 0:P]), (p1, mask[:, P:P + S]))[t]
                nc.vector.tensor_tensor_reduce(pt[:, i // 2, :], ps[:, i % 4, 0:(1 + t) * P], mk, 1.0, -3e38,
                                               ALU.add, ALU.max, smx[:, 0, i:i + 1]).then_inc(sc_done, 1)

            def maxima(batch):
                dve.wait_ge(sc_done, 16 * batch + 16)
                sk = sink_b[:, 8 * batch:8 * batch + 8].rearrange("p (h a) -> p h a", a=1).broadcast_to([P, 8, 2])

                def pair(r):
                    return smx[:, r, :].rearrange("p (h a) -> p h a", a=2)

                link(nc.vector.scalar_tensor_tensor(pair(1), pair(0), AD ** -0.5, sk, ALU.mult, ALU.max))
                nc.vector.tensor_scalar(smx[:, 2, :], smx[:, 1, :], -1.0, None, ALU.mult).then_inc(nm_ready, 1)
                nc.vector.tensor_tensor(pair(4), sk, pair(1), ALU.subtract).then_inc(nm_ready, 1)

            def normalise(batch, part):
                if part == 0:
                    dve.wait_ge(exp_done, 16 * batch + 16)
                    dve.wait_ge(esink, batch + 1)
                    link(nc.vector.tensor_tensor(smx[:, 5, :], smx[:, 3, :], smx[:, 4, :], ALU.add))
                    link(nc.vector.reciprocal(smx[:, 5, :], smx[:, 5, :]))
                for i in range(4 * part, 4 * part + 4):
                    pt = (p0, p1)[i % 2][:, i // 2, :]
                    nc.vector.tensor_scalar(pt, pt, smx[:, 5, i:i + 1], None, ALU.mult).then_inc(p_norm, 1)

            def att_lo(i):
                dve.wait_ge(hhi_ready, H_ATT + i + 1)
                nc.vector.tensor_tensor(hlo[:, 8 + 2 * i:10 + 2 * i, :], aqT[:, 2 * i:2 * i + 2, :],
                                        hhi[:, 8 + 2 * i:10 + 2 * i, :], ALU.subtract).then_inc(hlo_ready, 1)

            full = (6, 14, 15, 16, 17, 20, 22, 24, 29, 37, 38, 42, 44, 46, 50, 52, 57, 66, 69, 70, 78, 79)
            light = (12, 18, 19, 26, 27, 28, 31, 34, 35, 36, 40, 47, 48, 49, 53, 55, 59, 75, 77)
            units = 4

            def units_at(p):
                return 0 if p in full else 2 if p in light else 1

            for p in range(STEP_WO0 - STEP_RQ):
                lo(STEP_RQ + p)
                if p == 4:
                    values_out()
                if 4 <= p < 12:
                    scores_out(0, 2 * (p - 4))
                    scores_out(0, 2 * (p - 4) + 1)
                    if p == 11:
                        maxima(0)
                elif 14 <= p < 18:
                    normalise(0, p - 14)
                elif 20 <= p < 26:
                    rotate(qT, rq_raw, 0, p - 20)
                elif 28 <= p < 34:
                    for i in range(3 * (p - 28), min(3 * (p - 27), 16)):
                        scores_out(1, i)
                    if p == 33:
                        maxima(1)
                elif 37 <= p < 41:
                    normalise(1, p - 37)
                elif 41 <= p < 47:
                    rotate(kT, rk_raw, 6, p - 41)
                elif p == 48:
                    dve.wait_ge(ada_red, 6)
                    mod_cols(4, 0, 0)
                    mod_cols(5, 0, 8)
                elif p in (50, 51):
                    dve.wait_ge(rot_done, 12)
                    dve.wait_ge(step_done, STEP_RG)
                    t = p - 50
                    for b in range(2):
                        nc.vector.tensor_tensor(v_sb[:, t, b * 512:(b + 1) * 512], ps[:, 4 + 2 * t + b, :],
                                                gate[:, b * 512:(b + 1) * 512], ALU.add).then_inc(v_ready, 1)
                elif p in (55, 57, 59, 61):
                    h = (p - 55) // 2
                    dve.wait_ge(dec_in, 16)
                    dve.wait_ge(st_ps, h + 1)
                    nc.vector.tensor_tensor(sT[:, h, :], ps[:, 4 + h, 0:384], dec[:, h, :], ALU.mult).then_inc(st_ready, 1)
                if p >= 60:
                    att_lo(p - 60)
                for _ in range(units_at(p)):
                    unit(units)
                    units += 1
            for i in range(KT):
                lo(STEP_WO0 + i)
                if i == 2:
                    dve.wait_ge(step_done, STEP_WO0)
                    for n in range(4):
                        t, b = n // 2, n % 2
                        nc.vector.tensor_tensor(g_sb[:, t, b * 512:(b + 1) * 512], ps[:, n, :],
                                                gate[:, GW + b * 512:GW + (b + 1) * 512], ALU.add).then_inc(g_raw, 1)
                elif i == 3:
                    dve.wait_ge(o_ssq, 8)
                    rstd_of(rstd[:, 0:8], ssq[:, 0:8], RD)
                elif i in (5, 6):
                    dve.wait_ge(rstd_ready, 2)
                    dve.wait_ge(g_ready, 2)
                    for n in range(4 * (i - 5), 4 * (i - 5) + 4):
                        h, t = n // 2, n % 2
                        g = g_sb[:, t, h * RD:(h + 1) * RD]
                        nc.vector.scalar_tensor_tensor(g, ps[:, 4 + h, t * RD:(t + 1) * RD], rstd[:, n:n + 1], g,
                                                       ALU.mult, ALU.mult).then_inc(mix_ready, 1)
                elif i in (9, 10):
                    for b in (2 * (i - 9), 2 * (i - 9) + 1):
                        dve.wait_ge(hhi_ready, H_RET + b + 1)
                        nc.vector.tensor_tensor(hlo[:, 2 * b:2 * b + 2, :].rearrange("p k s -> p (k s)"), ps[:, 4 + b, :],
                                                hhi[:, 2 * b:2 * b + 2, :].rearrange("p k s -> p (k s)"),
                                                ALU.subtract).then_inc(hlo_ready, 1)
                for _ in range(units_at(STEP_WO0 - STEP_RQ + i)):
                    unit(units)
                    units += 1

            def residual(n, bank0, part, gt_base, res_tmp):
                t, b = (n % 4) // 2, 2 * (n // 4) + n % 2
                dve.wait_ge(gt_ready, gt_base + b + 1)
                link(nc.vector.tensor_tensor(res_tmp, ps[:, bank0 + n % 4, :], gate[:, b * 512:(b + 1) * 512], ALU.mult))
                xs = xb[:, t, b * 512:(b + 1) * 512]
                nc.vector.tensor_tensor(xs, xs, res_tmp, ALU.add).then_inc(part, 1)
                dve.wait_ge(part, n + 1)

            dve.wait_ge(x_again, 16)
            for i in range(KT):
                lo(STEP_WO1 + i)
                if i in (4, 6, 8, 10):
                    residual((i - 4) // 2, 0, x1_part, 0, res1_tmp)
                if units < 6 * KT:
                    unit(units)
                    units += 1
            for step in range(STEP_UP, STEP_UP + 3):
                lo(step)
            for n in range(4, 8):
                dve.wait_ge(*((out_ps, n - 3) if n < 7 else (step_done, STEP_UP)))
                residual(n, 4, x1_part, 0, res1_tmp)

            def total_rstd(done):
                dve.wait_ge(done, 8)
                s = ssq[:, 8:16].rearrange("p (g t b) -> p t g b", g=2, t=2)
                half = ssq[:, 0:4].rearrange("p (t b) -> p t b", t=2)
                link(nc.vector.tensor_tensor(half, s[:, :, 0, :], s[:, :, 1, :], ALU.add))
                link(nc.vector.tensor_tensor(rstd[:, 0:2].rearrange("p (t b) -> p t b", b=1), half[:, :, 0:1], half[:, :, 1:2],
                                             ALU.add))
                rstd_of(rstd[:, 0:2], rstd[:, 0:2], D)

            total_rstd(x1_ssq)
            mod_cols(6, 2, 0)
            mod_cols(7, 3, 0)
            dve.wait_ge(rstd_ready, 3)
            for b in range(4):
                cb = slice(b * 512, (b + 1) * 512)
                nc.vector.tensor_scalar(xn[:, 0, cb], xb[:, 0, cb], rstd[:, 0:1], None, ALU.mult).then_inc(xn2_dve, 1)
            for k in range(KT):
                h_lo(k, H_UP)
                if k >= 3:
                    lo(STEP_UP + k)
            dve.wait_ge(hlo_ready, H_ACT)
            nc.vector.memset(ssq[:, 0:1], 0.0).then_inc(glu_done, 1)

            def taps(tile, bank_tiles, slot, bank):
                dve.wait_ge(glu_lin, bank_tiles)
                for d in (1, 2):
                    if d == 2:
                        dve.wait_ge(glu_conv, tile * 2 + 1)
                    nc.vector.scalar_tensor_tensor(slot(d), bank(d), conv_col[:, bass.ds(tile + (2 - d) * FT, 1)], slot(d),
                                                   ALU.mult, ALU.add).then_inc(glu_conv, 1)

            def glu_product(tile, slot, b_branch):
                dve.wait_ge(glu_silu, tile + 1)
                return nc.vector.tensor_tensor(actT[:, bass.ds(tile * S, S)], slot, b_branch, ALU.mult)

            def up_pair(pair, with_ada):
                with dve.Fori(0, 2) as q:
                    with dve.Fori(0, 2) as half:
                        for i in range(LOOP):
                            lo_turn(i, STEP_UP + KT, pair * 2 * KT + q * KT + half * LOOP)
                            if i in (5, 6):
                                m = i - 5
                                taps(pair * 8 + q * 4 + half * 2 + m, pair * 8 + q * 4 + half * 2 + 2,
                                     lambda d: glu_tmp[:, bass.ds(half * 2 + m, 1), d:S],
                                     lambda d: ps[:, bass.ds(half - q * 4 + 4, 1), m * S:(m + 1) * S - d])
                            if with_ada and i % 2:
                                ada_turn(pair + JOB_GT2, pair, q * 2 + half, i // 2)
                        for m in range(2):
                            glu_product(pair * 8 + q * 4 + half * 2 + m, glu_tmp[:, bass.ds(half * 2 + m, 1), :],
                                        ps[:, bass.ds(half - q * 4 + 6, 1), m * S:(m + 1) * S]).then_inc(glu_done, 1)

            with dve.Fori(0, ADA_PAIRS) as pair:
                up_pair(pair, True)
            with dve.Fori(ADA_PAIRS, UG // 2) as pair:
                up_pair(pair, False)

            def down_turn(turn, ada_of=None):
                for i in range(LOOP):
                    dve.wait_ge(hhi_ready, turn * LOOP + (H_ACT + i + 1))
                    tile = down_tile(turn, i)
                    nc.vector.tensor_tensor(hlo[:, i, :], actT[:, bass.ds(tile * S, S)], hhi[:, i, :],
                                            ALU.subtract).then_inc(hlo_ready, 1)
                    lo_turn(i, STEP_DN, turn * LOOP)
                    if ada_of is not None and i % 2:
                        ada_of(i // 2)

            def down_tile(turn, i):
                if type(turn) is int:
                    return (turn * LOOP + i) % FT
                return turn * LOOP + i - down_group[0] * FT

            down_group = [0]
            down_turn(0)
            for m in range(4):
                taps(4 * (UG - 1) + m, 4 * (UG - 1) + m - m % 2 + 2, lambda d: glu_tmp[:, m, d:S], lambda d: ps[:, 4 + m // 2, (m % 2) * S:(m % 2 + 1) * S - d])
            for m in range(4):
                glu_product(4 * (UG - 1) + m, glu_tmp[:, m, :], ps[:, 6 + m // 2, (m % 2) * S:(m % 2 + 1) * S])\
                    .then_inc(glu_done, 1)
            with dve.Fori(1, 3) as turn:
                down_turn(turn)
            with dve.Fori(0, 2) as n:
                down_turn(n + 3, lambda i: ada_turn(JOB_FSH, 0, n, i))
            down_turn(5, lambda i: ada_turn(JOB_FSH, 0, 2, i))
            down_turn(6, lambda i: ada_turn(JOB_FSH, 0, 3, i))
            dve.wait_ge(step_done, STEP_DN + FT)
            for n in range(4):
                residual(n, 0, x2_part, 4, res2_tmp)
            down_group[0] = 1
            with dve.Fori(0, 2) as n:
                down_turn(n + 7, lambda i: ada_turn(JOB_FSH + 1, 1, n, i))
            dve.wait_ge(gfin_in, 16)
            for b in range(4):
                dve.wait_ge(fsc_ps, b + 1)
                g = g_fin[:, b * 512:(b + 1) * 512]
                nc.vector.scalar_tensor_tensor(g, ps[:, b, :], 1.0, g, ALU.add, ALU.mult).then_inc(fin_scale, 1)
            dve.wait_ge(x2_ssq, 4)
            dve.wait_ge(fin_scale, 2)
            for t in range(TT):
                nc.vector.tensor_tensor(xb[:, t, 0:GW], xb[:, t, 0:GW], g_fin[:, 0:GW], ALU.mult).then_inc(x_scaled, 1)
            with dve.Fori(2, 4) as n:
                down_turn(n + 7, lambda i: ada_turn(JOB_FSH + 1, 1, n, i))
            for n in range(4, 8):
                dve.wait_ge(*((out_ps, n) if n < 7 else (step_done, STEPS)))
                residual(n, 4, x2_part, 4, res2_tmp)
            total_rstd(x2_ssq)
            dve.wait_ge(rstd_ready, 4)
            dve.wait_ge(x_scaled, 2)
            dve.wait_ge(fin_scale, 4)
            for t in range(TT):
                for q in range(2):
                    xs = xb[:, t, q * GW:(q + 1) * GW]
                    blocks = xs.rearrange("p (b n) -> p b n", b=2)
                    dve.wait_ge(fsh_ps, 2 * q + 2)
                    if q == 0:
                        nc.vector.scalar_tensor_tensor(blocks, blocks, rstd[:, t:t + 1], ps[:, 0:2, :],
                                                       ALU.mult, ALU.add).then_inc(y_ready, 1)
                    else:
                        link(nc.vector.scalar_tensor_tensor(xs, xs, rstd[:, t:t + 1], g_fin[:, GW:D], ALU.mult, ALU.mult))
                        nc.vector.tensor_tensor(blocks, blocks, ps[:, 2:4, :], ALU.add).then_inc(y_ready, 1)

        @block.tensor
        def _(pe):
            def passes(out_ap, lhs, rhs, start, skip):
                nc.tensor.matmul(out_ap, lhs[0], rhs[0], start=start, stop=False, skip_group_check=skip)
                nc.tensor.matmul(out_ap, lhs[0], rhs[1], start=False, stop=False, skip_group_check=skip)
                return nc.tensor.matmul(out_ap, lhs[1], rhs[0], start=False, stop=True, skip_group_check=skip)

            def columns(slot, k, start, bank_of, cols=None, order=range(4), free=None):
                for b in order:
                    if free and free[b]:
                        pe.wait_ge(*free[b])
                    for m in (2 * b, 2 * b + 1):
                        c0 = cols(m) if cols else slice(m * P, (m + 1) * P)
                        last = passes(bank_of(b)[:, (m % 2) * S:(m % 2 + 1) * S],
                                      (whi[:, slot, c0], wlo[:, slot, c0]), (hhi[:, k, :], hlo[:, k, :]),
                                      start and m % 2 == 0, True)
                last.then_inc(step_done, 1)

            def tokens(slot, k, start, bank0, order=range(4), free=None, final=False):
                for n in order:
                    if free and free[n]:
                        pe.wait_ge(*free[n])
                    t, b = n // 2, n % 2
                    ts, cb = slice(t * P, (t + 1) * P), slice(b * 512, (b + 1) * 512)
                    last = passes(ps[:, bank0 + n, :], (hhi[:, k, ts], hlo[:, k, ts]),
                                  (whi[:, slot, cb], wlo[:, slot, cb]), start, True)
                    if final and n < 3:
                        last.then_inc(out_ps, 1)
                last.then_inc(step_done, 1)

            def sum_columns(job, bank, col0):
                pe.wait_ge(ada_acc, rows_before(job + 1))
                for i in range(8):
                    last = nc.tensor.matmul(ps[:, bank, col0 + i:col0 + i + 1], acc[:, acc_of(job), i * P:(i + 1) * P],
                                            ones[:, 0:1], start=True, stop=True)
                last.then_inc(ada_red, 1)

            def sum_rows(job, bank0, done):
                pe.wait_ge(ada_acc, rows_before(job + 1))
                for b in range(2):
                    nc.tensor.matmul(ps[:, bank0 + b, :], ones[:, :], acc[:, acc_of(job), b * 512:(b + 1) * 512],
                                     start=True, stop=True).then_inc(done, 1)

            def ada_unit(job, turn):
                k = turn * RING
                slot = ada_slot(job, k)
                pe.wait_ge(ada_in[slot], ada_value(job, k))
                for b in range(2):
                    last = nc.tensor.matmul(ps[0:1, 5 + b, :], c_act[:, k:k + 1], ada_of_slot(slot)[:, b * 512:(b + 1) * 512],
                                            start=turn == 0, stop=True, skip_group_check=True)
                last.then_inc(ada_pe, 1)

            pe.wait_ge(cact_ready, 1)
            ada_unit(0, 0)
            ada_unit(0, 1)
            pe.wait_ge(rows_in, 16 * 9)
            pe.wait_ge(xn_ready, TT)
            for k in range(KT):
                if k == 12:
                    pe.wait_ge(xt_even, 1)
                if k == 14:
                    pe.wait_ge(xt_odd, 1)
                for t in range(TT):
                    c0 = (k % 2) * S + t * P
                    last = nc.tensor.transpose(ps[:, x_bank(k // 2), c0:c0 + P], xn1[:, t, k * P:(k + 1) * P], ident[:, :])
                if k % 2:
                    last.then_inc(xt_ps, 1)
            pe.wait_ge(xt_even, 4)
            pe.wait_ge(xt_odd, 4)
            for col, n, src in ((0, 2 * KT, rows[0:2 * KT, 0, 0:P]), (32, 2 * FT, rows[0:2 * FT, 1, 0:P]),
                                (128, 2 * FT + 10, rows[0:2 * FT + 10, 2, 0:P]), (256, 8, rows[0:8, 3, 0:RD:2]),
                                (264, 8, rows[0:8, 3, 1:RD:2])):
                nc.tensor.transpose(ps[:, 4, col:col + n], src, ident[0:n, 0:n]).then_inc(cols_ps, 1)
            def keys_values(n):
                pe.wait_ge(lo_ready, AK_STEPS[n] + 1)
                slot = AK_STEPS[n] % RING
                for i in range(AK_TILES):
                    k, c0 = AK_TILES * n + i, i * AKV_W
                    for part in range(2):
                        c = slice(c0 + part * P, c0 + (part + 1) * P)
                        last = passes(ps[:, 4, part * S:(part + 1) * S], (whi[:, slot, c], wlo[:, slot, c]),
                                      (hhi[:, k, :], hlo[:, k, :]), k == 0 and part == 0, True)
                last.then_inc(step_done, 1)

            ada_unit(0, 2)
            ada_unit(0, 3)
            pe.wait_ge(ones_ready, 1)
            for job in range(4):
                if job:
                    pe.wait_ge(mod_ready, job)
                sum_columns(job, 7, 8 * job)
                if job < 3:
                    ada_unit(job + 1, 0)
                if job == 3:
                    pe.wait_ge(cols_ready, 4)
                    for i in range(3):
                        keys_values(i)
                for i in range(4):
                    k = 4 * job + i
                    pe.wait_ge(hlo_ready, k + 1)
                    pe.wait_ge(lo_ready, AQ_STEPS[k] + 1)
                    columns(AQ_STEPS[k] % RING, k, k == 0, lambda b: ps[:, b, :])
                    if job < 3 and i < 3:
                        ada_unit(job + 1, i + 1)
            keys_values(3)

            def split_dims(m):
                return slice((m // 2) * RD + m % 2, (m // 2 + 1) * RD, 2)

            def att_scores(batch, i):
                n, h, t = 16 * batch + i, i // 2, i % 2
                if i >= 4:
                    pe.wait_ge(sc_done, n - 3)
                half = slice(AD * (h % 2), AD * (h % 2 + 1))
                nc.tensor.matmul(ps[:, i % 4, 0:(1 + t) * P], aqT[half, 4 * batch + h // 2, t * P:(t + 1) * P],
                                 k2[half, batch, 0:(1 + t) * P], start=True, stop=True).then_inc(sc_ps, 1)

            def att_values(batch, h):
                n = 8 * batch + h
                pe.wait_ge(pt_done, n + 1)
                if h % 2 == 0 and h >= 4:
                    pe.wait_ge(att_ready, n // 2 - 1)
                o = ps[AD * (h % 2):AD * (h % 2 + 1), 2 + (h // 2) % 2, :]
                v0, v1 = (av[:, t, AD * batch:AD * (batch + 1)] for t in range(TT))
                pr = pT[:, h % 2, :]
                nc.tensor.matmul(o[:, 0:P], v0, pr[:, 0:P], start=True, stop=True, skip_group_check=True)
                nc.tensor.matmul(o[:, P:2 * P], v1, pr[:, 192:320], start=False, stop=False, skip_group_check=True)
                last = nc.tensor.matmul(o[:, P:P + 64], v0, pr[:, P:192], start=False, stop=True, skip_group_check=True)
                last.then_inc(pt_used, 1)

            def att_head(batch, h):
                n = 8 * batch + h
                if h < 8:
                    pe.wait_ge(p_norm, 16 * batch + 2 * h + 2)
                    if h >= 2:
                        pe.wait_ge(pt_done, n - 1)
                    bank = ps[:, h % 2, :]
                    nc.tensor.transpose(bank[:, 0:P], p0[:, h, :], ident[:, :])
                    nc.tensor.transpose(bank[:, P:192], p1[0:64, h, 0:P], ident[0:64, 0:64])
                    nc.tensor.transpose(bank[:, 192:320], p1[:, h, P:2 * P], ident[:, :]).then_inc(pt_ps, 1)
                if h:
                    att_values(batch, h - 1)

            def ret_scores(h):
                for m, cols in ((0, slice(0, S)), (1, slice(P, S))):
                    o = ps[:, 4 + h, m * S:m * S + cols.stop - cols.start]
                    for e in range(2):
                        last = nc.tensor.matmul(o, kT[:, h, e, m * P:(m + 1) * P], qT[:, h, e, cols],
                                                start=m == 0 and e == 0, stop=e == 1, skip_group_check=True)
                last.then_inc(st_ps, 1)

            def ret_values(h):
                pe.wait_ge(st_ready, h + 1)
                v0, v1 = (v_sb[:, t, h * RD:(h + 1) * RD] for t in range(TT))
                o = ps[:, 4 + h, :]
                nc.tensor.matmul(o[:, 0:RD], sT[:, h, 0:P], v0, start=True, stop=True, skip_group_check=True)
                nc.tensor.matmul(o[:, RD:2 * RD], sT[:, h, P:2 * P], v0, start=False, stop=False, skip_group_check=True)
                nc.tensor.matmul(o[:, RD:2 * RD], sT[:, h, S:S + P], v1, start=False, stop=True, skip_group_check=True)\
                    .then_inc(o_ps, 1)

            freed = {STEP_RQ: [(k2_ready, 5), None, None, None],
                     STEP_RK: [(rq_raw, 2 * b + 2) for b in range(4)],
                     STEP_RV: [(rk_raw, 2 * b + 2) for b in range(4)],
                     STEP_RG: [(mod_ready, 6), (pt_done, 16), (att_ready, 7), (att_ready, 8)]}
            pe.wait_ge(mod_ready, 4)
            for p in range(STEP_WO0 - STEP_RQ):
                step, k = STEP_RQ + p, p % KT
                order = (1, 2, 3, 0) if step in (STEP_RQ, STEP_RG) else range(4)
                pe.wait_ge(lo_ready, step + 1)
                if step < STEP_RV:
                    columns(k % RING, k, k == 0, lambda b: ps[:, 4 + b, :], split_dims, order, freed.get(step))
                elif step < STEP_RG:
                    tokens(k % RING, k, k == 0, 4, order, freed.get(step))
                else:
                    tokens(k % RING, (8 + k) % KT, k == 0, 0, order, freed.get(step))
                if 1 <= p < 9:
                    if p == 1:
                        pe.wait_ge(aq_ready, 8)
                        for t in range(TT):
                            last = nc.tensor.transpose(ps[:, 3, t * P:(t + 1) * P], avT[:, t * P:(t + 1) * P], ident[:, :])
                        last.then_inc(vt_ps, 1)
                    if p == 2:
                        pe.wait_ge(av_ready, 1)
                    att_scores(0, 2 * p - 2)
                    att_scores(0, 2 * p - 1)
                elif 15 <= p < 24:
                    att_head(0, p - 15)
                elif 25 <= p < 31:
                    if p == 25:
                        pe.wait_ge(att_ready, 4)
                    for i in range(3 * (p - 25), min(3 * (p - 24), 16)):
                        att_scores(1, i)
                elif 37 <= p < 46:
                    att_head(1, p - 37)
                elif p == 46:
                    pe.wait_ge(pt_done, 15)
                    sum_columns(4, 0, 0)
                    sum_columns(5, 0, 8)
                elif p in (52, 54, 56, 58):
                    if p == 52:
                        pe.wait_ge(rot_done, 12)
                        pe.wait_ge(v_ready, 4)
                    ret_scores((p - 52) // 2)
                elif p in (57, 59, 61, 63):
                    ret_values((p - 57) // 2)
            for i in range(KT):
                if i % 2 == 0:
                    pe.wait_ge(hlo_ready, H_ATT + i // 2 + 1)
                pe.wait_ge(lo_ready, STEP_WO0 + i + 1)
                tokens(i % RING, (8 + i) % KT, i == 0, 0, free=None if i else [(g_raw, b + 1) for b in range(4)])
                if i in (5, 6):
                    for b in (2 * (i - 5), 2 * (i - 5) + 1):
                        pe.wait_ge(mix_ready, 2 * b + 2)
                        for j in range(4):
                            k, t = 2 * b + j // 2, j % 2
                            last = nc.tensor.transpose(ps[:, 4 + b, j * P:(j + 1) * P], g_sb[:, t, k * P:(k + 1) * P],
                                                       ident[:, :])
                        last.then_inc(mixt_ps, 1)
            sum_rows(JOB_GT1, 6, gt_ps)
            for i in range(KT):
                pe.wait_ge(lo_ready, STEP_WO1 + i + 1)
                tokens(i % RING, (8 + i) % KT, i == 0, 4, free=None if i else [None, None, (gt_ready, 1), (gt_ready, 2)],
                       final=i == KT - 1)
                if i == 13:
                    pe.wait_ge(x1_part, 4)
                    sum_rows(JOB_GT1 + 1, 0, gt_ps)
            for job in (6, 7):
                sum_columns(job, job - 4, 0)
            def x_tiles(k0):
                if k0 % 4 == 0:
                    pe.wait_ge(xn2_dve, k0 // 4 + 1)
                    pe.wait_ge(xn2_act, k0 // 4 + 1)
                if k0 >= 8:
                    pe.wait_ge(tmp_ready, KT + k0 - 6)
                for k in (k0, k0 + 1):
                    for t in range(TT):
                        c0 = (k % 2) * S + t * P
                        last = nc.tensor.transpose(ps[:, (k // 2) % 4, c0:c0 + P], xn[:, t, k * P:(k + 1) * P], ident[:, :])
                    last.then_inc(xn2_ps, 1)

            pe.wait_ge(gt_ready, 4)
            pe.wait_ge(mod_ready, 8)
            x_tiles(0)
            x_tiles(2)
            for k in range(KT):
                pe.wait_ge(hlo_ready, H_UP + k + 1)
                pe.wait_ge(lo_ready, STEP_UP + k + 1)
                columns(k % RING, k, k == 0, lambda b: ps[:, 4 + b, :], free=None if k else [(x1_part, 5 + b) for b in range(4)])
                if k < 6:
                    x_tiles(2 * k + 4)
            with pe.Fori(0, UG // 2) as pair:
                with pe.Fori(0, 2) as q:
                    pe.wait_ge(glu_done, pair * 8 + q * 4 + 1)
                    for k in range(KT):
                        pe.wait_ge(lo_ready, pair * 2 * KT + q * KT + (STEP_UP + KT + k + 1))
                        columns(k % RING, k, k == 0, lambda b: ps[:, bass.ds(q * 4 + b, 1), :].rearrange("p a n -> p (a n)"))
            def down_turn(turn, start, bank_of, final=None):
                for i in range(LOOP):
                    pe.wait_ge(hlo_ready, turn * LOOP + (H_ACT + i + 1))
                    pe.wait_ge(lo_ready, turn * LOOP + (STEP_DN + i + 1))
                    tokens(i % RING, i, start == i, bank_of(i), final=final == i)

            pe.wait_ge(glu_done, FT - 4 + 1)
            down_turn(0, 0, lambda i: 0)
            down_turn(1, None, lambda i: 0)
            pe.wait_ge(glu_done, FT + 1)
            sum_rows(JOB_GT2, 4, gt_ps)
            sum_rows(JOB_GT2 + 1, 6, gt_ps)
            with pe.Fori(2, 5) as turn:
                down_turn(turn, None, lambda i: 0)
            pe.wait_ge(gt_ready, 8)
            down_turn(5, 4, lambda i: 0 if i < 4 else 4)
            down_turn(6, None, lambda i: 4)
            pe.wait_ge(x2_part, 4)
            for half in range(2):
                sum_rows(JOB_FSC + half, 2 * half, fsc_ps)
            with pe.Fori(7, 10) as turn:
                down_turn(turn, None, lambda i: 4)
            pe.wait_ge(fin_scale, 4)
            sum_rows(JOB_FSH, 0, fsh_ps)
            down_turn(10, None, lambda i: 4, final=LOOP - 1)
            sum_rows(JOB_FSH + 1, 2, fsh_ps)


_INS = ["x", "c", "w_ada", "b_ada", "g_mix", "w_in", "b_in", "sinks", "w_out", "g_ffn", "w_up", "w_conv", "b_conv",
        "w_down", "w_final_ada", "b_final_ada", "g_final"]


def _constants():
    f32 = np.float32
    freq = f32(10000.0) ** -np.linspace(0.0, 1.0, RD // 2, dtype=f32)
    angle = (freq[:, None] * np.arange(S, dtype=f32)[None, :]).astype(np.float64)
    rot = np.stack([np.cos(angle), np.sin(angle)], axis=1).astype(f32)
    pos = np.arange(S)
    gap = np.abs(pos[None, :] - pos[:, None])
    seen = (pos[None, :] // CHUNK) >= (pos[:, None] // CHUNK)
    decay = np.zeros((P, RH, 384))
    for h in range(RH):
        d = np.where(seen, (1.0 - 2.0 ** (-5.0 - h)) ** gap, 0.0) * RD ** -0.5
        decay[:, h, 0:S] = d[0:P]
        decay[:, h, S:] = d[P:, P:]
    behind = (pos[:, None] // CHUNK) - (pos[None, :] // CHUNK)
    hidden = np.where((behind >= 0) & (behind < 2), 0.0, -1e30)
    masks = np.concatenate([hidden[0:P, 0:P], hidden[P:, :]], axis=1)
    return {"rot": rot, "decay": decay.astype(f32), "masks": masks.astype(f32), "eye": np.eye(P, dtype=f32)}


def kernel(**inputs):
    import concourse.bacc as bacc
    from concourse.bass_utils import run_bass_kernel_spmd

    nc = bacc.Bacc("TRN2", target_bir_lowering=False, num_devices=1)
    arrays, args = {}, []
    given = {name: np.ascontiguousarray(inputs[name]) for name in _INS} | _constants()
    for name, a in given.items():
        arrays[f"in_{name}"] = a
        args.append(nc.dram_tensor(f"in_{name}", a.shape, mybir.dt.from_np(a.dtype), kind="ExternalInput").ap())
    args.append(nc.dram_tensor("out_y", (1, S, D), F32, kind="ExternalOutput").ap())
    build(nc, *args)
    r = run_bass_kernel_spmd(nc, [arrays], core_ids=[0])
    return r.results[0]["out_y"]
```
